# Optimizing a Trainium2 kernel written in Bass

```python
import jax, jax.numpy as jnp
from jax import lax
import numpy as np

D_MODEL = 1024
BATCH = 1
SEQ = 2048
DEPTH = 1

CHUNK = 64
N_MIXERS = 2
N_POOL_LAYERS = (DEPTH + N_MIXERS - 1) // N_MIXERS
N_GLA_LAYERS = DEPTH // N_MIXERS

POOL_WIDTH = D_MODEL
POOL_WINDOWS = (2, 4, 8, 16)
POOL_GROUPS = len(POOL_WINDOWS)
POOL_GROUP_DIM = POOL_WIDTH // POOL_GROUPS

GLA_HEADS = 4
GLA_KEY_WIDTH = D_MODEL // 2
GLA_VALUE_WIDTH = D_MODEL
GLA_HEAD_K = GLA_KEY_WIDTH // GLA_HEADS
GLA_HEAD_V = GLA_VALUE_WIDTH // GLA_HEADS
GLA_GATE_RANK = 16
GLA_GATE_NORMALIZER = 16.0
GLA_IN_WIDTH = 2 * GLA_KEY_WIDTH + 2 * GLA_VALUE_WIDTH + GLA_GATE_RANK

RMS_EPS = 1e-6


def rms_norm(x, w):
    xf = x.astype(jnp.float32)
    y = xf * lax.rsqrt(jnp.mean(xf * xf, axis=-1, keepdims=True) + RMS_EPS)
    return (y * w.astype(jnp.float32)).astype(x.dtype)

def trailing_mean(u, window):
    seq = u.shape[1]
    cs = jnp.cumsum(u.astype(jnp.float32), axis=1)
    lagged = jnp.pad(cs, ((0, 0), (window, 0), (0, 0)))[:, :seq]
    count = jnp.minimum(jnp.arange(1, seq + 1), window).astype(jnp.float32)
    return ((cs - lagged) / count[None, :, None]).astype(u.dtype)

def pool_mixer(h, in_w, group_w, group_b, scale, out_w):
    b, s, _ = h.shape
    u, gate = jnp.split(h @ in_w, 2, axis=-1)
    ug = u.reshape(b, s, POOL_GROUPS, POOL_GROUP_DIM)
    pooled = jnp.stack([trailing_mean(ug[:, :, g], w) for g, w in enumerate(POOL_WINDOWS)],
                       axis=2) - ug
    mixed = jnp.einsum('bsgc,gcd->bsgd', pooled, group_w) + group_b
    y = mixed.reshape(b, s, POOL_WIDTH) * scale * jax.nn.silu(gate)
    return y @ out_w

def gla_mixer(h, in_w, gk_w, gk_b, head_norm_w, out_w):
    b, s, _ = h.shape
    n_chunks = s // CHUNK
    f32 = jnp.float32
    proj = h @ in_w
    q, k, v, gate, gk_low = jnp.split(
        proj, [GLA_KEY_WIDTH, 2 * GLA_KEY_WIDTH, 2 * GLA_KEY_WIDTH + GLA_VALUE_WIDTH,
               2 * GLA_KEY_WIDTH + 2 * GLA_VALUE_WIDTH], axis=-1)
    log_g = jax.nn.log_sigmoid((gk_low @ gk_w + gk_b).astype(f32)) / GLA_GATE_NORMALIZER

    def to_chunks(t, d):
        return t.astype(f32).reshape(b, n_chunks, CHUNK, GLA_HEADS, d)

    qc = to_chunks(q, GLA_HEAD_K) * (GLA_HEAD_K ** -0.5)
    kc = to_chunks(k, GLA_HEAD_K)
    vc = to_chunks(v, GLA_HEAD_V)
    cum = jnp.cumsum(to_chunks(log_g, GLA_HEAD_K), axis=2)
    cum_last = cum[:, :, -1:]
    e_pos, e_neg = jnp.exp(cum), jnp.exp(-cum)

    fwd = jnp.einsum('bnthk,bnshk->bnhts', qc * e_pos, kc * e_neg)
    bwd = jnp.einsum('bnthk,bnshk->bnhts', qc * e_neg, kc * e_pos)
    idx = jnp.arange(CHUNK)
    lower = idx[:, None] >= idx[None, :]
    scores = jnp.where(lower, fwd, bwd)
    o_intra = jnp.einsum('bnhts,bnshv->bnthv', scores, vc)

    q_dec = qc * e_pos
    k_dec = kc * jnp.exp(cum_last - cum)
    chunk_decay = jnp.exp(cum_last[:, :, 0])

    def step(state, inp):
        q_n, k_n, v_n, d_n = inp
        o_n = jnp.einsum('bthk,bhkv->bthv', q_n, state)
        state = state * d_n[..., None] + jnp.einsum('bthk,bthv->bhkv', k_n, v_n)
        return state, o_n

    xs = (jnp.moveaxis(q_dec, 1, 0), jnp.moveaxis(k_dec, 1, 0),
          jnp.moveaxis(vc, 1, 0), jnp.moveaxis(chunk_decay, 1, 0))
    state0 = jnp.zeros((b, GLA_HEADS, GLA_HEAD_K, GLA_HEAD_V), f32)
    _, o_inter = lax.scan(step, state0, xs)
    o = (o_intra + jnp.moveaxis(o_inter, 0, 1)).reshape(b, s, GLA_HEADS, GLA_HEAD_V)

    o = o * lax.rsqrt(jnp.mean(o * o, axis=-1, keepdims=True) + RMS_EPS) * head_norm_w.astype(f32)
    y = o.reshape(b, s, GLA_VALUE_WIDTH).astype(h.dtype) * jax.nn.silu(gate)
    return y @ out_w

def first_inputs(seed: int = 0) -> dict:
    key = jax.random.key(seed)
    ks = jax.random.split(key, 16)
    nrm = jax.random.normal
    f32 = jnp.float32
    NP, NG = N_POOL_LAYERS, N_GLA_LAYERS
    return {
        "x": nrm(ks[0], (BATCH, SEQ, D_MODEL), f32),
        "norm_w": 1.0 + 0.02 * nrm(ks[1], (DEPTH, D_MODEL), f32),
        "pool_in_w": nrm(ks[2], (NP, D_MODEL, 2 * POOL_WIDTH), f32) * D_MODEL ** -0.5,
        "pool_group_w": nrm(ks[3], (NP, POOL_GROUPS, POOL_GROUP_DIM, POOL_GROUP_DIM), f32) * POOL_GROUP_DIM ** -0.5,
        "pool_group_b": 0.02 * nrm(ks[4], (NP, POOL_GROUPS, POOL_GROUP_DIM), f32),
        "pool_scale": 1.0 + 0.1 * nrm(ks[5], (NP, POOL_WIDTH), f32),
        "pool_out_w": nrm(ks[6], (NP, POOL_WIDTH, D_MODEL), f32) * POOL_WIDTH ** -0.5,
        "gla_in_w": nrm(ks[7], (NG, D_MODEL, GLA_IN_WIDTH), f32) * D_MODEL ** -0.5,
        "gla_gk_w": nrm(ks[8], (NG, GLA_GATE_RANK, GLA_KEY_WIDTH), f32) * GLA_GATE_RANK ** -0.5,
        "gla_gk_b": 0.02 * nrm(ks[9], (NG, GLA_KEY_WIDTH), f32),
        "gla_head_norm_w": 1.0 + 0.02 * nrm(ks[10], (NG, GLA_HEAD_V), f32),
        "gla_out_w": nrm(ks[11], (NG, GLA_VALUE_WIDTH, D_MODEL), f32) * GLA_VALUE_WIDTH ** -0.5,
        "final_norm_w": 1.0 + 0.02 * nrm(ks[12], (D_MODEL,), f32),
    }

def first_block(x, norm_w, pool_in_w, pool_group_w, pool_group_b, pool_scale, pool_out_w,
              gla_in_w, gla_gk_w, gla_gk_b, gla_head_norm_w, gla_out_w, final_norm_w):
    h = x
    for i in range(DEPTH):
        normed = rms_norm(h, norm_w[i])
        j = i // N_MIXERS
        if i % N_MIXERS == 0:
            h = h + pool_mixer(normed, pool_in_w[j], pool_group_w[j], pool_group_b[j],
                               pool_scale[j], pool_out_w[j])
        else:
            h = h + gla_mixer(normed, gla_in_w[j], gla_gk_w[j], gla_gk_b[j],
                              gla_head_norm_w[j], gla_out_w[j])
    return rms_norm(h, final_norm_w)


GRID_W = 64
NA_W = D_MODEL // 2
NA_HEAD_DIM = 64
NA_HEADS = NA_W // NA_HEAD_DIM
NA_KH = 8
NA_KW = 16
ML_W = D_MODEL // 2
ML_HEADS = 4
ML_HEAD_DIM = ML_W // ML_HEADS
MIX_W = NA_W + ML_W
ML_CHUNK = 64
CONV_W = 5
EPS = 1e-6
IN_SPLITS = (NA_W,) * 4 + (ML_W,) * 5 + (ML_HEADS,) * 4
IN_W = 4 * NA_W + 5 * ML_W + 4 * ML_HEADS


def rmsnorm(x, w):
    x32 = x.astype(jnp.float32)
    return x32 * lax.rsqrt(jnp.mean(x32 * x32, axis=-1, keepdims=True) + EPS) * w

def centred_short_conv(u, w, b):
    T = u.shape[1]
    pad = CONV_W // 2
    up = jnp.pad(u, ((0, 0), (pad, pad), (0, 0)))
    out = up[:, 0:T] * w[0]
    for j in range(1, CONV_W):
        out = out + up[:, j:j + T] * w[j]
    return out + b

def neighbourhood_attention(q, k, v, rpb):
    B, T, _ = q.shape
    rows = T // GRID_W
    kh = min(NA_KH, rows)

    def to_grid(t):
        return t.reshape(B, rows, GRID_W, NA_HEADS, NA_HEAD_DIM).transpose(0, 3, 1, 2, 4)

    qg = to_grid(q) * (NA_HEAD_DIM ** -0.5)
    kgrid, vgrid = to_grid(k), to_grid(v)
    r = jnp.arange(rows)
    row_idx = jnp.clip(r - kh // 2, 0, rows - kh)[:, None] + jnp.arange(kh)[None, :]
    kg = kgrid[:, :, row_idx]
    vg = vgrid[:, :, row_idx]
    col = jnp.arange(GRID_W)
    col_start = jnp.clip(col - NA_KW // 2, 0, GRID_W - NA_KW)
    col_mask = (col[None, :] >= col_start[:, None]) & (col[None, :] < col_start[:, None] + NA_KW)
    dy = row_idx - r[:, None] + NA_KH - 1
    dx = jnp.clip(col[None, :] - col[:, None], -(NA_KW - 1), NA_KW - 1) + NA_KW - 1
    bias = rpb[:, dy[:, None, :, None], dx[None, :, None, :]]
    s = jnp.einsum('bhrcd,bhrjkd->bhrcjk', qg, kg).astype(jnp.float32) + bias[None]
    s = jnp.where(col_mask[:, None, :], s, -jnp.inf)
    p = jax.nn.softmax(s.reshape(B, NA_HEADS, rows, GRID_W, kh * GRID_W), axis=-1).reshape(s.shape)
    o = jnp.einsum('bhrcjk,bhrjkd->bhrcd', p, vg)
    return o.transpose(0, 2, 3, 1, 4).reshape(B, T, NA_W)

def mlstm_chunkwise(q, k, v, i_pre, f_pre):
    B, H, T, d = q.shape
    L = ML_CHUNK
    nc = T // L
    q = q.reshape(B, H, nc, L, d)
    k = (k * (d ** -0.5)).reshape(B, H, nc, L, d)
    v = v.reshape(B, H, nc, L, d)
    i_pre = i_pre.reshape(B, H, nc, L)
    b = jnp.cumsum(jax.nn.log_sigmoid(f_pre).reshape(B, H, nc, L), axis=-1)
    b_last = b[..., -1]
    a = b_last[..., None] - b + i_pre

    def step(carry, inp):
        C, n, m = carry
        k_c, v_c, a_c, bl_c = inp
        m_new = jnp.maximum(bl_c + m, jnp.max(a_c, axis=-1))
        decay = jnp.exp(bl_c + m - m_new)
        w = jnp.exp(a_c - m_new[..., None])
        C_new = decay[..., None, None] * C + jnp.einsum('bhs,bhse,bhsd->bhed', w, v_c, k_c)
        n_new = decay[..., None] * n + jnp.einsum('bhs,bhsd->bhd', w, k_c)
        return (C_new, n_new, m_new), (C, n, m)

    init = (jnp.zeros((B, H, d, d), q.dtype), jnp.zeros((B, H, d), q.dtype), jnp.zeros((B, H), q.dtype))
    xs = (jnp.moveaxis(k, 2, 0), jnp.moveaxis(v, 2, 0), jnp.moveaxis(a, 2, 0), jnp.moveaxis(b_last, 2, 0))
    _, (C_prev, n_prev, m_prev) = lax.scan(step, init, xs)
    C_prev = jnp.moveaxis(C_prev, 0, 2)
    n_prev = jnp.moveaxis(n_prev, 0, 2)
    m_prev = jnp.moveaxis(m_prev, 0, 2)

    lower = jnp.tril(jnp.ones((L, L), dtype=bool))
    Dlog = jnp.where(lower, b[..., :, None] - b[..., None, :] + i_pre[..., None, :], -jnp.inf)
    m_inter = b + m_prev[..., None]
    m_t = jnp.maximum(m_inter, jnp.max(Dlog, axis=-1))
    S = jnp.einsum('bhntd,bhnsd->bhnts', q, k) * jnp.exp(Dlog - m_t[..., None])
    inter = jnp.exp(m_inter - m_t)
    num = jnp.einsum('bhnts,bhnse->bhnte', S, v) + inter[..., None] * jnp.einsum('bhned,bhntd->bhnte', C_prev, q)
    den = jnp.sum(S, axis=-1) + inter * jnp.einsum('bhnd,bhntd->bhnt', n_prev, q)
    h = num / jnp.maximum(jnp.abs(den), jnp.exp(-m_t))[..., None]
    return h.reshape(B, H, T, d)

def hybrid_mixer(h, w_in, b_in, conv_w, conv_b, rpb, ml_norm_w, w_out):
    B, T, _ = h.shape
    proj = h @ w_in + b_in
    split_idx = np.cumsum(IN_SPLITS)[:-1].tolist()
    (na_q, na_k, na_v, na_z, ml_q, ml_k, ml_v, ml_o, ml_z,
     i_f, f_f, i_b, f_b) = jnp.split(proj, split_idx, axis=-1)

    na_out = neighbourhood_attention(na_q, na_k, na_v, rpb) * jax.nn.silu(na_z)

    qk = jax.nn.silu(centred_short_conv(jnp.concatenate([ml_q, ml_k], axis=-1), conv_w, conv_b))
    mq, mk = jnp.split(qk, 2, axis=-1)

    def heads(t):
        return t.reshape(B, T, ML_HEADS, ML_HEAD_DIM).transpose(0, 2, 1, 3)

    mq, mk, mv = heads(mq), heads(mk), heads(ml_v)
    i_f, f_f, i_b, f_b = (g.transpose(0, 2, 1) for g in (i_f, f_f, i_b, f_b))
    h_fwd = mlstm_chunkwise(mq, mk, mv, i_f, f_f)
    flip = lambda t: jnp.flip(t, axis=2)
    h_bwd = flip(mlstm_chunkwise(flip(mq), flip(mk), flip(mv), flip(i_b), flip(f_b)))
    hm = (h_fwd + h_bwd).transpose(0, 2, 1, 3) * jax.nn.sigmoid(ml_o).reshape(B, T, ML_HEADS, ML_HEAD_DIM)
    mu = jnp.mean(hm, axis=-1, keepdims=True)
    var = jnp.mean(jnp.square(hm - mu), axis=-1, keepdims=True)
    hm = ((hm - mu) * lax.rsqrt(var + EPS)).reshape(B, T, ML_W) * ml_norm_w
    ml_out = hm * jax.nn.silu(ml_z)

    return jnp.concatenate([na_out, ml_out], axis=-1) @ w_out

def second_inputs(seed: int = 0) -> dict:
    key = jax.random.key(seed)
    ks = jax.random.split(key, 14)
    D = D_MODEL
    x = jax.random.normal(ks[0], (BATCH, SEQ, D), jnp.float32)
    c = jax.random.normal(ks[1], (BATCH, D), jnp.float32)
    w_ada = jax.random.normal(ks[2], (DEPTH, D, 3 * D), jnp.float32) * (0.5 * D ** -0.5)
    b_ada = jax.random.normal(ks[3], (DEPTH, 3 * D), jnp.float32) * 0.02
    norm_w = 1.0 + 0.1 * jax.random.normal(ks[4], (DEPTH, D), jnp.float32)
    w_in = jax.random.normal(ks[5], (DEPTH, D, IN_W), jnp.float32) * (D ** -0.5)
    n_main = 4 * NA_W + 5 * ML_W
    fgate_base = jnp.linspace(3.0, 6.0, ML_HEADS, dtype=jnp.float32)
    gk = jax.random.split(ks[6], 5)
    b_in = jnp.concatenate([
        0.02 * jax.random.normal(gk[0], (DEPTH, n_main), jnp.float32),
        0.1 * jax.random.normal(gk[1], (DEPTH, ML_HEADS), jnp.float32),
        fgate_base + 0.1 * jax.random.normal(gk[2], (DEPTH, ML_HEADS), jnp.float32),
        0.1 * jax.random.normal(gk[3], (DEPTH, ML_HEADS), jnp.float32),
        fgate_base + 0.1 * jax.random.normal(gk[4], (DEPTH, ML_HEADS), jnp.float32),
    ], axis=-1)
    conv_w = jax.random.normal(ks[7], (DEPTH, CONV_W, 2 * ML_W), jnp.float32) * (CONV_W ** -0.5)
    conv_b = 0.02 * jax.random.normal(ks[8], (DEPTH, 2 * ML_W), jnp.float32)
    rpb = 0.1 * jax.random.normal(ks[9], (DEPTH, NA_HEADS, 2 * NA_KH - 1, 2 * NA_KW - 1), jnp.float32)
    ml_norm_w = 1.0 + 0.1 * jax.random.normal(ks[10], (DEPTH, ML_W), jnp.float32)
    w_out = jax.random.normal(ks[11], (DEPTH, MIX_W, D), jnp.float32) * (MIX_W ** -0.5)
    final_norm_w = 1.0 + 0.1 * jax.random.normal(ks[12], (D,), jnp.float32)
    return {'x': x, 'c': c, 'w_ada': w_ada, 'b_ada': b_ada, 'norm_w': norm_w, 'w_in': w_in,
            'b_in': b_in, 'conv_w': conv_w, 'conv_b': conv_b, 'rpb': rpb, 'ml_norm_w': ml_norm_w,
            'w_out': w_out, 'final_norm_w': final_norm_w}

def second_block(x, c, w_ada, b_ada, norm_w, w_in, b_in, conv_w, conv_b, rpb, ml_norm_w, w_out, final_norm_w):
    h_res = x.astype(jnp.float32)
    c_act = jax.nn.silu(c.astype(jnp.float32))
    for l in range(DEPTH):
        mod = c_act @ w_ada[l] + b_ada[l]
        shift, scale, gate = jnp.split(mod, 3, axis=-1)
        h = rmsnorm(h_res, norm_w[l]) * (1.0 + scale[:, None, :]) + shift[:, None, :]
        y = hybrid_mixer(h, w_in[l], b_in[l], conv_w[l], conv_b[l], rpb[l], ml_norm_w[l], w_out[l])
        h_res = h_res + gate[:, None, :] * y
    return rmsnorm(h_res, final_norm_w).astype(x.dtype)


def setup_inputs(seed=0):
    out = dict(first_inputs(seed))
    for name, value in second_inputs(seed + 1).items():
        if name != "x":
            out[name + "_2"] = value
    return out


def reference(
    x, norm_w, pool_in_w, pool_group_w, pool_group_b, pool_scale, pool_out_w, gla_in_w,
    gla_gk_w, gla_gk_b, gla_head_norm_w, gla_out_w, final_norm_w, c_2, w_ada_2, b_ada_2,
    norm_w_2, w_in_2, b_in_2, conv_w_2, conv_b_2, rpb_2, ml_norm_w_2, w_out_2, final_norm_w_2,
):
    x = first_block(
        x, norm_w, pool_in_w, pool_group_w, pool_group_b, pool_scale, pool_out_w, gla_in_w,
        gla_gk_w, gla_gk_b, gla_head_norm_w, gla_out_w, final_norm_w,
    )
    return second_block(
        x, c_2, w_ada_2, b_ada_2, norm_w_2, w_in_2, b_in_2, conv_w_2, conv_b_2, rpb_2,
        ml_norm_w_2, w_out_2, final_norm_w_2,
    )


_drawn_inputs = setup_inputs


def setup_inputs(seed=0):
    import zlib

    import numpy as np

    out = dict(_drawn_inputs(seed))
    spreads = {}
    factors = {'norm_w': 3.917,
     'pool_group_b': 5.295,
     'final_norm_w': 2.858,
     'b_ada_2': 4.042,
     'norm_w_2': 2.854,
     'conv_b_2': 64.0,
     'rpb_2': 8.0,
     'ml_norm_w_2': 3.64}
    for name, (base, spread) in spreads.items():
        noise = np.random.default_rng([zlib.crc32(name.encode()), seed]).standard_normal(out[name].shape)
        drawn = base * np.exp(spread * noise) if base else spread * noise
        out[name] = __import__('jax').numpy.asarray(drawn.astype(out[name].dtype))
    for name, factor in factors.items():
        out[name] = (out[name] * factor).astype(out[name].dtype)
    return out
```

```python
from contextlib import ExitStack

import concourse.bass as bass
from concourse import mybir

F32 = mybir.dt.float32
F32R = mybir.dt.float32r
ALU = mybir.AluOpType
ACT = mybir.ActivationFunctionType
AX = mybir.AxisListType

P = 128
S = 2048
D = 1024
KT = D // P
NT = S // P
TB = 4
W = 512
EPS = 1e-6
NEG = -1.0e30
NA_H = 8
ML_H = 4
RPB = 128 + NA_H * 465


class Engine:

    def __init__(self, name, sem):
        self.name, self.sem, self.n, self.q, self.seen = name, sem, 0, [], {}

    def op(self, fn, *waits):
        self.q.append([fn, list(flat(waits)), (self.sem, 1)])
        self.n += 1
        return (self.sem, self.n)

    def quiet(self, fn, *waits):
        self.q.append([fn, list(flat(waits)), None])

    def dma(self, slot, out, in_, *waits, slow=False):
        slot.n += 16
        self.q.append([lambda e: e.dma_start(out, in_, allow_slow_non_contiguous=slow), list(flat(waits)), (slot.sem, 16)])
        return (slot.sem, slot.n)

    def wait(self, *waits):
        self.q.append([None, list(flat(waits)), None])

    def emit(self, e):
        for fn, waits, inc in self.q:
            for w in waits:
                if self.seen.get(id(w[0]), 0) < w[1]:
                    e.wait_ge(w[0], w[1])
                    self.seen[id(w[0])] = w[1]
            if fn is not None:
                ins = fn(e)
                if inc is not None:
                    ins.then_inc(inc[0], inc[1])
        self.q = []


def flat(ws):
    for w in ws:
        if isinstance(w, list):
            yield from flat(w)
        elif w is not None:
            yield w


class Slot:

    def __init__(self, sem):
        self.sem, self.n = sem, 0


class Ring:

    def __init__(self, bufs, slots=None):
        self.bufs, self.slots, self.i = bufs, slots, 0
        self.free = [[] for _ in bufs]

    def take(self):
        i = self.i % len(self.bufs)
        self.i += 1
        f, self.free[i] = self.free[i], None
        assert f is not None, "a buffer is taken again before its readers are queued"
        return i, self.bufs[i], f


class Kernel:
    def __init__(self, nc, io, scratch_kind):
        self.nc, self.io = nc, io
        self.ctx = ExitStack()
        self.pe, self.act, self.dve, self.pool, self.sp = (
            Engine(n, self.ctx.enter_context(nc.semaphore(f"done_{n}"))) for n in ("pe", "act", "dve", "pool", "sp"))
        self.nsem = 0
        self.slots = {False: [], True: []}
        self.pending = []
        self.kind = scratch_kind

    def slot(self, out=False):
        have, n = self.slots[out], self.nslot[out]
        if n == len(have):
            have.append(Slot(self.ctx.enter_context(self.nc.semaphore(f"dma_{'out' if out else 'in'}{n}"))))
        self.nslot[out] += 1
        return have[n]

    def dram(self, name, shape):
        return self.nc.dram_tensor(name, shape, F32, kind=self.kind).ap()

    def phase(self, fn):
        self.nslot = {False: 0, True: 0}
        self.pending = []
        with ExitStack() as ctx:
            self.px = ctx
            fn()
            self.sp.wait(self.pending)
            with self.nc.Block() as block:
                block.sync(self.sp.emit)
                block.scalar(self.act.emit)
                block.gpsimd(self.pool.emit)
                block.tensor(self.pe.emit)
                block.vector(self.dve.emit)

    def sb(self, name, shape, dt=F32):
        self.nsem += 1
        return self.px.enter_context(self.nc.sbuf_tensor(f"{name}_{self.nsem}", shape, dt))

    def ps(self, name, shape=(P, W), dt=F32):
        self.nsem += 1
        return self.px.enter_context(self.nc.psum_tensor(f"{name}_{self.nsem}", list(shape), dt))

    def ring(self, name, n, shape, dt=F32, dma=True, out=False):
        bufs = [self.sb(f"{name}{i}", shape, dt) for i in range(n)]
        return Ring(bufs, [self.slot(out) for _ in range(n)] if dma else None)

    def psring(self, name, n, shape=(P, W), dt=F32):
        return Ring([self.ps(f"{name}{i}", shape, dt) for i in range(n)])

    def load(self, ring, src, eng=None, dst=lambda b: b[:], after=()):
        i, b, free = ring.take()
        t = (eng or self.sp).dma(ring.slots[i], dst(b), src, free, *after)
        return i, b, t

    def store(self, dst, src, slot, *waits, eng=None):
        t = (eng or self.pool).dma(slot, dst, src, *waits)
        self.pending.append(t)
        return t

    def split(self, hi, lo, x, *waits):
        a = self.act.op(lambda e: e.activation(hi, x, ACT.Copy), *waits)
        d = self.dve.op(lambda e: e.tensor_tensor(lo, x, hi.bitcast(F32), ALU.subtract), a)
        return [a, d]

    def mm3(self, ps, lh, ll, rh, rl, first, last, *waits):
        pe = self.pe
        pe.quiet(lambda e: e.matmul(ps, lh, rh, start=first, stop=False), *waits)
        pe.quiet(lambda e: e.matmul(ps, lh, rl, start=False, stop=False))
        if last:
            return pe.op(lambda e: e.matmul(ps, ll, rh, start=False, stop=True))
        pe.quiet(lambda e: e.matmul(ps, ll, rh, start=False, stop=False))

    def identity(self):
        ident = self.sb("ident", [P, P])
        t = self.pool.op(lambda e: e.memset(ident[:], 0.0))
        t = self.pool.op(lambda e: e.affine_select(out=ident[:], in_=ident[:], compare_op=ALU.not_equal, fill=1.0,
                                                   base=0, pattern=[[-1, P]], channel_multiplier=1), t)
        return ident, t

    def row(self, vec, n, name="row"):
        t = self.sb(name, [P, n])
        return t, self.sp.dma(self.slot(), t[:], vec.partition_broadcast(P))

    def cols(self, vec, n, name="cols"):
        t = self.sb(name, [P, n])
        return t, self.sp.dma(self.slot(), t[:], vec.rearrange("(j p) -> p j", p=P), slow=True)

    def rstd(self, out, tmp, ssq, n, *waits):
        a = self.dve.op(lambda e: e.tensor_scalar(tmp, ssq, 1.0 / n, EPS, ALU.mult, ALU.add), *waits)
        b = self.act.op(lambda e: e.activation(tmp, tmp, ACT.Sqrt), a)
        return self.dve.op(lambda e: e.reciprocal(out, tmp), b)

    def sumsq(self, out, junk, x, *waits):
        return self.act.op(lambda e: e.activation(junk, x, ACT.Square, accum_out=out), *waits)

    def pool_block(self):
        hT = self.sb("hT", [P, 2, KT, S], F32R)
        ident, t_id = self.identity()
        hr = {}
        x = self.io["x"][0]
        with ExitStack() as sub:
            keep, self.px = self.px, sub
            nw, t_nw = self.row(self.io["norm_w"][0], D)
            xr = self.ring("x", 3, [P, D])
            xn = self.ring("xn", 2, [P, D], dma=False)
            junk = self.sb("junk", [P, D])
            st = self.sb("st", [P, NT, 3])
            tp = self.psring("tp", 8)
            loads = {}

            def ld(m):
                loads[m] = self.load(xr, x[m * P:(m + 1) * P, :])
                i, b, t = loads[m]
                loads[m] += (self.rstd(st[:, m, 2:3], st[:, m, 1:2], st[:, m, 0:1], D,
                                       self.sumsq(st[:, m, 0:1], junk[:], b[:], t)),)

            ld(0)
            for m in range(NT):
                if m + 1 < NT:
                    ld(m + 1)
                i, b, t, tr = loads.pop(m)
                j, n, nf = xn.take()
                tn = self.dve.op(lambda e, n=n, b=b, m=m: e.scalar_tensor_tensor(
                    out=n[:], in0=b[:], scalar=st[:, m, 2:3], in1=nw[:], op0=ALU.mult, op1=ALU.mult), tr, t_nw, t, nf)
                xr.free[i] = [tn]
                for g in range(2):
                    q, pb, pf = tp.take()
                    for k in range(4):
                        kk = 4 * g + k
                        f = lambda e, pb=pb, n=n, k=k, kk=kk: e.transpose(
                            pb[:, k * P:(k + 1) * P], n[:, kk * P:(kk + 1) * P], ident[:])
                        if k < 3:
                            self.pe.quiet(f, tn, pf, t_id)
                        else:
                            tt = self.pe.op(f)
                    sl = (slice(None), slice(4 * g, 4 * g + 4), slice(m * P, (m + 1) * P))
                    pv = pb[:].rearrange("p (k t) -> p k t", k=4)
                    hr[(m, g)] = self.split(hT[:, 0][sl], hT[:, 1][sl], pv, tt)
                    tp.free[q] = hr[(m, g)]
                xn.free[j] = [tt]
            with self.nc.Block() as block:
                block.sync(self.sp.emit)
                block.scalar(self.act.emit)
                block.gpsimd(self.pool.emit)
                block.tensor(self.pe.emit)
                block.vector(self.dve.emit)
            self.px = keep
        self.nslot = {False: 0, True: 0}

        win = self.io["pool_in_w"][0].rearrange("(k p) n -> p k n", p=P)
        gw = self.io["pool_group_w"][0]
        units = self.ring("wu", 5, [P, 2, KT, P], F32R, dma=False)
        raw = self.ring("raw", 2, [P, KT, P])
        gb, t_gb = self.cols(self.io["pool_group_b"][0].rearrange("g c -> (g c)"), KT)
        sc, t_sc = self.cols(self.io["pool_scale"][0], KT)
        graw = self.ring("graw", 1, [P, 2, 256])
        gsp = self.ring("gsp", 1, [P, 2, 2, 256], F32R, dma=False)
        ub = self.ring("ub", 2, [P, 16 + W], dma=False)
        sa = self.ring("sa", 2, [P, 16 + W], dma=False)
        pld = self.ring("pld", 1, [P, 2, 2, W], F32R, dma=False)
        pra = self.ring("pra", 1, [P, W], dma=False)
        sg = self.ring("sg", 3, [P, W], out=True)
        halo = self.sb("halo", [P, KT, 16])
        invc = self.sb("invc", [P, 4, 16])
        pg = self.psring("pg", 6)
        pm = self.psring("pm", 2)
        t_inv = None
        for g in range(4):
            w = 2 << g
            for c in range(16):
                t_inv = self.pool.op(lambda e, g=g, c=c, w=w: e.memset(invc[:, g, c:c + 1], 1.0 / min(c + 1, w)))
        t_h0 = self.pool.op(lambda e: e.memset(halo[:], 0.0))
        halos = {a: t_h0 for a in range(KT)}

        def unit(col):
            i, r, t = self.load(raw, win[:, :, col:col + P])
            j, u, f = units.take()
            ts = self.split(u[:, 0], u[:, 1], r[:], t, f)
            raw.free[i] = ts
            return j, u, ts

        def unit_cols(g):
            return [g * 256, g * 256 + P, D + g * 256, D + g * 256 + P]

        order = [c for g in range(4) for c in unit_cols(g)]
        ready = {}

        def prefetch(n):
            while len(ready) < min(n, 16):
                u = len(ready)
                ready[u] = unit(order[u])

        def proj(u, tb):
            j, wt, tw = ready[u]
            q, pb, pf = pg.take()
            for k in range(KT):
                t = self.mm3(pb[:], wt[:, 0, k, :], wt[:, 1, k, :], hT[:, 0, k, tb * W:(tb + 1) * W],
                             hT[:, 1, k, tb * W:(tb + 1) * W], k == 0, k == KT - 1, tw, pf)
            if tb == 3:
                units.free[j] = [t]
            return q, pb, t

        prefetch(5)
        for g in range(4):
            gi, gr, tgr = self.load(graw, gw[g].rearrange("(k p) d -> p k d", p=P))
            gj, gs, gf = gsp.take()
            tgs = self.split(gs[:, 0], gs[:, 1], gr[:], tgr, gf)
            graw.free[gi] = tgs
            for tb in range(4):
                pj, pl, plf = pld.take()
                tp2 = []
                for a in range(2):
                    q, pb, t = proj(4 * g + a, tb)
                    ch = 2 * g + a
                    ui, u, uf = ub.take()
                    tu = self.act.op(lambda e, u=u, pb=pb: e.activation(u[:, 16:], pb[:], ACT.Copy), t, uf)
                    pg.free[q] = [tu]
                    th = self.dve.op(lambda e, u=u, ch=ch: e.tensor_copy(u[:, 0:16], halo[:, ch, :]), halos[ch], uf)
                    halos[ch] = self.dve.op(lambda e, u=u, ch=ch: e.tensor_copy(halo[:, ch, :], u[:, W:W + 16]), tu, th)
                    cur, tc, lo = u, [tu, th], 0
                    for l in range(g + 1):
                        s = 1 << l
                        si, nx, sf = sa.take()
                        sa.free[si] = []
                        lo += s
                        tc = self.dve.op(lambda e, nx=nx, cur=cur, lo=lo, s=s: e.tensor_tensor(
                            nx[:, lo:], cur[:, lo:], cur[:, lo - s:16 + W - s], ALU.add), tc, sf)
                        cur = nx
                    ri, r, rf = pra.take()
                    tr = self.dve.op(lambda e, r=r, cur=cur, u=u, g=g: e.scalar_tensor_tensor(
                        out=r[:], in0=cur[:, 16:], scalar=1.0 / (2 << g), in1=u[:, 16:], op0=ALU.mult, op1=ALU.subtract), tc, rf)
                    if tb == 0:
                        tr = self.dve.op(lambda e, r=r, cur=cur, g=g: e.tensor_tensor(
                            r[:, 0:16], cur[:, 16:32], invc[:, g, :], ALU.mult), tr, t_inv)
                        tr = self.dve.op(lambda e, r=r, u=u: e.tensor_tensor(
                            r[:, 0:16], r[:, 0:16], u[:, 16:32], ALU.subtract), tr)
                    ub.free[ui] = [tr, halos[ch]]
                    ts = self.split(pl[:, 0, a], pl[:, 1, a], r[:], tr, plf)
                    pra.free[ri] = ts
                    tp2 += ts
                gates = []
                for a in range(2):
                    q, pb, t = proj(4 * g + 2 + a, tb)
                    i, s, sf = sg.take()
                    t = self.act.op(lambda e, s=s, pb=pb: e.activation(s[:], pb[:], ACT.Silu), t, sf)
                    pg.free[q] = [t]
                    gates.append((i, s, t))
                for a in range(2):
                    ch = 2 * g + a
                    q, pb, pf = pm.take()
                    for k in range(2):
                        t = self.mm3(pb[:], gs[:, 0, k, a * P:(a + 1) * P], gs[:, 1, k, a * P:(a + 1) * P],
                                     pl[:, 0, k], pl[:, 1, k], k == 0, k == 1, tgs, tp2, pf)
                    i, s, tsg = gates[a]
                    ty = self.dve.op(lambda e, s=s, pb=pb, ch=ch: e.scalar_tensor_tensor(
                        out=s[:], in0=pb[:], scalar=gb[:, ch:ch + 1], in1=s[:], op0=ALU.add, op1=ALU.mult), t, tsg, t_gb)
                    pm.free[q] = [ty]
                    ty = self.dve.op(lambda e, s=s, ch=ch: e.tensor_scalar(
                        s[:], s[:], sc[:, ch:ch + 1], None, ALU.mult), ty, t_sc)
                    sg.free[i] = [self.store(self.yT[ch * P:(ch + 1) * P, tb * W:(tb + 1) * W], s[:], sg.slots[i], ty)]
                pld.free[pj] = [t]
            gsp.free[gj] = [t]
            prefetch(4 * g + 9)

    def ada(self):
        c = self.sb("c", [P, KT])
        t = self.sp.dma(self.slot(), c[:], self.io["c_2"][0].rearrange("(k p) -> p k", p=P), slow=True)
        t_c = self.act.op(lambda e: e.activation(c[:], c[:], ACT.Silu), t)
        b = self.sb("b", [1, 3 * D])
        t_b = self.sp.dma(self.slot(), b[:], self.io["b_ada_2"])
        ones = self.sb("ones", [P, 2])
        t_1 = self.dve.op(lambda e: e.memset(ones[:], 1.0))
        wr = self.ring("w", 4, [P, 3 * D])
        acc = self.sb("acc", [P, 3 * D])
        mod = self.sb("mod", [1, 3 * D])
        pr = [self.ps(f"p{j}") for j in range(6)]
        ta = None
        for k in range(KT):
            i, w, t = self.load(wr, self.io["w_ada_2"][0][k * P:(k + 1) * P, :])
            if k == 0:
                ta = self.dve.op(lambda e, w=w: e.tensor_scalar(acc[:], w[:], c[:, 0:1], None, ALU.mult), t, t_c)
            else:
                ta = self.dve.op(lambda e, w=w, k=k: e.scalar_tensor_tensor(
                    out=acc[:], in0=w[:], scalar=c[:, k:k + 1], in1=acc[:], op0=ALU.mult, op1=ALU.add), t, ta)
            wr.free[i] = [ta]
        for j in range(6):
            t = self.pe.op(lambda e, j=j: e.matmul(pr[j][0:1, :], ones[:, 0:1], acc[:, j * W:(j + 1) * W],
                                                   start=True, stop=True), ta, t_1)
            t = self.dve.op(lambda e, j=j: e.tensor_tensor(mod[:, j * W:(j + 1) * W], pr[j][0:1, :],
                                                           b[:, j * W:(j + 1) * W], ALU.add), t, t_b)
        self.store(self.mod, mod[:], self.slot(True), t)

    def out_block(self, w_dram, yT_dram, res, last):
        ident, t_id = self.identity()
        wv = w_dram.rearrange("(k p) n -> p k n", p=P)
        raw = self.ring("raw", 4, [P, W])
        ws = self.sb("ws", [P, 2, KT, D], F32R)
        tw = {}
        fw, t_fw = self.row(self.io["final_norm_w_2"] if last else self.io["final_norm_w"], D, "fw")
        if last:
            gate, t_gate = self.row(self.mod[0, 2 * D:3 * D], D, "gate")
        else:
            A, t_sc = self.row(self.mod[0, D:2 * D], D, "A")
            B, t_sh = self.row(self.mod[0, 0:D], D, "B")
            nw, t_nw = self.row(self.io["norm_w_2"][0], D, "nw")
            t_A = self.dve.op(lambda e: e.scalar_tensor_tensor(out=A[:], in0=A[:], scalar=1.0, in1=nw[:],
                                                               op0=ALU.add, op1=ALU.mult), t_sc, t_nw)
        ys = self.ring("ys", 2, [P, 2, KT, W], F32R, dma=False)
        xr = self.ring("xr", 2, [P, D])
        hr = self.ring("hr", 2, [P, D], out=True)
        junk = self.sb("junk", [P, D])
        st = self.sb("st", [P, NT, 6])
        pg = self.psring("pg", 4)
        if not last:
            h1r = self.ring("h1", 2, [P, D], out=True)
            tr = self.ring("tr", 2, [P, KT, P], out=True)
            tp = self.psring("tp", 4)

        def load_w(k):
            for c in range(2):
                i, r, t = self.load(raw, wv[:, k, c * W:(c + 1) * W])
                sl = slice(c * W, (c + 1) * W)
                tw[(k, c)] = self.split(ws[:, 0, k, sl], ws[:, 1, k, sl], r[:], t)
                raw.free[i] = tw[(k, c)]

        ysb = {}

        def load_y(tb, k):
            if k == 0:
                j, y, f = ys.take()
                ysb[tb] = (j, y, [], f)
            j, y, ts, f = ysb[tb]
            i, r, t = self.load(raw, yT_dram[k * P:(k + 1) * P, tb * W:(tb + 1) * W])
            s = self.split(y[:, 0, k], y[:, 1, k], r[:], t, f)
            raw.free[i] = s
            ts.append(s)

        for k in range(KT):
            load_y(0, k)
            load_w(k)
        pend = []

        def tail(m, h, hi, ti, t):
            s0 = self.sumsq(st[:, m, 0:1], junk[:], h[:], t)
            r0 = self.rstd(st[:, m, 2:3], st[:, m, 1:2], st[:, m, 0:1], D, s0)
            rows = slice(m * P, (m + 1) * P)
            if last:
                t1 = self.dve.op(lambda e: e.scalar_tensor_tensor(out=h[:], in0=h[:], scalar=st[:, m, 2:3], in1=fw[:],
                                                                  op0=ALU.mult, op1=ALU.mult), r0, t_fw, s0)
                hr.free[hi] = [self.store(self.out[0, rows, :], h[:], hr.slots[hi], t1)]
                return
            i1, h1, f1 = h1r.take()
            t1 = self.dve.op(lambda e: e.scalar_tensor_tensor(out=h1[:], in0=h[:], scalar=st[:, m, 2:3], in1=fw[:],
                                                              op0=ALU.mult, op1=ALU.mult), r0, t_fw, f1)
            t_st = self.store(self.h[rows, :], h1[:], h1r.slots[i1], t1)
            s1 = self.sumsq(st[:, m, 3:4], junk[:], h1[:], t1)
            r1 = self.rstd(st[:, m, 5:6], st[:, m, 4:5], st[:, m, 3:4], D, s1)
            t2 = self.dve.op(lambda e: e.scalar_tensor_tensor(out=h[:], in0=h1[:], scalar=st[:, m, 5:6], in1=A[:],
                                                              op0=ALU.mult, op1=ALU.mult), r1, t_A, s0)
            h1r.free[i1] = [t_st, t2, s1]
            t3 = self.pool.op(lambda e: e.tensor_tensor(h[:], h[:], B[:], ALU.add), t2, t_sh)
            pend.append((m, h, hi, t3))

        def turn():
            m, h, hi, t3 = pend.pop(0)
            oi, o, of = tr.take()
            te = []
            for g in range(2):
                q, pb, pf = tp.take()
                for k in range(4):
                    kk = 4 * g + k
                    f = lambda e, pb=pb, k=k, kk=kk: e.transpose(pb[:, k * P:(k + 1) * P], h[:, kk * P:(kk + 1) * P], ident[:])
                    tt = self.pe.op(f, t3, pf, t_id)
                e_ = self.act.op(lambda e, g=g, pb=pb: e.activation(
                    o[:, 4 * g:4 * g + 4, :], pb[:].rearrange("p (k t) -> p k t", k=4), ACT.Copy), tt, of)
                tp.free[q] = [e_]
                te.append(e_)
            hr.free[hi] = [tt]
            tr.free[oi] = [self.store(self.hT2.rearrange("(k p) t -> p k t", p=P)[:, :, m * P:(m + 1) * P],
                                      o[:], tr.slots[oi], te)]

        for m in range(NT):
            tb, o = m // 4, (m % 4) * P
            j, y, tys, _ = ysb[tb]
            xi, x, tx = self.load(xr, res[m * P:(m + 1) * P, :])
            hi, h, hf = hr.take()
            th = []
            for c in range(2):
                q, pb, pf = pg.take()
                sl = slice(c * W, (c + 1) * W)
                for k in range(KT):
                    t = self.mm3(pb[:], y[:, 0, k, o:o + P], y[:, 1, k, o:o + P], ws[:, 0, k, sl], ws[:, 1, k, sl],
                                 k == 0, k == KT - 1, tys[k], tw[(k, c)], pf)
                if last:
                    t = self.dve.op(lambda e, h=h, pb=pb, sl=sl: e.tensor_tensor(h[:, sl], pb[:], gate[:, sl], ALU.mult),
                                    t, t_gate, hf)
                    pg.free[q] = [t]
                    t = self.pool.op(lambda e, h=h, x=x, sl=sl: e.tensor_tensor(h[:, sl], h[:, sl], x[:, sl], ALU.add), t, tx)
                else:
                    t = self.dve.op(lambda e, h=h, x=x, pb=pb, sl=sl: e.tensor_tensor(h[:, sl], pb[:], x[:, sl], ALU.add),
                                    t, tx, hf)
                    pg.free[q] = [t]
                th.append(t)
            xr.free[xi] = th
            if m % 4 == 3:
                ys.free[j] = [(self.pe.sem, self.pe.n)]
            if tb + 1 < TB:
                load_y(tb + 1, 2 * (m % 4))
                load_y(tb + 1, 2 * (m % 4) + 1)
            if pend:
                turn()
            tail(m, h, hi, xi, th)
        while pend:
            turn()

    def in_block(self):
        io = self.io
        hT = self.sb("hT", [P, 2, KT, S], F32R)
        NU = 6
        wu = self.sb("wu", [P, NU, 2, KT, P], F32R)
        ufree = [[] for _ in range(NU)]
        raw = self.ring("raw", 2, [P, KT, P])
        st = self.ring("st", 2, [P, W], out=True)
        bc, t_bc = self.cols(io["b_in_2"][0, 0:36 * P], 36)
        br = self.sb("br", [P, 3, W])
        t_br = [self.sp.dma(self.slot(), br[:, j, :], io["b_in_2"][0, c * W:(c + 1) * W].partition_broadcast(P))
                for j, c in enumerate((2, 6, 7))]
        bg, t_bg = self.row(io["b_in_2"][0, 36 * P:36 * P + 16], 16)
        cw = self.sb("cw", [P, 5, 8])
        t_cw = self.sp.dma(self.slot(), cw[:], io["conv_w_2"][0].rearrange("j (c p) -> p j c", p=P), slow=True)
        cb, t_cb = self.cols(io["conv_b_2"][0], 8)
        mw, t_mw = self.cols(io["ml_norm_w_2"][0], 4)
        win = io["w_in_2"][0].rearrange("(k p) n -> p k n", p=P)
        wgr = self.sb("wgr", [P, KT, 16])
        t_wg = self.sp.dma(self.slot(), wgr[:], win[:, :, 36 * P:36 * P + 16])
        wg = self.sb("wg", [P, 2, KT, 16], F32R)
        cu = self.ring("cu", 2, [P, 4 + W + 2], dma=False)
        ca = self.ring("ca", 2, [P, W + 2], out=True)
        G = self.sb("G", [P, NT, 16])
        pg = self.psring("pg", 6)
        pgt = self.psring("pgt", 2)

        hs = {}

        def load_h(tb, kk):
            i, r, t = self.load(raw, self.hT2.rearrange("(k p) t -> p k t", p=P)[:, 2 * kk:2 * kk + 2, tb * W:(tb + 1) * W],
                                dst=lambda b: b[:].rearrange("p k c -> p (k c)").rearrange("p (a t) -> p a t", a=2))
            v = r[:].rearrange("p k c -> p (k c)").rearrange("p (a t) -> p a t", a=2)
            sl = (slice(None), slice(2 * kk, 2 * kk + 2), slice(tb * W, (tb + 1) * W))
            s = self.split(hT[:, 0][sl], hT[:, 1][sl], v, t)
            raw.free[i] = s
            hs[(tb, 2 * kk)] = hs[(tb, 2 * kk + 1)] = s

        blocks = [(0, "nq"), (1, "nk"), (2, "nv"), (4, "mq"), (5, "mk"), (6, "mv"), (3, "nz"), (8, "mz"), (7, "mo")]
        cols = [b * W + j * P for b, _ in blocks for j in range(4)]
        ready = []

        def prefetch(n):
            while len(ready) < min(n, 36):
                u = len(ready)
                i, r, t = self.load(raw, win[:, :, cols[u]:cols[u] + P])
                s = self.split(wu[:, u % NU, 0], wu[:, u % NU, 1], r[:], t, ufree[u % NU])
                raw.free[i] = s
                ready.append(s)

        prefetch(1)
        for kk in range(4):
            load_h(0, kk)
        prefetch(2)
        for tb in range(1, 4):
            for kk in range(4):
                load_h(tb, kk)
            if tb == 1:
                prefetch(3)
        prefetch(NU)
        t_wgs = self.split(wg[:, 0], wg[:, 1], wgr[:], t_wg)

        def conv(name, j, tb, pb, t, state):
            ch = (4 if name == "mk" else 0) + j
            bcol = (4 if name == "mq" else 5) * 4 + j
            i, u, f = cu.take()
            tu = self.act.op(lambda e: e.activation(u[:, 4:4 + W], pb[:], ACT.Identity, bias=bc[:, bcol:bcol + 1]), t, f, t_bc)
            if tb == 0:
                th = self.dve.op(lambda e: e.memset(u[:, 2:4], 0.0), f)
            else:
                pu, ptu, pi = state[0]
                th = self.dve.op(lambda e: e.tensor_copy(u[:, 0:4], pu[:, W:W + 4]), f, ptu)
                cu.free[pi].append(th)
            tz = None
            lo, hi = (2 if tb == 0 else 0), (W + 2 if tb == 3 else W)
            if tb == 3:
                tz = self.dve.op(lambda e: e.memset(u[:, W + 4:W + 6], 0.0), f)
            state[0] = (u, tu, i)
            ai, a, af = ca.take()
            tc = self.dve.op(lambda e: e.tensor_scalar(a[:, lo:hi], u[:, lo:hi], cw[:, 0, ch:ch + 1], cb[:, ch:ch + 1],
                                                       ALU.mult, ALU.add), tu, th, tz, af, t_cw, t_cb)
            for w in range(1, 5):
                tc = self.dve.op(lambda e, w=w: e.scalar_tensor_tensor(
                    out=a[:, lo:hi], in0=u[:, lo + w:hi + w], scalar=cw[:, w, ch:ch + 1], in1=a[:, lo:hi],
                    op0=ALU.mult, op1=ALU.add), tc)
            cu.free[i] = [tc]
            ts = self.act.op(lambda e: e.activation(a[:, lo:hi], a[:, lo:hi], ACT.Silu), tc)
            o0 = tb * W - 2 + lo
            ca.free[ai] = [self.store(self.s[name][j * P:(j + 1) * P, o0:o0 + hi - lo], a[:, lo:hi], ca.slots[ai], ts)]
            return tu

        def evac_c(name, blk, j, tb, pb, t, state):
            if name in ("mq", "mk"):
                return conv(name, j, tb, pb, t, state)
            i, s, f = st.take()
            b = bc[:, blk * 4 + j:blk * 4 + j + 1]
            if name == "nq":
                for x in range(2):
                    o = s[:, x * 256:(x + 1) * 256].rearrange("p (a r c) -> p a r c", a=2, r=4)
                    v = pb[:, x * 256:(x + 1) * 256].rearrange("p (r a c) -> p a r c", a=2, r=4)
                    te = self.dve.op(lambda e, o=o, v=v: e.tensor_scalar(o, v, b, 0.125, ALU.add, ALU.mult), t, f, t_bc)
                t2 = te
            else:
                te = t2 = self.act.op(lambda e: e.activation(s[:], pb[:], ACT.Identity if name == "nk" else ACT.Silu,
                                                             bias=b), t, f, t_bc)
            if name == "mz":
                t2 = self.dve.op(lambda e: e.tensor_scalar(s[:], s[:], mw[:, j:j + 1], None, ALU.mult), te, t_mw)
            st.free[i] = [self.store(self.s[name][j * P:(j + 1) * P, tb * W:(tb + 1) * W], s[:], st.slots[i], t2)]
            return te

        for bi, (blk, name) in enumerate(blocks):
            u0 = 4 * bi
            if name in ("nv", "mv", "mo"):
                s0 = u0 % NU
                assert s0 + 4 <= NU
                x = ("nv", "mv", "mo").index(name)
                tw = ready[u0:u0 + 4]
                for m in range(NT):
                    q, pb, pf = pg.take()
                    if name == "mv":
                        gq, gb, gf = pgt.take()
                    for k in range(KT):
                        lh, ll = hT[:, 0, k, m * P:(m + 1) * P], hT[:, 1, k, m * P:(m + 1) * P]
                        t = self.mm3(pb[:], lh, ll, wu[:, s0:s0 + 4, 0, k, :], wu[:, s0:s0 + 4, 1, k, :],
                                     k == 0, k == KT - 1, tw, pf, hs[(m // 4, k)])
                        if name == "mv":
                            tg = self.mm3(gb[:, 0:16], lh, ll, wg[:, 0, k], wg[:, 1, k], k == 0, k == KT - 1, t_wgs, gf)
                    i, s, f = st.take()
                    t = self.dve.op(lambda e, s=s, pb=pb, x=x: e.tensor_tensor(s[:], pb[:], br[:, x, :], ALU.add), t, f, t_br[x])
                    pg.free[q] = [t]
                    if name == "mo":
                        t = self.act.op(lambda e, s=s: e.activation(s[:], s[:], ACT.Sigmoid), t)
                    st.free[i] = [self.store(self.s[name][m * P:(m + 1) * P, :], s[:], st.slots[i], t)]
                    if name == "mv":
                        t_g = self.dve.op(lambda e, gb=gb, m=m: e.tensor_tensor(G[:, m, :], gb[:, 0:16], bg[:], ALU.add), tg, t_bg)
                        pgt.free[gq] = [t_g]
                for j in range(4):
                    ufree[s0 + j] = [(self.pe.sem, self.pe.n)]
                prefetch(u0 + 4 + NU)
                if name == "mv":
                    self.store(self.gt, G[:].rearrange("p c g -> p (c g)"), self.slot(True), t_g)
            else:
                for j in range(4):
                    u = u0 + j
                    state = [None]
                    for tb in range(TB):
                        q, pb, pf = pg.take()
                        for k in range(KT):
                            t = self.mm3(pb[:], wu[:, u % NU, 0, k, :], wu[:, u % NU, 1, k, :],
                                         hT[:, 0, k, tb * W:(tb + 1) * W], hT[:, 1, k, tb * W:(tb + 1) * W],
                                         k == 0, k == KT - 1, ready[u], pf, hs[(tb, k)])
                        pg.free[q] = [evac_c(name, blk, j, tb, pb, t, state)]
                    ufree[u % NU] = [t]
                    prefetch(u + 1 + NU)

    def bias_rows(self):
        z = self.sb("z", [32, 64])
        t = self.dve.op(lambda e: e.memset(z[:], 0.0))
        n = NA_H * 465
        self.store(self.rpb[:, 0:64], z[:], self.slot(True), t)
        self.store(self.rpb[:, 64 + n:128 + n], z[:], self.slot(True), t)
        self.store(self.rpb[:, 64:64 + n], self.io["rpb_2"].rearrange("a h y x -> (a h y x)").partition_broadcast(32),
                   self.slot(True))

    def na_block(self):
        ident, t_id = self.identity()
        Z = [self.sb(f"Z{a}", [32, NA_H, 17, 40]) for a in range(2)]
        tZ = []
        for a, X in enumerate((15, 7)):
            z = Z[a]
            tm = [self.pool.op(lambda e, z=z, y=y: e.memset(z[:, :, y, :], NEG)) for y in (0, 16)]
            tl = []
            for h in range(NA_H):
                src = bass.AP(tensor=self.rpb.tensor, offset=64 + X + h * 465, ap=[[RPB - 1, 32], [31, 15], [1, 40]])
                tl.append(self.sp.dma(self.slot(), z[:, h, 1:16, :], src))

            def sel(c0, c1, base, step, cm, t):
                v = z[:, :, 1:16, c0:c1].rearrange("p h y c -> p (h y) c") if False else None
                last = None
                for h in range(NA_H):
                    v = z[:, h, 1:16, c0:c1]
                    last = self.pool.op(lambda e, v=v: e.affine_select(
                        out=v, in_=v, compare_op=ALU.is_ge, fill=NEG, base=base, pattern=[[0, 15], [step, c1 - c0]],
                        channel_multiplier=cm), tl, t)
                return last
            if a == 0:
                t = sel(0, 40, 8, 1, -1, None)
                t = sel(16, 40, 7 - 16, -1, 1, t)
            else:
                t = sel(0, 24, 0, 1, -1, None)
                t = sel(0, 40, 15, -1, 1, t)
            tZ += [t, tm]
        kinds = {"mid": (0, 12, 3), "top": (480, 9, 7), "bot": (840, 9, 2)}
        tabs = self.ring("tab", 2, [P, 2, 2, 1200])
        tslots = [[self.slot() for _ in range(24)] for _ in range(2)]
        qr = self.ring("q", 2, [P, S])
        kr = self.ring("k", 2, [P, S])
        zr = self.ring("z", 2, [P, S])
        vr = self.ring("v", 3, [120, 4, P], dma=False)
        vslots = [[self.slot() for _ in range(4)] for _ in range(3)]
        sr = self.ring("s", 3, [P, 480], dma=False)
        pr = self.ring("p", 3, [P, 480], dma=False)
        ptr = self.ring("pt", 3, [120, W], dma=False)
        orr = self.ring("o", 3, [P, P], dma=False)
        yr = self.ring("y", 2, [P, 256], out=True)
        st = self.sb("st", [P, 128, 4])
        pS, pT, pO, pX = self.psring("pS", 3), self.psring("pT", 2), self.psring("pO", 2), self.psring("pX", 1)
        heads = {}

        def prep(hp):
            q, k, z = (self.load(r, self.s[n][hp * P:(hp + 1) * P, :]) for r, n in ((qr, "nq"), (kr, "nk"), (zr, "nz")))
            ti, tab, tf = tabs.take()
            tt, n = [], 0
            for off, nk, dd in kinds.values():
                for a in range(2):
                    for ri in range(4):
                        y0 = 1 + dd - ri
                        tt.append(self.sp.dma(
                            tslots[ti][n], tab[32 * ri:32 * ri + 32, :, a, off:off + nk * 40],
                            Z[a][:, 2 * hp:2 * hp + 2, y0:y0 + nk, :].rearrange("c h y k -> c h (y k)"), tf, tZ))
                        n += 1
            tm = []
            for ri in range(4):
                for c0, c1 in ((0, ri * 40), ((ri + 8) * 40, 480)):
                    if c1 > c0:
                        tm.append(self.pool.op(lambda e, ri=ri, c0=c0, c1=c1: e.memset(
                            tab[32 * ri:32 * ri + 32, :, :, c0:c1], NEG), tt, tm[-1:]))
            for c0 in (480 + 320, 840):
                tm.append(self.pool.op(lambda e, c0=c0: e.memset(tab[:, :, :, c0:c0 + 40], NEG), tt, tm[-1:]))
            heads[hp] = dict(q=q, k=k, z=z, ti=ti, tab=tab, t=[tt, tm])

        tiles = []
        for hp in range(4):
            for i in range(8):
                for a in range(2):
                    for hh in range(2):
                        tiles.append((hp, i, a, hh))
        info = {}

        def stage_a(n):
            hp, i, a, hh = tiles[n]
            H = heads[hp]
            kind = "top" if i == 0 else "bot" if i == 7 else "mid"
            off, nk, _ = kinds[kind]
            ks = {"top": 0, "bot": 23, "mid": 4 * i - 4}[kind]
            c0, k0 = (0, 0) if a == 0 else (32, 24)
            N = nk * 40
            if hh == 0:
                vi, v, vf = vr.take()
                tv = []
                for j in range(nk // 3):
                    r0 = ks + 3 * j
                    src = self.s["nv"].rearrange("(r c) d -> r c d", c=64)[r0:r0 + 3, k0:k0 + 40, hp * P:(hp + 1) * P]
                    tv.append(self.sp.dma(vslots[vi][j], v[:, j, :], src, vf))
                info[n] = dict(v=v, vi=vi, tv=tv)
            else:
                info[n] = dict(v=info[n - 1]["v"], vi=info[n - 1]["vi"], tv=info[n - 1]["tv"])
            d = info[n]
            rows = slice(64 * hh, 64 * hh + 64)
            q = H["q"][1][rows, (2 * i + a) * P:(2 * i + a + 1) * P]
            k = H["k"][1][rows, :].rearrange("p (r c) -> p r c", c=64)[:, ks:ks + nk, k0:k0 + 40]
            si, ps, pf = pS.take()
            t = self.pe.op(lambda e: e.matmul(ps[:, 0:N], q, k, start=True, stop=True), H["q"][2], H["k"][2], pf)
            bi, s, sf = sr.take()
            tab = H["tab"][:, hh, a, off:off + N]
            t = self.dve.op(lambda e: e.tensor_tensor_reduce(
                out=s[:, 0:N], in0=ps[:, 0:N], in1=tab, scale=1.0, scalar=-3.0e38, op0=ALU.add, op1=ALU.max,
                accum_out=st[:, n, 0:1]), t, H["t"], sf)
            pS.free[si] = [t]
            tn = self.dve.op(lambda e: e.tensor_scalar(st[:, n, 1:2], st[:, n, 0:1], -1.0, None, ALU.mult), t)
            pi, p, pff = pr.take()
            te = self.act.op(lambda e: e.activation(p[:, 0:N], s[:, 0:N], ACT.Exp, bias=st[:, n, 1:2],
                                                    accum_out=st[:, n, 2:3]), tn, t, pff)
            sr.free[bi] = [te]
            d.update(nk=nk, p=p, pi=pi, te=te)
            if n % 32 == 31:
                tabs.free[H["ti"]] = [t]
                qr.free[H["q"][0]] = kr.free[H["k"][0]] = [(self.pe.sem, self.pe.n)]

        def stage_b(n):
            d = info[n]
            nj = d["nk"] // 3
            qi, ps, pf = pT.take()
            for j in range(nj):
                t = self.pe.op(lambda e, j=j: e.transpose(ps[0:120, j * P:(j + 1) * P], d["p"][:, j * 120:(j + 1) * 120],
                                                          ident[:]), d["te"], pf, t_id)
            pr.free[d["pi"]] = [t]
            i, pt, f = ptr.take()
            if n % 2:
                te = self.act.op(lambda e: e.activation(pt[:, 0:nj * P], ps[0:120, 0:nj * P], ACT.Copy), t, f)
            else:
                te = self.dve.op(lambda e: e.tensor_copy(pt[:, 0:nj * P], ps[0:120, 0:nj * P]), t, f)
            pT.free[qi] = [te]
            d.update(pt=pt, pti=i, tpt=te)

        def stage_c(n):
            hp, i, a, hh = tiles[n]
            d = info[n]
            nj = d["nk"] // 3
            if hh == 0:
                d["oi"], d["o"], f = pO.take()
                d["ri"], d["or"], rf = orr.take()
            else:
                d["oi"], d["o"], d["ri"], d["or"] = (info[n - 1][x] for x in ("oi", "o", "ri", "or"))
                f, rf = [], info[n - 1]["rf"]
            d["rf"] = rf
            po = d["o"]
            for j in range(nj):
                t = self.pe.op(lambda e, j=j: e.matmul(po[:, 64 * hh:64 * hh + 64], d["pt"][:, j * P:(j + 1) * P],
                                                       d["v"][:, j, 64 * hh:64 * hh + 64], start=(j == 0),
                                                       stop=(j == nj - 1)), d["tpt"], d["tv"], f)
            ptr.free[d["pti"]] = [t]
            if hh == 0:
                return
            vr.free[d["vi"]] = [t]
            tr = self.dve.op(lambda e: e.reciprocal(st[:, n - 1:n + 1, 3:4], st[:, n - 1:n + 1, 2:3]),
                             d["te"], info[n - 1]["te"])
            d["ton"] = self.dve.op(lambda e: e.tensor_tensor(
                d["or"][:].rearrange("p (h e) -> p h e", h=2), po[:, 0:P].rearrange("p (h e) -> p h e", h=2),
                st[:, n - 1:n + 1, 3:4].to_broadcast([P, 2, 64]), ALU.mult), t, tr, rf)
            pO.free[d["oi"]] = [d["ton"]]

        yb = {}

        def stage_d(n):
            hp, i, a, hh = tiles[n]
            if hh == 0:
                return
            d = info[n]
            H = heads[hp]
            xi, px, f = pX.take()
            t = self.pe.op(lambda e: e.transpose(px[:, 0:P], d["or"][:], ident[:]), d["ton"], f)
            orr.free[d["ri"]] = [t]
            if a == 0:
                yb[0] = yr.take()
            yi, y, yf = yb[0]
            c0 = 32 * a
            z = H["z"][1][:].rearrange("p (r c) -> p r c", c=64)[:, 4 * i:4 * i + 4, c0:c0 + 32]
            t = self.dve.op(lambda e: e.tensor_tensor(y[:].rearrange("p (r c) -> p r c", c=64)[:, :, c0:c0 + 32],
                                                      px[:, 0:P].rearrange("p (r c) -> p r c", c=32), z, ALU.mult),
                            t, H["z"][2], yf if a == 0 else [])
            pX.free[xi] = [t]
            if a == 1:
                yr.free[yi] = [self.store(self.y2T[hp * P:(hp + 1) * P, i * 256:(i + 1) * 256], y[:], yr.slots[yi], t)]
            if n % 32 == 31:
                zr.free[H["z"][0]] = [t]

        prep(0)
        for n in range(128 + 4):
            if n % 32 == 8 and n // 32 + 1 < 4 and n // 32 >= 0:
                if n < 128:
                    prep(n // 32 + 1)
            if n < 128:
                stage_a(n)
            if 0 <= n - 1 < 128:
                stage_b(n - 1)
            if 0 <= n - 2 < 128:
                stage_c(n - 2)
            if 0 <= n - 4 < 128:
                stage_d(n - 4)

    def ml_block(self):
        dve, act, pe, pool, sp = self.dve, self.act, self.pe, self.pool, self.sp
        C = NT
        ident, t_id = self.identity()
        ones = self.sb("ones", [P, P])
        zero = self.sb("zero", [P, P])
        t_1 = pool.op(lambda e: e.memset(ones[:], 1.0))
        t_0 = pool.op(lambda e: e.memset(zero[:], 0.0))
        mask = [self.sb(f"mask{d}", [P, 4, P]) for d in range(2)]
        t_mask = []
        for d in range(2):
            t = pool.op(lambda e, d=d: e.memset(mask[d][:], 0.0))
            s = 1 if d == 0 else -1
            t_mask.append(pool.op(lambda e, d=d, s=s: e.affine_select(
                out=mask[d][:], in_=mask[d][:], compare_op=ALU.is_ge, fill=NEG, base=0,
                pattern=[[0, 4], [s, P]], channel_multiplier=-s), t))
        G = self.sb("G", [P, C, 16])
        tG = sp.dma(self.slot(), G[:].rearrange("p c g -> p (c g)"), self.gt)
        kC = self.sb("kC", [P, 4, S])
        tk = [sp.dma(self.slot(), kC[:, h, :], self.s["mk"][h * P:(h + 1) * P, :]) for h in range(4)]
        v1 = self.sb("v1", [P, C, 4, P + 1])
        tv = [sp.dma(self.slot(), v1[:, c, :, 0:P], self.s["mv"][c * P:(c + 1) * P, :].rearrange("t (h e) -> t h e", h=4))
              for c in range(C)]
        tv1 = pool.op(lambda e: e.memset(v1[:, :, :, P:P + 1], 1.0))
        kT = self.sb("kT", [P, C, 4, P])
        Cb = self.sb("Cb", [P, C, 4, P + 1])
        pA = self.psring("pA", 1)
        pB = self.psring("pB", 1)
        pU = self.psring("pU", 2)

        gi = self.sb("gi", [P, 2, 2, 4, C])
        tgi = []
        for f in range(2):
            for d in range(2):
                tgi.append(dve.op(lambda e, f=f, d=d: e.tensor_copy(
                    gi[:, f, d, :, :], G[:, :, 8 * d + 4 * f:8 * d + 4 * f + 4].rearrange("p c h -> p h c")), tG))
        X = {n: self.sb(n, [P, P]) for n in ("I", "F", "lf", "b", "u", "M", "nN", "w", "em")}

        def turn(dst, src, ring, *ts):
            i, pb, f = ring.take()
            t = pe.op(lambda e: e.transpose(pb[:, 0:P], src, ident[:]), t_id, f, *ts)
            t = dve.op(lambda e: e.tensor_copy(dst, pb[:, 0:P]), t)
            ring.free[i] = [t]
            return t

        tI = turn(X["I"][:], gi[:, 0].rearrange("p d h c -> p (d h c)"), pA, tgi)
        tF = turn(X["F"][:], gi[:, 1].rearrange("p d h c -> p (d h c)"), pB, tgi)
        t = act.op(lambda e: e.activation(X["w"][:], X["F"][:], ACT.Abs), tF)
        t = act.op(lambda e: e.activation(X["em"][:], X["w"][:], ACT.Exp, scale=-1.0), t)
        t = act.op(lambda e: e.activation(X["u"][:], X["em"][:], ACT.Ln, bias=1.0), t)
        tlf = dve.op(lambda e: e.scalar_tensor_tensor(out=X["lf"][:], in0=X["F"][:], scalar=0.0, in1=X["u"][:],
                                                      op0=ALU.min, op1=ALU.subtract), t, tF)

        def both(fn, *ts):
            return [dve.op(lambda e, r=r, o=o: fn(e, r, o), *ts)
                    for r, o in ((slice(0, 64), slice(None)), (slice(64, 128), slice(None, None, -1)))]

        tb_ = both(lambda e, r, o: e.tensor_tensor_scan(X["b"][r, o], ones[r, :], X["lf"][r, o], 0.0,
                                                        ALU.mult, ALU.add), tlf, t_1)
        tu = dve.op(lambda e: e.tensor_tensor(X["u"][:], X["I"][:], X["b"][:], ALU.subtract), tI, tb_)
        tM = both(lambda e, r, o: e.tensor_tensor_scan(X["M"][r, o], zero[r, :], X["u"][r, o], -3.0e38,
                                                       ALU.add, ALU.max), tu, t_0)
        L = self.sb("L", [P, 8])
        tl = []
        for r, z in ((slice(0, 64), P - 1), (slice(64, 128), 0)):
            tl.append(dve.op(lambda e, r=r, z=z: e.tensor_copy(L[r, 0:1], X["b"][r, z:z + 1]), tb_))
            tl.append(dve.op(lambda e, r=r, z=z: e.tensor_copy(L[r, 1:2], X["M"][r, z:z + 1]), tM))
        tl.append(dve.op(lambda e: e.tensor_tensor(L[:, 2:3], L[:, 0:1], L[:, 1:2], ALU.add), tl))
        R = self.sb("R", [1, 4, P])
        tR = []
        for x, (col, ring) in enumerate(((0, pA), (2, pB))):
            i, pb, f = ring.take()
            t = pe.op(lambda e, pb=pb, col=col: e.matmul(pb[0:1, 0:P], L[:, col:col + 1], ident[:], start=True, stop=True),
                      tl, f, t_id)
            t = dve.op(lambda e, pb=pb, x=x: e.tensor_copy(R[:, x, :], pb[0:1, 0:P]), t)
            ring.free[i] = [t]
            tR.append(t)
        tm = []
        for n in range(8):
            o = slice(n * C, (n + 1) * C) if n < 4 else slice((n + 1) * C - 1, n * C - 1 if n * C > 0 else None, -1)
            tm.append(dve.op(lambda e, o=o: e.tensor_tensor_scan(R[:, 2, o], R[:, 0, o], R[:, 1, o], 0.0, ALU.add, ALU.max), tR))
        t = dve.op(lambda e: e.memset(R[:, 3, :], 0.0))
        Rp = R[:, 3, :].rearrange("p (n c) -> p n c", c=C)
        Rn = R[:, 2, :].rearrange("p (n c) -> p n c", c=C)
        tp = [dve.op(lambda e: e.tensor_copy(Rp[:, 0:4, 1:C], Rn[:, 0:4, 0:C - 1]), tm, t),
              dve.op(lambda e: e.tensor_copy(Rp[:, 4:8, 0:C - 1], Rn[:, 4:8, 1:C]), tm, t)]
        i, pb, f = pA.take()
        t = pe.op(lambda e, pb=pb: e.matmul(pb[:, 0:1], R[:, 3, :], ones[0:1, 0:1], start=True, stop=True), tp, t_1, f)
        tmp = dve.op(lambda e, pb=pb: e.tensor_copy(L[:, 3:4], pb[:, 0:1]), t)
        pA.free[i] = [tmp]
        tN = dve.op(lambda e: e.tensor_scalar(X["nN"][:], X["M"][:], L[:, 3:4], -1.0, ALU.max, ALU.mult), tM, tmp)
        tNl = dve.op(lambda e: e.tensor_scalar(L[:, 4:5], L[:, 1:2], L[:, 3:4], -1.0, ALU.max, ALU.mult), tl, tmp)
        tNd = self.store(self.nN, X["nN"][:], self.slot(True), tN)
        tw = act.op(lambda e: e.activation(X["w"][:], X["u"][:], ACT.Exp, bias=L[:, 4:5]), tu, tNl, tlf)
        tdc = act.op(lambda e: e.activation(L[:, 5:6], L[:, 3:4], ACT.Exp, bias=L[:, 4:5]), tNl)
        t = dve.op(lambda e: e.tensor_tensor(X["I"][:], X["nN"][:], X["b"][:], ALU.subtract), tN, tb_, tu)
        tem = act.op(lambda e: e.activation(X["em"][:], X["I"][:], ACT.Exp), t)
        uT, wT, eT = (self.sb(n, [P, 8, C]) for n in ("uT", "wT", "eT"))
        flat2 = lambda a: a[:].rearrange("p n c -> p (n c)")
        tuT, twT, teT = (turn(flat2(a), X[n][:], r, ts) for a, n, r, ts in
                         ((wT, "w", pA, tw), (uT, "u", pB, tu), (eT, "em", pA, tem)))
        tuT, twT = twT, tuT
        mpB, dcB = (self.sb(n, [P, 8, C]) for n in ("mpB", "dcB"))
        dg = self.sb("dg", [P, 2, P])
        tB = []
        for x, (col, a, ts) in enumerate(((3, mpB, tmp), (5, dcB, tdc))):
            t = dve.op(lambda e, x=x, col=col: e.tensor_scalar(dg[:, x, :], ident[:], L[:, col:col + 1], None, ALU.mult), ts, t_id)
            i, pb, f = pB.take()
            t = pe.op(lambda e, pb=pb, x=x: e.matmul(pb[:, 0:P], ones[:], dg[:, x, :], start=True, stop=True), t, f, t_1)
            t = dve.op(lambda e, pb=pb, a=a: e.tensor_copy(flat2(a), pb[:, 0:P]), t)
            pB.free[i] = [t]
            tB.append(t)

        SC = P ** -0.5
        wv = self.ring("wv", 2, [P, 4, P + 1], dma=False)
        tkT = {}

        def kturn(c):
            i, pb, f = pA.take()
            for h in range(4):
                t = pe.op(lambda e, h=h: e.transpose(pb[:, h * P:(h + 1) * P], kC[:, h, c * P:(c + 1) * P], ident[:]),
                          tk[h], f, t_id)
            tkT[c] = act.op(lambda e: e.activation(kT[:, c].rearrange("p h d -> p (h d)"), pb[:], ACT.Copy, scale=SC), t)
            pA.free[i] = [tkT[c]]

        def update(d, c, new, old, t_old, f_new):
            i, w, f = wv.take()
            t = pool.op(lambda e: e.tensor_tensor(w[:], v1[:, c], wT[:, 4 * d:4 * d + 4, c:c + 1].to_broadcast([P, 4, P + 1]),
                                                  ALU.mult), tv[c], tv1, twT, f)
            out, tr = [], []
            for g in range(2):
                q, pb, pf = pU.take()
                for h in (2 * g, 2 * g + 1):
                    tt = pe.op(lambda e, h=h, g=g, pb=pb: e.matmul(
                        pb[:, (h - 2 * g) * (P + 1):(h - 2 * g + 1) * (P + 1)], kT[:, c, h, :], w[:, h, :],
                        start=True, stop=True), t, tkT[c], pf)
                tr.append(tt)
                for h in (2 * g, 2 * g + 1):
                    src = pb[:, (h - 2 * g) * (P + 1):(h - 2 * g + 1) * (P + 1)]
                    if old is None:
                        o = dve.op(lambda e, h=h, src=src: e.tensor_copy(new[:, h, :], src), tt, f_new)
                    else:
                        o = dve.op(lambda e, h=h, src=src: e.scalar_tensor_tensor(
                            out=new[:, h, :], in0=old[:, h, :], scalar=dcB[:, 4 * d + h, c:c + 1], in1=src,
                            op0=ALU.mult, op1=ALU.add), tt, t_old, tB, f_new)
                    out.append(o)
                pU.free[q] = [o]
            wv.free[i] = tr
            return out

        tCb = {C - 1: None}
        for c in range(C - 1, 0, -1):
            kturn(c)
            tCb[c - 1] = update(1, c, Cb[:, c - 1], None if c == C - 1 else Cb[:, c], tCb[c], None)
        kturn(0)

        Cf = self.ring("Cf", 2, [P, 4, P + 1], dma=False)
        qr = self.ring("q", 2, [P, 4, P])
        orr = self.ring("o", 2, [P, 4, P])
        zr = self.ring("z", 2, [P, 4, P])
        nb = self.ring("nb", 3, [P, 4, P])
        ab = self.ring("ab", 2, [P, 4, P], dma=False)
        eb = self.ring("eb", 4, [P, 4, P], dma=False)
        ib = self.ring("ib", 4, [P, 4, P], dma=False)
        hb = self.ring("hb", 2, [P, 4, P], dma=False)
        yb = self.ring("yb", 2, [P, 4, P], out=True)
        rd = self.sb("rd", [P, C, 2, 4])
        bn = self.sb("bn", [P, C, 4, 6])
        mv = self.sb("mv", [P, C, 4, 2])
        rs = self.sb("rs", [P, C, 4])
        pN = self.psring("pN", 4, (P, 2 * (P + 1)))
        A = {}

        def stage_a(c):
            cs = slice(c * P, (c + 1) * P)
            q = self.load(qr, self.s["mq"].rearrange("(h d) t -> d h t", d=P)[:, :, cs])
            si, ps, pf = pA.take()
            for h in range(4):
                t = pe.op(lambda e, h=h: e.matmul(ps[:, h * P:(h + 1) * P], kC[:, h, cs], q[1][:, h, :],
                                                  start=True, stop=True), q[2], tk[h], pf)
            tS = t
            A[c] = dict(q=q, dirs=[])
            frees = []
            for d in range(2):
                src = self.nN.rearrange("(n c) t -> n c t", c=C)[4 * d:4 * d + 4, c, :]
                n = self.load(nb, src.partition_broadcast(P), after=[tNd])
                ai, a, af = ab.take()
                tm_ = pool.op(lambda e, a=a, n=n, d=d: e.tensor_tensor(a[:], n[1][:], mask[d][:], ALU.add), n[2], t_mask[d], af)
                ei, x, ef = eb.take()
                for h in range(4):
                    te = act.op(lambda e, a=a, x=x, d=d, h=h: e.activation(
                        x[:, h, :], a[:, h, :], ACT.Exp, bias=uT[:, 4 * d + h, c:c + 1]), tm_, tuT, ef)
                ab.free[ai] = [te]
                tP = dve.op(lambda e, x=x: e.scalar_tensor_tensor(
                    out=x[:], in0=ps[:].rearrange("p (h t) -> p h t", h=4), scalar=SC, in1=x[:],
                    op0=ALU.mult, op1=ALU.mult), tS, te)
                frees.append(tP)
                ii, y, yf = ib.take()
                tq = None
                if not (d == 0 and c == 0 or d == 1 and c == C - 1):
                    t = pool.op(lambda e, y=y, n=n, d=d: e.tensor_tensor(
                        y[:], n[1][:], mpB[:, 4 * d:4 * d + 4, c:c + 1].to_broadcast([P, 4, P]), ALU.add), n[2], tB, yf)
                    tn = t
                    t = act.op(lambda e, y=y: e.activation(y[:], y[:], ACT.Exp), t)
                    tq = dve.op(lambda e, y=y: e.tensor_tensor(y[:], y[:], q[1][:], ALU.mult), t, q[2])
                    nb.free[n[0]] = [tm_, tn]
                else:
                    ib.free[ii] = yf
                    nb.free[n[0]] = [tm_]
                A[c]["dirs"].append(dict(x=x, ei=ei, tP=tP, y=y, ii=ii, tq=tq))
            pA.free[si] = frees
            qr.free[q[0]] = [tS] + [D_["tq"] for D_ in A[c]["dirs"]]

        cf = [None, None, None]

        def stage_b(c):
            a = A[c]
            a["num"] = []
            for d in range(2):
                D_ = a["dirs"][d]
                st_, t_st = (cf[0], cf[1]) if d == 0 else (Cb[:, c], tCb[c])
                for g in range(2):
                    i, pb, f = pN.take()
                    for h in (2 * g, 2 * g + 1):
                        o = pb[:, (h - 2 * g) * (P + 1):(h - 2 * g + 1) * (P + 1)]
                        inter = D_["tq"] is not None
                        t = pe.op(lambda e, o=o, D_=D_, h=h, inter=inter: e.matmul(
                            o, D_["x"][:, h, :], v1[:, c, h, :], start=True, stop=not inter), D_["tP"], tv[c], tv1, f)
                        if inter:
                            t = pe.op(lambda e, o=o, D_=D_, h=h, st_=st_: e.matmul(
                                o, D_["y"][:, h, :], st_[:, h, :], start=False, stop=True), D_["tq"], t_st)
                    a["num"].append((i, pb, t))
                eb.free[D_["ei"]] = [t]
                if D_["tq"] is not None:
                    ib.free[D_["ii"]] = [t]
            if c < C - 1:
                used = (pe.sem, pe.n)
                i, new, f = Cf.take()
                if cf[2] is not None:
                    Cf.free[cf[2]] = [used]
                t = update(0, c, new, cf[0], cf[1], f)
                if cf[2] is not None:
                    Cf.free[cf[2]] += t
                cf[0], cf[1], cf[2] = new, t, i

        def stage_c(c):
            a = A[c]
            cs = slice(c * P, (c + 1) * P)
            o = self.load(orr, self.s["mo"][cs, :].rearrange("t (h e) -> t h e", h=4))
            z = self.load(zr, self.s["mz"].rearrange("(h e) t -> e h t", e=P)[:, :, cs])
            hi, hbuf, hf = hb.take()
            tH = hf
            for d in range(2):
                tr = []
                for g in range(2):
                    i, pb, t = a["num"][2 * d + g]
                    den = pb[:].rearrange("p (h e) -> p h e", h=2)[:, :, P:P + 1]
                    r = rd[:, c, d, 2 * g:2 * g + 2].unsqueeze(2)
                    x = dve.op(lambda e, den=den, d=d, g=g, r=r: e.scalar_tensor_tensor(
                        out=r, in0=den, scalar=-1.0, in1=eT[:, 4 * d + 2 * g:4 * d + 2 * g + 2, c:c + 1],
                        op0=ALU.mult, op1=ALU.max), t, teT)
                    tr.append(dve.op(lambda e, den=den, r=r: e.tensor_tensor(r, r, den, ALU.max), x))
                tr = dve.op(lambda e, d=d: e.reciprocal(rd[:, c, d, :], rd[:, c, d, :]), tr)
                nH = []
                for g in range(2):
                    i, pb, t = a["num"][2 * d + g]
                    num = pb[:].rearrange("p (h e) -> p h e", h=2)[:, :, 0:P]
                    if d == 0:
                        x = dve.op(lambda e, num=num, g=g: e.tensor_tensor(
                            hbuf[:, 2 * g:2 * g + 2, :], num,
                            rd[:, c, 0, 2 * g:2 * g + 2].unsqueeze(2).to_broadcast([P, 2, P]), ALU.mult), tr, t, tH)
                        nH.append(x)
                    else:
                        for h in range(2):
                            x = dve.op(lambda e, num=num, g=g, h=h: e.scalar_tensor_tensor(
                                out=hbuf[:, 2 * g + h, :], in0=num[:, h, :], scalar=rd[:, c, 1, 2 * g + h:2 * g + h + 1],
                                in1=hbuf[:, 2 * g + h, :], op0=ALU.mult, op1=ALU.add), tr, t, tH)
                            nH.append(x)
                    pN.free[i] = [x]
                tH = nH
            t = pool.op(lambda e: e.tensor_tensor(hbuf[:], hbuf[:], o[1][:], ALU.mult), tH, o[2])
            orr.free[o[0]] = [t]
            tb = [dve.op(lambda e, h=h: e.bn_stats(bn[:, c, h, :], hbuf[:, h, :]), t) for h in range(4)]
            tb = [dve.op(lambda e, h=h: e.bn_aggr(mv[:, c, h, :], bn[:, c, h, :]), tb[h]) for h in range(4)]
            t = dve.op(lambda e: e.tensor_scalar(rs[:, c, :].unsqueeze(2), mv[:, c, :, 1:2], EPS, None, ALU.add), tb)
            t = act.op(lambda e: e.activation(rs[:, c, :], rs[:, c, :], ACT.Ln), t)
            t = act.op(lambda e: e.activation(rs[:, c, :], rs[:, c, :], ACT.Exp, scale=-0.5), t)
            tn = [dve.op(lambda e, h=h: e.tensor_scalar(hbuf[:, h, :], hbuf[:, h, :], mv[:, c, h, 0:1], rs[:, c, h:h + 1],
                                                        ALU.subtract, ALU.mult), t) for h in range(4)]
            a.update(hi=hi, hbuf=hbuf, tn=tn, z=z)

        def stage_d(c):
            a = A[c]
            z = a["z"]
            i, pb, f = pB.take()
            for h in range(4):
                t = pe.op(lambda e, h=h: e.transpose(pb[:, h * P:(h + 1) * P], a["hbuf"][:, h, :], ident[:]), a["tn"], f, t_id)
            hb.free[a["hi"]] = [t]
            yi, y, yf = yb.take()
            t = dve.op(lambda e: e.tensor_tensor(y[:], pb[:].rearrange("p (h t) -> p h t", h=4), z[1][:], ALU.mult),
                       t, z[2], yf)
            pB.free[i] = [t]
            zr.free[z[0]] = [t]
            yb.free[yi] = [self.store(self.y2T[4 * P:8 * P, :].rearrange("(h e) t -> e h t", e=P)[:, :, c * P:(c + 1) * P],
                                      y[:], yb.slots[yi], t)]

        stage_a(0)
        for c in range(C):
            if c + 1 < C:
                stage_a(c + 1)
            stage_b(c)
            stage_c(c)
            if c >= 1:
                stage_d(c - 1)
        stage_d(C - 1)


def program(nc, io, out, scratch="Internal", upto=9):
    kr = Kernel(nc, io, scratch)
    kr.out = out
    kr.yT = kr.dram("yT", (D, S))
    kr.mod = kr.dram("mod", (1, 3 * D))
    kr.h = kr.dram("h", (S, D))
    kr.hT2 = kr.dram("hT2", (D, S))
    kr.gt = kr.dram("gt", (P, NT * 16))
    kr.s = {n: kr.dram(n, (S, W) if n in ("nv", "mv", "mo") else (W, S))
            for n in ("nq", "nk", "nv", "nz", "mq", "mk", "mv", "mo", "mz")}
    kr.rpb = kr.dram("rpbp", (32, RPB))
    kr.nN = kr.dram("nN", (P, P))
    kr.y2T = kr.dram("y2T", (D, S))
    with kr.ctx:
        kr.phase(kr.pool_block)
        kr.phase(kr.ada)
        kr.phase(lambda: kr.out_block(io["pool_out_w"][0], kr.yT, io["x"][0], False))
        if upto >= 4:
            kr.phase(kr.in_block)
        if upto >= 5:
            kr.phase(kr.bias_rows)
            kr.phase(kr.na_block)
        if upto >= 6:
            kr.phase(kr.ml_block)
        if upto >= 7:
            kr.phase(lambda: kr.out_block(io["w_out_2"][0], kr.y2T, kr.h, True))


_INS = ["x", "norm_w", "pool_in_w", "pool_group_w", "pool_group_b", "pool_scale", "pool_out_w", "final_norm_w",
        "c_2", "w_ada_2", "b_ada_2", "norm_w_2", "w_in_2", "b_in_2", "conv_w_2", "conv_b_2", "rpb_2", "ml_norm_w_2",
        "w_out_2", "final_norm_w_2"]


def kernel(**inputs):
    import numpy as np
    import concourse.bacc as bacc
    from concourse.bass_utils import run_bass_kernel_spmd

    nc = bacc.Bacc("TRN2", target_bir_lowering=False, num_devices=1)
    arrays, io = {}, {}
    for name in _INS:
        a = np.ascontiguousarray(inputs[name])
        arrays[f"in_{name}"] = a
        io[name] = nc.dram_tensor(f"in_{name}", a.shape, mybir.dt.from_np(a.dtype), kind="ExternalInput").ap()
    out = nc.dram_tensor("out", (1, S, D), F32, kind="ExternalOutput").ap()
    program(nc, io, out)
    r = run_bass_kernel_spmd(nc, [arrays], core_ids=[0])
    return r.results[0]["out"]
```

```python
from contextlib import ExitStack

import concourse.bass as bass
from concourse import mybir

F32 = mybir.dt.float32
F32R = mybir.dt.float32r
ALU = mybir.AluOpType
ACT = mybir.ActivationFunctionType
AX = mybir.AxisListType

P = 128
S = 2048
D = 1024
KT = D // P
NT = S // P
TB = 4
W = 512
EPS = 1e-6
NEG = -1.0e30
NA_H = 8
ML_H = 4
RPB = 128 + NA_H * 465


class Engine:

    def __init__(self, name, sem):
        self.name, self.sem, self.n, self.q, self.seen = name, sem, 0, [], {}

    def op(self, fn, *waits):
        self.q.append([fn, list(flat(waits)), (self.sem, 1)])
        self.n += 1
        return (self.sem, self.n)

    def quiet(self, fn, *waits):
        self.q.append([fn, list(flat(waits)), None])

    def dma(self, slot, out, in_, *waits, slow=False):
        slot.n += 16
        self.q.append([lambda e: e.dma_start(out, in_, allow_slow_non_contiguous=slow), list(flat(waits)), (slot.sem, 16)])
        return (slot.sem, slot.n)

    def wait(self, *waits):
        self.q.append([None, list(flat(waits)), None])

    def emit(self, e):
        for fn, waits, inc in self.q:
            for w in waits:
                if self.seen.get(id(w[0]), 0) < w[1]:
                    e.wait_ge(w[0], w[1])
                    self.seen[id(w[0])] = w[1]
            if fn is not None:
                ins = fn(e)
                if inc is not None:
                    ins.then_inc(inc[0], inc[1])
        self.q = []


def flat(ws):
    for w in ws:
        if isinstance(w, list):
            yield from flat(w)
        elif w is not None:
            yield w


class Slot:

    def __init__(self, sem):
        self.sem, self.n = sem, 0


class Ring:

    def __init__(self, bufs, slots=None):
        self.bufs, self.slots, self.i = bufs, slots, 0
        self.free = [[] for _ in bufs]

    def take(self):
        i = self.i % len(self.bufs)
        self.i += 1
        f, self.free[i] = self.free[i], None
        assert f is not None, "a buffer is taken again before its readers are queued"
        return i, self.bufs[i], f


class Kernel:
    def __init__(self, nc, io, scratch_kind):
        self.nc, self.io = nc, io
        self.ctx = ExitStack()
        self.pe, self.act, self.dve, self.pool, self.sp = (
            Engine(n, self.ctx.enter_context(nc.semaphore(f"done_{n}"))) for n in ("pe", "act", "dve", "pool", "sp"))
        self.nsem = 0
        self.slots = {False: [], True: []}
        self.pending = []
        self.kind = scratch_kind
        self.t_junk = None

    def slot(self, out=False):
        have, n = self.slots[out], self.nslot[out]
        if n == len(have):
            have.append(Slot(self.ctx.enter_context(self.nc.semaphore(f"dma_{'out' if out else 'in'}{n}"))))
        self.nslot[out] += 1
        return have[n]

    def dram(self, name, shape):
        return self.nc.dram_tensor(name, shape, F32, kind=self.kind).ap()

    def phase(self, fn):
        self.nslot = {False: 0, True: 0}
        self.pending = []
        with ExitStack() as ctx:
            self.px = ctx
            fn()
            self.sp.wait(self.pending)
            with self.nc.Block() as block:
                block.sync(self.sp.emit)
                block.scalar(self.act.emit)
                block.gpsimd(self.pool.emit)
                block.tensor(self.pe.emit)
                block.vector(self.dve.emit)

    def sb(self, name, shape, dt=F32):
        self.nsem += 1
        return self.px.enter_context(self.nc.sbuf_tensor(f"{name}_{self.nsem}", shape, dt))

    def ps(self, name, shape=(P, W), dt=F32):
        self.nsem += 1
        return self.px.enter_context(self.nc.psum_tensor(f"{name}_{self.nsem}", list(shape), dt))

    def ring(self, name, n, shape, dt=F32, dma=True, out=False):
        bufs = [self.sb(f"{name}{i}", shape, dt) for i in range(n)]
        return Ring(bufs, [self.slot(out) for _ in range(n)] if dma else None)

    def psring(self, name, n, shape=(P, W), dt=F32):
        return Ring([self.ps(f"{name}{i}", shape, dt) for i in range(n)])

    def load(self, ring, src, eng=None, dst=lambda b: b[:], after=()):
        i, b, free = ring.take()
        t = (eng or self.sp).dma(ring.slots[i], dst(b), src, free, *after)
        return i, b, t

    def store(self, dst, src, slot, *waits, eng=None):
        t = (eng or self.pool).dma(slot, dst, src, *waits)
        self.pending.append(t)
        return t

    def split(self, hi, lo, x, *waits):
        a = self.act.op(lambda e: e.activation(hi, x, ACT.Copy), *waits)
        d = self.dve.op(lambda e: e.tensor_tensor(lo, x, hi.bitcast(F32), ALU.subtract), a)
        return [a, d]

    def mm3(self, ps, lh, ll, rh, rl, first, last, *waits):
        pe = self.pe
        pe.quiet(lambda e: e.matmul(ps, lh, rh, start=first, stop=False), *waits)
        pe.quiet(lambda e: e.matmul(ps, lh, rl, start=False, stop=False))
        if last:
            return pe.op(lambda e: e.matmul(ps, ll, rh, start=False, stop=True))
        pe.quiet(lambda e: e.matmul(ps, ll, rh, start=False, stop=False))

    def identity(self):
        ident = self.sb("ident", [P, P])
        t = self.pool.op(lambda e: e.memset(ident[:], 0.0))
        t = self.pool.op(lambda e: e.affine_select(out=ident[:], in_=ident[:], compare_op=ALU.not_equal, fill=1.0,
                                                   base=0, pattern=[[-1, P]], channel_multiplier=1), t)
        return ident, t

    def row(self, vec, n, name="row"):
        t = self.sb(name, [P, n])
        return t, self.sp.dma(self.slot(), t[:], vec.partition_broadcast(P))

    def cols(self, vec, n, name="cols"):
        t = self.sb(name, [P, n])
        return t, self.sp.dma(self.slot(), t[:], vec.rearrange("(j p) -> p j", p=P), slow=True)

    def rstd(self, out, tmp, ssq, n, *waits):
        a = self.dve.op(lambda e: e.tensor_scalar(tmp, ssq, 1.0 / n, EPS, ALU.mult, ALU.add), *waits)
        return self.pool.op(lambda e: e.tensor_tensor(out, tmp, self.mhalf[:, 0:1], ALU.pow), a, self.t_mhalf)

    def minus_half(self, n=1):
        self.mhalf = self.sb("mhalf", [P, n])
        self.t_mhalf = self.pool.op(lambda e: e.memset(self.mhalf[:], -0.5))

    def sumsq(self, out, junk, x, *waits):
        self.t_junk = self.act.op(lambda e: e.activation(junk, x, ACT.Square, accum_out=out), self.t_junk, *waits)
        return self.t_junk

    def pool_block(self):
        hT = self.sb("hT", [P, 2, KT, S], F32R)
        hr = {}
        x = self.io["x"][0]
        with ExitStack() as sub:
            keep, self.px = self.px, sub
            ident, t_id = self.identity()
            xr = self.ring("x", 4, [P, D])
            xn = self.ring("xn", 2, [P, D], dma=False)
            junk = self.ps("junk", [P, D])
            st = self.sb("st", [P, NT, 3])
            tp = self.psring("tp", 4)
            self.minus_half()
            loads = {}

            def ld(m):
                i, b, t = self.load(xr, x[m * P:(m + 1) * P, :])
                loads[m] = (i, b, t, self.sumsq(st[:, m, 0:1], junk[:], b[:], t))

            def stat(m):
                loads[m] += (self.rstd(st[:, m, 2:3], st[:, m, 1:2], st[:, m, 0:1], D, loads[m][3]),)

            for m in range(2):
                ld(m)
                stat(m)
            nw, t_nw = self.row(self.io["norm_w"][0], D)
            for m in range(NT):
                if m + 2 < NT:
                    ld(m + 2)
                i, b, t, _, tr = loads.pop(m)
                j, n, nf = xn.take()
                tn = self.dve.op(lambda e, n=n, b=b, m=m: e.scalar_tensor_tensor(
                    out=n[:], in0=b[:], scalar=st[:, m, 2:3], in1=nw[:], op0=ALU.mult, op1=ALU.mult), tr, t_nw, t, nf)
                xr.free[i] = [tn]
                if m + 2 < NT:
                    stat(m + 2)
                for g in range(2):
                    q, pb, pf = tp.take()
                    for k in range(4):
                        kk = 4 * g + k
                        f = lambda e, pb=pb, n=n, k=k, kk=kk: e.transpose(
                            pb[:, k * P:(k + 1) * P], n[:, kk * P:(kk + 1) * P], ident[:])
                        if k < 3:
                            self.pe.quiet(f, tn, pf, t_id)
                        else:
                            tt = self.pe.op(f)
                    sl = (slice(None), slice(4 * g, 4 * g + 4), slice(m * P, (m + 1) * P))
                    pv = pb[:].rearrange("p (k t) -> p k t", k=4)
                    hr[(m, g)] = self.split(hT[:, 0][sl], hT[:, 1][sl], pv, tt)
                    tp.free[q] = hr[(m, g)]
                xn.free[j] = [tt]
            self.sp.wait(self.pending)
            self.pending = []
            with self.nc.Block() as block:
                block.sync(self.sp.emit)
                block.scalar(self.act.emit)
                block.gpsimd(self.pool.emit)
                block.tensor(self.pe.emit)
                block.vector(self.dve.emit)
            self.px = keep
        self.nslot = {False: 0, True: 0}

        win = self.io["pool_in_w"][0].rearrange("(k p) n -> p k n", p=P)
        gw = self.io["pool_group_w"][0]
        units = self.ring("wu", 4, [P, 2, KT, P], F32R, dma=False)
        raw = self.ring("raw", 2, [P, KT, P])
        graw = self.ring("graw", 1, [P, 2, 256])
        gsp = self.ring("gsp", 1, [P, 2, 2, 256], F32R, dma=False)
        ub = self.ring("ub", 2, [P, 16 + W], dma=False)
        sa = self.ring("sa", 2, [P, 16 + W], dma=False)
        pld = self.ring("pld", 1, [P, 2, 2, W], F32R, dma=False)
        sg = self.ring("sg", 3, [P, W], out=True)
        halo = self.sb("halo", [P, KT, 16])
        invc = self.sb("invc", [P, 4, 16])
        pg = self.psring("pg", 6)
        pm = self.psring("pm", 2)
        t_inv = None
        for g in range(4):
            w = 2 << g
            for c in range(16):
                t_inv = self.pool.op(lambda e, g=g, c=c, w=w: e.memset(invc[:, g, c:c + 1], 1.0 / min(c + 1, w)))
        t_h0 = self.pool.op(lambda e: e.memset(halo[:], 0.0))
        halos = {a: t_h0 for a in range(KT)}
        ada, tables = self.ada(pm), self.bias_tables()

        def unit(col):
            i, r, t = self.load(raw, win[:, :, col:col + P])
            j, u, f = units.take()
            ts = self.split(u[:, 0], u[:, 1], r[:], t, f)
            raw.free[i] = ts
            return j, u, ts

        def unit_cols(g):
            return [g * 256, g * 256 + P, D + g * 256, D + g * 256 + P]

        order = [c for g in range(4) for c in unit_cols(g)]
        ready = {}

        def prefetch(n):
            while len(ready) < min(n, 16):
                u = len(ready)
                ready[u] = unit(order[u])

        def proj(u, tb):
            j, wt, tw = ready[u]
            q, pb, pf = pg.take()
            for k in range(KT):
                t = self.mm3(pb[:], wt[:, 0, k, :], wt[:, 1, k, :], hT[:, 0, k, tb * W:(tb + 1) * W],
                             hT[:, 1, k, tb * W:(tb + 1) * W], k == 0, k == KT - 1, tw, pf)
            if tb == 3:
                units.free[j] = [t]
                prefetch(u + 5)
            return q, pb, t

        def load_gw(g):
            return self.load(graw, gw[g].rearrange("(k p) d -> p k d", p=P))

        prefetch(1)
        gld = load_gw(0)
        gb, t_gb = self.cols(self.io["pool_group_b"][0].rearrange("g c -> (g c)"), KT)
        sc, t_sc = self.cols(self.io["pool_scale"][0], KT)
        prefetch(4)
        for g in range(4):
            gi, gr, tgr = gld
            gj, gs, gf = gsp.take()
            tgs = self.split(gs[:, 0], gs[:, 1], gr[:], tgr, gf)
            graw.free[gi] = tgs
            for tb in range(4):
                pj, pl, plf = pld.take()
                tp2 = []
                for a in range(2):
                    q, pb, t = proj(4 * g + a, tb)
                    ch = 2 * g + a
                    ui, u, uf = ub.take()
                    tu = self.act.op(lambda e, u=u, pb=pb: e.activation(u[:, 16:], pb[:], ACT.Copy), t, uf)
                    pg.free[q] = [tu]
                    th = self.dve.op(lambda e, u=u, ch=ch: e.tensor_copy(u[:, 0:16], halo[:, ch, :]), halos[ch], uf)
                    halos[ch] = self.dve.op(lambda e, u=u, ch=ch: e.tensor_copy(halo[:, ch, :], u[:, W:W + 16]), tu, th)
                    cur, tc, lo = u, [tu, th], 0
                    for l in range(g + 1):
                        s = 1 << l
                        si, nx, sf = sa.take()
                        sa.free[si] = []
                        lo += s
                        tc = self.dve.op(lambda e, nx=nx, cur=cur, lo=lo, s=s: e.tensor_tensor(
                            nx[:, lo:], cur[:, lo:], cur[:, lo - s:16 + W - s], ALU.add), tc, sf)
                        cur = nx
                    c0, tr = 16, None
                    if tb == 0:
                        c0 = 32
                        tr = self.dve.op(lambda e, cur=cur, g=g: e.tensor_tensor(
                            cur[:, 16:32], cur[:, 16:32], invc[:, g, :], ALU.mult), tc, t_inv)
                        tr = self.dve.op(lambda e, cur=cur, u=u: e.tensor_tensor(
                            cur[:, 16:32], cur[:, 16:32], u[:, 16:32], ALU.subtract), tr)
                    tr = self.dve.op(lambda e, cur=cur, u=u, g=g, c0=c0: e.scalar_tensor_tensor(
                        out=cur[:, c0:], in0=cur[:, c0:], scalar=1.0 / (2 << g), in1=u[:, c0:],
                        op0=ALU.mult, op1=ALU.subtract), tc, tr)
                    ub.free[ui] = [tr, halos[ch]]
                    ts = self.split(pl[:, 0, a], pl[:, 1, a], cur[:, 16:], tr, plf)
                    sa.free[si] = ts
                    tp2 += ts
                gates = []
                for a in range(2):
                    q, pb, t = proj(4 * g + 2 + a, tb)
                    i, s, sf = sg.take()
                    t = self.act.op(lambda e, s=s, pb=pb: e.activation(s[:], pb[:], ACT.Silu), t, sf)
                    pg.free[q] = [t]
                    gates.append((i, s, t))
                for a in range(2):
                    ch = 2 * g + a
                    q, pb, pf = pm.take()
                    for k in range(2):
                        t = self.mm3(pb[:], gs[:, 0, k, a * P:(a + 1) * P], gs[:, 1, k, a * P:(a + 1) * P],
                                     pl[:, 0, k], pl[:, 1, k], k == 0, k == 1, tgs, tp2, pf)
                    i, s, tsg = gates[a]
                    ty = self.dve.op(lambda e, s=s, pb=pb, ch=ch: e.scalar_tensor_tensor(
                        out=s[:], in0=pb[:], scalar=gb[:, ch:ch + 1], in1=s[:], op0=ALU.add, op1=ALU.mult), t, tsg, t_gb)
                    pm.free[q] = [ty]
                    ty = self.dve.op(lambda e, s=s, ch=ch: e.tensor_scalar(
                        s[:], s[:], sc[:, ch:ch + 1], None, ALU.mult), ty, t_sc)
                    sg.free[i] = [self.store(self.yT[ch * P:(ch + 1) * P, tb * W:(tb + 1) * W], s[:], sg.slots[i], ty)]
                pld.free[pj] = [t]
                if tb == 2 and g < 3:
                    gld = load_gw(g + 1)
                if tb < 3 or g == 3:
                    for _ in range(5):
                        next(ada, None)
                next(tables, None)
            gsp.free[gj] = [t]
        for step in (ada, tables):
            for _ in step:
                pass

    def ada(self, pr):
        c = self.sb("c", [P, KT])
        ones = self.sb("ones", [P, 2])
        wr = self.ring("w", 2, [P, W])
        acc = self.sb("acc", [P, W])
        b_out = self.slot(True)
        t = self.sp.dma(self.slot(), c[:], self.io["c_2"][0].rearrange("(k p) -> p k", p=P), slow=True)
        t_c = self.act.op(lambda e: e.activation(c[:], c[:], ACT.Silu), t)
        t_1 = self.dve.op(lambda e: e.memset(ones[:], 1.0))
        t_acc = None
        for j in range(6):
            sl = slice(j * W, (j + 1) * W)
            for k in range(KT):
                yield
                i, w, t = self.load(wr, self.io["w_ada_2"][0][k * P:(k + 1) * P, sl])
                if k == 0:
                    ta = self.dve.op(lambda e, w=w: e.tensor_scalar(acc[:], w[:], c[:, 0:1], None, ALU.mult), t, t_c, t_acc)
                else:
                    ta = self.dve.op(lambda e, w=w, k=k: e.scalar_tensor_tensor(
                        out=acc[:], in0=w[:], scalar=c[:, k:k + 1], in1=acc[:], op0=ALU.mult, op1=ALU.add), t, ta)
                wr.free[i] = [ta]
            yield
            i, b, t_b = self.load(wr, self.io["b_ada_2"][:, sl], dst=lambda b: b[0:1, :])
            q, pb, pf = pr.take()
            t_acc = self.pe.op(lambda e, pb=pb: e.matmul(pb[0:1, :], ones[:, 0:1], acc[:], start=True, stop=True), ta, t_1, pf)
            t = self.dve.op(lambda e, pb=pb, b=b: e.tensor_tensor(b[0:1, :], pb[0:1, :], b[0:1, :], ALU.add),
                            t_acc, t_b)
            pr.free[q] = [t]
            wr.free[i] = [self.store(self.mod[:, sl], b[0:1, :], b_out, t)]

    def out_block(self, w_dram, yT_dram, res, last):
        ident, t_id = self.identity()
        wv = w_dram.rearrange("(k p) n -> p k n", p=P)
        raw = self.ring("raw", 4, [P, W])
        ws = self.sb("ws", [P, 2, KT, D], F32R)
        tw = {}
        ys = self.ring("ys", 2, [P, 2, KT, W], F32R, dma=False)
        ysb = {}

        def load_w(k):
            for c in range(2):
                i, r, t = self.load(raw, wv[:, k, c * W:(c + 1) * W])
                sl = slice(c * W, (c + 1) * W)
                tw[(k, c)] = self.split(ws[:, 0, k, sl], ws[:, 1, k, sl], r[:], t)
                raw.free[i] = tw[(k, c)]

        def load_y(tb, k):
            if k == 0:
                j, y, f = ys.take()
                ysb[tb] = (j, y, [], f)
            j, y, ts, f = ysb[tb]
            i, r, t = self.load(raw, yT_dram[k * P:(k + 1) * P, tb * W:(tb + 1) * W])
            s = self.split(y[:, 0, k], y[:, 1, k], r[:], t, f)
            raw.free[i] = s
            ts.append(s)

        for k in range(KT):
            load_y(0, k)
            load_w(k)
        fw, t_fw = self.row(self.io["final_norm_w_2"] if last else self.io["final_norm_w"], D, "fw")
        if last:
            gate, t_gate = self.row(self.mod[0, 2 * D:3 * D], D, "gate")
        else:
            A, t_sc = self.row(self.mod[0, D:2 * D], D, "A")
            B, t_sh = self.row(self.mod[0, 0:D], D, "B")
            nw, t_nw = self.row(self.io["norm_w_2"][0], D, "nw")
            t_A = self.dve.op(lambda e: e.scalar_tensor_tensor(out=A[:], in0=A[:], scalar=1.0, in1=nw[:],
                                                               op0=ALU.add, op1=ALU.mult), t_sc, t_nw)
        self.minus_half()
        xr = self.ring("xr", 2, [P, D])
        hr = self.ring("hr", 2, [P, D], out=True)
        junk = self.sb("junk", [P, D])
        st = self.sb("st", [P, NT, 6])
        pg, tp = self.psring("pg", 6), self.psring("tp", 2)
        if not last:
            h1r = self.ring("h1", 2, [P, D], out=True)
            tr = self.ring("tr", 2, [P, KT, P], out=True)

        pend = []

        def tail(m, h, hi, t):
            s0 = self.sumsq(st[:, m, 0:1], junk[:], h[:], t)
            r0 = self.rstd(st[:, m, 2:3], st[:, m, 1:2], st[:, m, 0:1], D, s0)
            rows = slice(m * P, (m + 1) * P)
            if last:
                t1 = self.dve.op(lambda e: e.scalar_tensor_tensor(out=h[:], in0=h[:], scalar=st[:, m, 2:3], in1=fw[:],
                                                                  op0=ALU.mult, op1=ALU.mult), r0, t_fw, s0)
                hr.free[hi] = [self.store(self.out[0, rows, :], h[:], hr.slots[hi], t1)]
                return
            i1, h1, f1 = h1r.take()
            t1 = self.dve.op(lambda e: e.scalar_tensor_tensor(out=h1[:], in0=h[:], scalar=st[:, m, 2:3], in1=fw[:],
                                                              op0=ALU.mult, op1=ALU.mult), r0, t_fw, f1)
            t_st = self.store(self.h[rows, :], h1[:], h1r.slots[i1], t1)
            s1 = self.sumsq(st[:, m, 3:4], junk[:], h1[:], t1)
            r1 = self.rstd(st[:, m, 5:6], st[:, m, 4:5], st[:, m, 3:4], D, s1)
            t2 = self.dve.op(lambda e: e.scalar_tensor_tensor(out=h[:], in0=h1[:], scalar=st[:, m, 5:6], in1=A[:],
                                                              op0=ALU.mult, op1=ALU.mult), r1, t_A, s0)
            h1r.free[i1] = [t_st, t2, s1]
            t3 = self.pool.op(lambda e: e.tensor_tensor(h[:], h[:], B[:], ALU.add), t2, t_sh)
            pend.append((m, h, hi, t3))

        def turn():
            m, h, hi, t3 = pend.pop(0)
            oi, o, of = tr.take()
            te = []
            for g in range(2):
                q, pb, pf = tp.take()
                for k in range(4):
                    kk = 4 * g + k
                    f = lambda e, pb=pb, k=k, kk=kk: e.transpose(pb[:, k * P:(k + 1) * P], h[:, kk * P:(kk + 1) * P], ident[:])
                    tt = self.pe.op(f, t3, pf, t_id)
                e_ = self.act.op(lambda e, g=g, pb=pb: e.activation(
                    o[:, 4 * g:4 * g + 4, :], pb[:].rearrange("p (k t) -> p k t", k=4), ACT.Copy), tt, of)
                tp.free[q] = [e_]
                te.append(e_)
            hr.free[hi] = [tt]
            tr.free[oi] = [self.store(self.hT2.rearrange("(k p) t -> p k t", p=P)[:, :, m * P:(m + 1) * P],
                                      o[:], tr.slots[oi], te)]

        banks = {}

        def mm(tiles, rings):
            j, y, tys, _ = ysb[tiles[0] // 4]
            for m, ring in zip(tiles, rings):
                banks[m] = [[ring, *ring.take(), None] for _ in range(2)]
            for k in range(KT):
                for m in tiles:
                    o = (m % 4) * P
                    for c in range(2):
                        b = banks[m][c]
                        sl = slice(c * W, (c + 1) * W)
                        b[4] = self.mm3(b[2][:], y[:, 0, k, o:o + P], y[:, 1, k, o:o + P], ws[:, 0, k, sl], ws[:, 1, k, sl],
                                        k == 0, k == KT - 1, tys[k], tw[(k, c)], b[3])
            if tiles[-1] % 4 == 3:
                ys.free[j] = [(self.pe.sem, self.pe.n)]

        def evac(m):
            xi, x, tx = self.load(xr, res[m * P:(m + 1) * P, :])
            hi, h, hf = hr.take()
            th = []
            for c in range(2):
                ring, q, pb, _, t = banks[m][c]
                sl = slice(c * W, (c + 1) * W)
                if last:
                    t = self.dve.op(lambda e, pb=pb, sl=sl: e.tensor_tensor(h[:, sl], pb[:], gate[:, sl], ALU.mult),
                                    t, t_gate, hf)
                    ring.free[q] = [t]
                    t = self.pool.op(lambda e, sl=sl: e.tensor_tensor(h[:, sl], h[:, sl], x[:, sl], ALU.add), t, tx)
                else:
                    t = self.dve.op(lambda e, pb=pb, sl=sl: e.tensor_tensor(h[:, sl], pb[:], x[:, sl], ALU.add), t, tx, hf)
                    ring.free[q] = [t]
                th.append(t)
            xr.free[xi] = th
            tail(m, h, hi, th)

        mm([0, 1, 2, 3], [tp, pg, pg, pg])
        for k in range(KT):
            load_y(1, k)
        evac(0)
        evac(1)
        for m in range(4, NT):
            mm([m], [pg])
            if m // 4 + 1 < TB:
                load_y(m // 4 + 1, 2 * (m % 4))
                load_y(m // 4 + 1, 2 * (m % 4) + 1)
            if pend:
                turn()
            evac(m - 2)
        for m in (NT - 2, NT - 1):
            if pend:
                turn()
            evac(m)
        while pend:
            turn()

    def in_block(self):
        io = self.io
        hT = self.sb("hT", [P, 2, KT, S], F32R)
        NU = 6
        wu = self.sb("wu", [P, NU, 2, KT, P], F32R)
        ufree = [[] for _ in range(NU)]
        raw = self.ring("raw", 2, [P, KT, P])
        st = self.ring("st", 2, [P, W], out=True)
        vs = [self.slot() for _ in range(2)]
        win = io["w_in_2"][0].rearrange("(k p) n -> p k n", p=P)
        cu = self.ring("cu", 2, [P, 4 + W + 2], dma=False)
        ca = self.ring("ca", 2, [P, W + 2], out=True)
        G = self.sb("G", [P, NT, 16])
        pg = self.psring("pg", 6)
        pgt = self.psring("pgt", 2)

        hs = {}

        def load_h(tb, kk):
            i, r, t = self.load(raw, self.hT2.rearrange("(k p) t -> p k t", p=P)[:, 2 * kk:2 * kk + 2, tb * W:(tb + 1) * W],
                                dst=lambda b: b[:].rearrange("p k c -> p (k c)").rearrange("p (a t) -> p a t", a=2))
            v = r[:].rearrange("p k c -> p (k c)").rearrange("p (a t) -> p a t", a=2)
            sl = (slice(None), slice(2 * kk, 2 * kk + 2), slice(tb * W, (tb + 1) * W))
            s = self.split(hT[:, 0][sl], hT[:, 1][sl], v, t)
            raw.free[i] = s
            hs[(tb, 2 * kk)] = hs[(tb, 2 * kk + 1)] = s

        blocks = [(0, "nq"), (1, "nk"), (2, "nv"), (4, "mq"), (5, "mk"), (6, "mv"), (3, "nz"), (8, "mz"), (7, "mo")]
        cols = [b * W + j * P for b, _ in blocks for j in range(4)]
        ready = []

        def prefetch(n):
            while len(ready) < min(n, 36):
                u = len(ready)
                i, r, t = self.load(raw, win[:, :, cols[u]:cols[u] + P])
                s = self.split(wu[:, u % NU, 0], wu[:, u % NU, 1], r[:], t, ufree[u % NU])
                raw.free[i] = s
                ready.append(s)

        prefetch(1)
        for kk in range(4):
            load_h(0, kk)
        bc, t_bc = self.cols(io["b_in_2"][0, 0:36 * P], 36)
        br = self.sb("br", [P, 3, W])
        t_br = [self.sp.dma(self.slot(), br[:, j, :], io["b_in_2"][0, c * W:(c + 1) * W].partition_broadcast(P))
                for j, c in enumerate((2, 6, 7))]
        bg, t_bg = self.row(io["b_in_2"][0, 36 * P:36 * P + 16], 16)
        cw = self.sb("cw", [P, 5, 8])
        t_cw = self.sp.dma(self.slot(), cw[:], io["conv_w_2"][0].rearrange("j (c p) -> p j c", p=P), slow=True)
        cb, t_cb = self.cols(io["conv_b_2"][0], 8)
        mw, t_mw = self.cols(io["ml_norm_w_2"][0], 4)
        wgr = self.sb("wgr", [P, KT, 16])
        t_wg = self.sp.dma(self.slot(), wgr[:], win[:, :, 36 * P:36 * P + 16])
        wg = self.sb("wg", [P, 2, KT, 16], F32R)
        prefetch(3)
        t_wgs = self.split(wg[:, 0], wg[:, 1], wgr[:], t_wg)

        def conv(name, j, tb, pb, t, state):
            ch = (4 if name == "mk" else 0) + j
            bcol = (4 if name == "mq" else 5) * 4 + j
            i, u, f = cu.take()
            tu = self.act.op(lambda e: e.activation(u[:, 4:4 + W], pb[:], ACT.Identity, bias=bc[:, bcol:bcol + 1]), t, f, t_bc)
            if tb == 0:
                th = self.dve.op(lambda e: e.memset(u[:, 2:4], 0.0), f)
            else:
                pu, ptu, pi = state[0]
                th = self.dve.op(lambda e: e.tensor_copy(u[:, 0:4], pu[:, W:W + 4]), f, ptu)
                cu.free[pi].append(th)
            tz = None
            lo, hi = (2 if tb == 0 else 0), (W + 2 if tb == 3 else W)
            if tb == 3:
                tz = self.dve.op(lambda e: e.memset(u[:, W + 4:W + 6], 0.0), f)
            state[0] = (u, tu, i)
            ai, a, af = ca.take()
            tc = self.dve.op(lambda e: e.tensor_scalar(a[:, lo:hi], u[:, lo:hi], cw[:, 0, ch:ch + 1], cb[:, ch:ch + 1],
                                                       ALU.mult, ALU.add), tu, th, tz, af, t_cw, t_cb)
            for w in range(1, 5):
                tc = self.dve.op(lambda e, w=w: e.scalar_tensor_tensor(
                    out=a[:, lo:hi], in0=u[:, lo + w:hi + w], scalar=cw[:, w, ch:ch + 1], in1=a[:, lo:hi],
                    op0=ALU.mult, op1=ALU.add), tc)
            cu.free[i] = [tc]
            ts = self.act.op(lambda e: e.activation(a[:, lo:hi], a[:, lo:hi], ACT.Silu), tc)
            o0 = tb * W - 2 + lo
            ca.free[ai] = [self.store(self.s[name][j * P:(j + 1) * P, o0:o0 + hi - lo], a[:, lo:hi], ca.slots[ai], ts)]
            return tu

        def evac_c(name, blk, j, tb, pb, t, state):
            if name in ("mq", "mk"):
                return conv(name, j, tb, pb, t, state)
            i, s, f = st.take()
            b = bc[:, blk * 4 + j:blk * 4 + j + 1]
            if name in ("nq", "nk"):
                i2, s2, f2 = st.take()
                hi, lo = s[:].bitcast(F32R), s2[:].bitcast(F32R)
                parts = [(hi, lo, s[:], pb[:])]
                if name == "nq":
                    parts = [tuple(v[:, o:o + P].rearrange("p (r c) -> p r c", r=4) for v in (hi, lo, s[:])) +
                             (pb[:, x * 256:(x + 1) * 256].rearrange("p (r c) -> p r c", r=4)[:, :, 32 * y:32 * y + 32],)
                             for x in range(2) for y in range(2) for o in (x * 256 + y * P,)]
                for h_, l_, hf, v in parts:
                    th = self.act.op(lambda e, h_=h_, v=v: e.activation(h_, v, ACT.Identity, bias=b), t, f, t_bc)
                for h_, l_, hf, v in parts:
                    te = self.dve.op(lambda e, l_=l_, hf=hf, v=v: e.scalar_tensor_tensor(
                        out=l_, in0=v, scalar=b, in1=hf, op0=ALU.add, op1=ALU.subtract), th, f2)
                dst = [self.s[name + x][j * P:(j + 1) * P, tb * W:(tb + 1) * W] for x in "hl"]
                st.free[i] = [self.store(dst[0], s[:], st.slots[i], th), te]
                st.free[i2] = [self.store(dst[1], s2[:], st.slots[i2], te)]
                return te
            te = t2 = self.act.op(lambda e: e.activation(s[:], pb[:], ACT.Silu, bias=b), t, f, t_bc)
            if name == "mz":
                t2 = self.dve.op(lambda e: e.tensor_scalar(s[:], s[:], mw[:, j:j + 1], None, ALU.mult), te, t_mw)
            st.free[i] = [self.store(self.s[name][j * P:(j + 1) * P, tb * W:(tb + 1) * W], s[:], st.slots[i], t2)]
            return te

        for bi, (blk, name) in enumerate(blocks):
            u0 = 4 * bi
            if name in ("nv", "mv", "mo"):
                s0 = u0 % NU
                assert s0 + 4 <= NU
                x = ("nv", "mv", "mo").index(name)
                tw = ready[u0:u0 + 4]
                for m in range(NT):
                    q, pb, pf = pg.take()
                    if name == "mv":
                        gq, gb, gf = pgt.take()
                    for k in range(KT):
                        lh, ll = hT[:, 0, k, m * P:(m + 1) * P], hT[:, 1, k, m * P:(m + 1) * P]
                        t = self.mm3(pb[:], lh, ll, wu[:, s0:s0 + 4, 0, k, :], wu[:, s0:s0 + 4, 1, k, :],
                                     k == 0, k == KT - 1, tw, pf, hs[(m // 4, k)])
                        if name == "mv":
                            tg = self.mm3(gb[:, 0:16], lh, ll, wg[:, 0, k], wg[:, 1, k], k == 0, k == KT - 1, t_wgs, gf)
                    i, s, f = st.take()
                    t = self.dve.op(lambda e, s=s, pb=pb, x=x: e.tensor_tensor(s[:], pb[:], br[:, x, :], ALU.add), t, f, t_br[x])
                    pg.free[q] = [t]
                    if name == "mo":
                        t = self.act.op(lambda e, s=s: e.activation(s[:], s[:], ACT.Sigmoid), t)
                    if name == "nv":
                        st.free[i] = [self.store(self.V[a, 2 * m + y], s[64 * y + k0:64 * y + k0 + 40, :], vs[i], t, eng=self.sp)
                                      for y in range(2) for a, k0 in enumerate((0, 24))][-1:]
                    else:
                        st.free[i] = [self.store(self.s[name][m * P:(m + 1) * P, :], s[:], st.slots[i], t)]
                    if name == "mv":
                        t_g = self.dve.op(lambda e, gb=gb, m=m: e.tensor_tensor(G[:, m, :], gb[:, 0:16], bg[:], ALU.add), tg, t_bg)
                        pgt.free[gq] = [t_g]
                for j in range(4):
                    ufree[s0 + j] = [(self.pe.sem, self.pe.n)]
                prefetch(u0 + 4 + NU)
                if name == "mv":
                    self.store(self.gt, G[:].rearrange("p c g -> p (c g)"), self.slot(True), t_g)
            else:
                order = [(u0 + j, tb) for j in range(4) for tb in range(TB)]
                if bi < 2:
                    order = [(u, tb) for tb in range(TB) for u in range(NU)] if bi == 0 else order[8:]
                for u, tb in order:
                        blk, name = blocks[u // 4]
                        j = u % 4
                        if tb == 0:
                            state = [None]
                        if bi == 0 and tb < 3:
                            prefetch(min(u + 4, NU) if tb == 0 else 0)
                            if u < 4:
                                load_h(tb + 1, u)
                        q, pb, pf = pg.take()
                        for k in range(KT):
                            t = self.mm3(pb[:], wu[:, u % NU, 0, k, :], wu[:, u % NU, 1, k, :],
                                         hT[:, 0, k, tb * W:(tb + 1) * W], hT[:, 1, k, tb * W:(tb + 1) * W],
                                         k == 0, k == KT - 1, ready[u], pf, hs[(tb, k)])
                        pg.free[q] = [evac_c(name, blk, j, tb, pb, t, state)]
                        if tb == 3:
                            ufree[u % NU] = [t]
                            prefetch(u + 1 + NU)

    def bias_tables(self):
        z = self.sb("z", [32, 64])
        t = self.dve.op(lambda e: e.memset(z[:], 0.0))
        n = NA_H * 465
        t_rpb = [
            self.store(self.rpb[:, 0:64], z[:], self.slot(True), t),
            self.store(self.rpb[:, 64 + n:128 + n], z[:], self.slot(True), t),
            self.store(self.rpb[:, 64:64 + n], self.io["rpb_2"].rearrange("a h y x -> (a h y x)").partition_broadcast(32),
                       self.slot(True))]
        zr = self.ring("zr", 1, [32, 17, 40])
        zo = [self.slot(True) for _ in range(2)]
        for a, X in enumerate((15, 7)):
            for h in range(NA_H):
                src = bass.AP(tensor=self.rpb.tensor, offset=64 + X + h * 465, ap=[[RPB - 1, 32], [31, 15], [1, 40]])
                yield
                i, zb, t = self.load(zr, src, dst=lambda b: b[:, 1:16, :], after=t_rpb)
                t = self.pool.op(lambda e, zb=zb: e.tensor_scalar(zb[:, 1:16, :], zb[:, 1:16, :], 8.0, 1.0,
                                                                  ALU.mult, ALU.mult), t)
                for y in (0, 16):
                    t = self.pool.op(lambda e, zb=zb, y=y: e.memset(zb[:, y, :], NEG), t)
                for c0, c1, base, step, cm in (((0, 40, 8, 1, -1), (16, 40, -9, -1, 1)) if a == 0 else
                                               ((0, 24, 0, 1, -1), (0, 40, 15, -1, 1))):
                    t = self.pool.op(lambda e, v=zb[:, 1:16, c0:c1], base=base, step=step, cm=cm, n=c1 - c0: e.affine_select(
                        out=v, in_=v, compare_op=ALU.is_ge, fill=NEG, base=base, pattern=[[0, 15], [step, n]],
                        channel_multiplier=cm), t)
                zr.free[i] = [self.store(self.Z[a, h], zb[:].rearrange("c y k -> c (y k)"), zo[i], t)]

    def na_block(self):
        ident, t_id = self.identity()
        kinds = {"mid": (0, 12, 3), "top": (480, 9, 7), "bot": (840, 9, 2)}
        tabs = self.ring("tab", 2, [P, 2, 2, 1200])
        tslots = [[self.slot() for _ in range(6)] for _ in range(2)]
        hd = self.ring("hd", 4, [P, 3, S], F32R, dma=False)
        hslots = [[self.slot() for _ in range(2)] for _ in range(4)]
        zr = self.ring("z", 2, [P, S])
        vr = self.ring("v", 4, [120, 4, P])
        sr = self.ring("s", 5, [P, 480], dma=False)
        pr = self.ring("p", 5, [P, 480], dma=False)
        ptr = self.ring("pt", 3, [120, W], dma=False)
        yr = self.ring("y", 2, [P, 256], out=True)
        st = self.sb("st", [P, 128, 4])
        pS, pT, pO = self.psring("pS", 3), self.psring("pT", 3), self.psring("pO", 2)
        heads = {}

        def prep(hp):
            qk = [hd.take() for _ in range(2)]
            ti, tab, tf = tabs.take()
            H = heads[hp] = dict(qk=qk, ti=ti, tab=tab, tq={}, tt={})

            def half(hh, x):
                i, b, f = qk[hh]
                r = slice((2 * hp + hh) * 64, (2 * hp + hh + 1) * 64)
                c = slice(1024 * x, 1024 * x + 1024)
                for y, n in enumerate(("nqh", "nql", "nkh", "nkh", "nkl", "nkl")):
                    yield
                    H["tq"][hh, x] = self.sp.dma(hslots[i][x], b[64 * (y % 2):64 * (y % 2) + 64, y // 2, c].bitcast(F32),
                                                 self.s[n][r, c], f)

            def table(n, kind):
                off, nk, dd = kinds[kind]
                for a in range(2):
                    for ri in range(4):
                        y0 = 1 + dd - ri
                        yield
                        H["tt"][kind, a] = self.sp.dma(
                            tslots[ti][2 * n + a], tab[32 * ri:32 * ri + 32, :, a, off:off + nk * 40],
                            self.Z[a, 2 * hp:2 * hp + 2, :, y0 * 40:(y0 + nk) * 40].rearrange("h c y -> c h y"), tf)

            yield from half(0, 0)
            yield from table(0, "top")
            yield from half(1, 0)
            yield from table(1, "mid")
            H["z"] = self.load(zr, self.s["nz"][hp * P:(hp + 1) * P, :])
            yield from half(0, 1)
            yield from half(1, 1)
            yield from table(2, "bot")

        last = []

        def window(hp, kind):
            H = heads[hp]
            tab, tt = H["tab"], [H["tt"][kind, a] for a in range(2)]
            off, nk, _ = kinds[kind]
            tm = last[-1:]
            if kind == "mid":
                for ri in range(4):
                    for c0, c1 in ((0, ri * 40), ((ri + 8) * 40, 480)):
                        if c1 > c0:
                            tm = [self.pool.op(lambda e, ri=ri, c0=c0, c1=c1: e.memset(
                                tab[32 * ri:32 * ri + 32, :, :, c0:c1], NEG), tt, tm)]
            else:
                c0 = off + (320 if kind == "top" else 0)
                tm = [self.pool.op(lambda e, c0=c0: e.memset(tab[:, :, :, c0:c0 + 40], NEG), tt, tm)]
            last.extend(tm)
            H["t", kind] = [tt, tm]

        tiles = []
        for hp in range(4):
            for i in range(8):
                for a in range(2):
                    for hh in range(2):
                        tiles.append((hp, i, a, hh))
        info = {}

        def stage_a(n):
            hp, i, a, hh = tiles[n]
            H = heads[hp]
            kind = "top" if i == 0 else "bot" if i == 7 else "mid"
            off, nk, _ = kinds[kind]
            ks = {"top": 0, "bot": 23, "mid": 4 * i - 4}[kind]
            c0, k0 = (0, 0) if a == 0 else (32, 24)
            N = nk * 40
            if hh == 0:
                src = self.V[a, ks:ks + nk].rearrange("r c d -> (r c) d")[:, hp * P:(hp + 1) * P]
                vi, v, tv = self.load(vr, src.rearrange("(j p) d -> p j d", p=120), dst=lambda b: b[:, 0:nk // 3, :])
                info[n] = dict(v=v, vi=vi, tv=tv)
            else:
                info[n] = dict(v=info[n - 1]["v"], vi=info[n - 1]["vi"], tv=info[n - 1]["tv"])
            d = info[n]
            hi_, b, _ = H["qk"][hh]
            tq = [H["tq"][hh, x] for x in range(2 if ks + nk > 16 else 1)]
            q = b[:, 0, (2 * i + a) * P:(2 * i + a + 1) * P]
            k = [b[:, x, :].rearrange("p (r c) -> p r c", c=64)[:, ks:ks + nk, k0:k0 + 40] for x in (1, 2)]
            si, ps, pf = pS.take()
            self.pe.quiet(lambda e: e.matmul(ps[:, 0:N], q, k[0], start=True, stop=False), tq, pf)
            t = self.pe.op(lambda e: e.matmul(ps[:, 0:N], q, k[1], start=False, stop=True))
            if n % 32 >= 30:
                hd.free[hi_] = [t]
            bi, s, sf = sr.take()
            tab = H["tab"][:, hh, a, off:off + N]
            t = self.dve.op(lambda e: e.tensor_tensor_reduce(
                out=s[:, 0:N], in0=ps[:, 0:N], in1=tab, scale=0.125, scalar=-3.0e38, op0=ALU.add, op1=ALU.max,
                accum_out=st[:, n, 0:1]), t, H["t", kind], sf)
            pS.free[si] = [t]
            tn = self.dve.op(lambda e: e.tensor_scalar(st[:, n, 1:2], st[:, n, 0:1], -1.0, None, ALU.mult), t)
            pi, p, pff = pr.take()
            te = self.act.op(lambda e: e.activation(p[:, 0:N], s[:, 0:N], ACT.Exp, bias=st[:, n, 1:2],
                                                    accum_out=st[:, n, 2:3]), tn, t, pff)
            sr.free[bi] = [te]
            d.update(nk=nk, p=p, pi=pi, te=te, N=N)
            if n % 32 == 31:
                tabs.free[H["ti"]] = [t]

        def stage_r(n):
            d = info[n]
            p, N = d["p"], d["N"]
            tr = self.dve.op(lambda e: e.reciprocal(st[:, n, 3:4], st[:, n, 2:3]), d["te"])
            d["te"] = self.pool.op(lambda e: e.tensor_scalar(p[:, 0:N], p[:, 0:N], st[:, n, 3:4], 1.0, ALU.mult, ALU.mult),
                                   d["te"], tr)

        def stage_b(n):
            d = info[n]
            nj = d["nk"] // 3
            qi, ps, pf = pT.take()
            for j in range(nj):
                t = self.pe.op(lambda e, j=j: e.transpose(ps[0:120, j * P:(j + 1) * P], d["p"][:, j * 120:(j + 1) * 120],
                                                          ident[:]), d["te"], pf, t_id)
            pr.free[d["pi"]] = [t]
            i, pt, f = ptr.take()
            if n % 2:
                te = self.act.op(lambda e: e.activation(pt[:, 0:nj * P], ps[0:120, 0:nj * P], ACT.Copy), t, f)
            else:
                te = self.dve.op(lambda e: e.tensor_copy(pt[:, 0:nj * P], ps[0:120, 0:nj * P]), t, f)
            pT.free[qi] = [te]
            d.update(pt=pt, pti=i, tpt=te)

        def stage_c(n):
            hp, i, a, hh = tiles[n]
            d = info[n]
            nj = d["nk"] // 3
            if hh == 0:
                d["oi"], d["o"], d["of"] = pO.take()
            else:
                d["oi"], d["o"], d["of"] = (info[n - 1][x] for x in ("oi", "o", "of"))
            po = d["o"]
            for j in range(nj):
                t = self.pe.op(lambda e, j=j: e.matmul(po[64 * hh:64 * hh + 64, 0:P], d["v"][:, j, 64 * hh:64 * hh + 64],
                                                       d["pt"][:, j * P:(j + 1) * P], start=(j == 0),
                                                       stop=(j == nj - 1)), d["tpt"], d["tv"], d["of"])
            ptr.free[d["pti"]] = [t]
            if hh == 0:
                return
            vr.free[d["vi"]] = [t]
            H = heads[hp]
            if a == 0:
                yb[0] = yr.take()
            yi, y, yf = yb[0]
            c0 = 32 * a
            z = H["z"][1][:].rearrange("p (r c) -> p r c", c=64)[:, 4 * i:4 * i + 4, c0:c0 + 32]
            t = self.dve.op(lambda e: e.tensor_tensor(y[:].rearrange("p (r c) -> p r c", c=64)[:, :, c0:c0 + 32],
                                                      po[:, 0:P].rearrange("p (r c) -> p r c", c=32), z, ALU.mult),
                            t, H["z"][2], yf)
            pO.free[d["oi"]] = [t]
            if a == 1:
                yr.free[yi] = [self.store(self.y2T[hp * P:(hp + 1) * P, i * 256:(i + 1) * 256], y[:], yr.slots[yi], t)]
            if n % 32 == 31:
                zr.free[H["z"][0]] = [t]

        yb = {}
        for _ in prep(0):
            pass
        for kind in kinds:
            window(0, kind)
        coming = iter(())
        for n in range(128 + 4):
            hp = n // 32 + 1
            if n % 32 == 5 and hp < 4:
                coming = prep(hp)
            if n % 32 == 28 and hp < 4:
                for _ in coming:
                    pass
                for kind in kinds:
                    window(hp, kind)
            for _ in range(3):
                next(coming, None)
            if n < 128:
                stage_a(n)
            if 0 <= n - 1 < 128:
                stage_r(n - 1)
            if 0 <= n - 3 < 128:
                stage_b(n - 3)
            if 0 <= n - 4 < 128:
                stage_c(n - 4)

    def ml_block(self):
        dve, act, pe, pool, sp = self.dve, self.act, self.pe, self.pool, self.sp
        C = NT
        ident, t_id = self.identity()
        ones = self.sb("ones", [P, P])
        zero = self.sb("zero", [P, P])
        t_1 = pool.op(lambda e: e.memset(ones[:], 1.0))
        t_0 = pool.op(lambda e: e.memset(zero[:], 0.0))
        mask = self.sb("mask", [P, 2, P])
        t_mask = []
        for d in range(2):
            t = pool.op(lambda e, d=d: e.memset(mask[:, d, :], 0.0))
            s = 1 if d == 0 else -1
            t_mask.append(pool.op(lambda e, d=d, s=s: e.affine_select(
                out=mask[:, d, :], in_=mask[:, d, :], compare_op=ALU.is_ge, fill=NEG, base=0,
                pattern=[[s, P]], channel_multiplier=-s), t))
        G = self.sb("G", [P, C, 16])
        tG = sp.dma(self.slot(), G[:].rearrange("p c g -> p (c g)"), self.gt)
        kC = self.sb("kC", [P, 4, S])
        tk = [sp.dma(self.slot(), kC[:, h, :], self.s["mk"][h * P:(h + 1) * P, :]) for h in range(4)]
        v1 = self.sb("v1", [P, C, 4, P + 1])
        tv = [sp.dma(self.slot(), v1[:, c, :, 0:P], self.s["mv"][c * P:(c + 1) * P, :].rearrange("t (h e) -> t h e", h=4))
              for c in range(C)]
        tv1 = pool.op(lambda e: e.memset(v1[:, :, :, P:P + 1], 1.0))
        kT = self.sb("kT", [P, C, 4, P])
        Cb = self.sb("Cb", [P, C, 4, P + 1])
        pA = self.psring("pA", 1)
        pB = self.psring("pB", 1)
        pU = self.psring("pU", 2)

        gi = self.sb("gi", [P, 2, 2, 4, C])
        tgi = []
        for f in range(2):
            for d in range(2):
                tgi.append(dve.op(lambda e, f=f, d=d: e.tensor_copy(
                    gi[:, f, d, :, :], G[:, :, 8 * d + 4 * f:8 * d + 4 * f + 4].rearrange("p c h -> p h c")), tG))
        X = {n: self.sb(n, [P, P]) for n in ("I", "F", "lf", "b", "u", "M", "nN", "w", "em")}

        def turn(dst, src, ring, *ts):
            i, pb, f = ring.take()
            t = pe.op(lambda e: e.transpose(pb[:, 0:P], src, ident[:]), t_id, f, *ts)
            t = dve.op(lambda e: e.tensor_copy(dst, pb[:, 0:P]), t)
            ring.free[i] = [t]
            return t

        tI = turn(X["I"][:], gi[:, 0].rearrange("p d h c -> p (d h c)"), pA, tgi)
        tF = turn(X["F"][:], gi[:, 1].rearrange("p d h c -> p (d h c)"), pB, tgi)
        t = act.op(lambda e: e.activation(X["w"][:], X["F"][:], ACT.Abs), tF)
        t = act.op(lambda e: e.activation(X["em"][:], X["w"][:], ACT.Exp, scale=-1.0), t)
        t = act.op(lambda e: e.activation(X["u"][:], X["em"][:], ACT.Ln, bias=1.0), t)
        tlf = dve.op(lambda e: e.scalar_tensor_tensor(out=X["lf"][:], in0=X["F"][:], scalar=0.0, in1=X["u"][:],
                                                      op0=ALU.min, op1=ALU.subtract), t, tF)

        def both(fn, *ts):
            return [dve.op(lambda e, r=r, o=o: fn(e, r, o), *ts)
                    for r, o in ((slice(0, 64), slice(None)), (slice(64, 128), slice(None, None, -1)))]

        tb_ = both(lambda e, r, o: e.tensor_tensor_scan(X["b"][r, o], ones[r, :], X["lf"][r, o], 0.0,
                                                        ALU.mult, ALU.add), tlf, t_1)
        tu = dve.op(lambda e: e.tensor_tensor(X["u"][:], X["I"][:], X["b"][:], ALU.subtract), tI, tb_)
        tM = both(lambda e, r, o: e.tensor_tensor_scan(X["M"][r, o], zero[r, :], X["u"][r, o], -3.0e38,
                                                       ALU.add, ALU.max), tu, t_0)
        L = self.sb("L", [P, 8])
        tl = []
        for r, z in ((slice(0, 64), P - 1), (slice(64, 128), 0)):
            tl.append(dve.op(lambda e, r=r, z=z: e.tensor_copy(L[r, 0:1], X["b"][r, z:z + 1]), tb_))
            tl.append(dve.op(lambda e, r=r, z=z: e.tensor_copy(L[r, 1:2], X["M"][r, z:z + 1]), tM))
        tl.append(dve.op(lambda e: e.tensor_tensor(L[:, 2:3], L[:, 0:1], L[:, 1:2], ALU.add), tl))
        R = self.sb("R", [1, 4, P])
        tR = []
        for x, (col, ring) in enumerate(((0, pA), (2, pB))):
            i, pb, f = ring.take()
            t = pe.op(lambda e, pb=pb, col=col: e.matmul(pb[0:1, 0:P], L[:, col:col + 1], ident[:], start=True, stop=True),
                      tl, f, t_id)
            t = dve.op(lambda e, pb=pb, x=x: e.tensor_copy(R[:, x, :], pb[0:1, 0:P]), t)
            ring.free[i] = [t]
            tR.append(t)
        tm = []
        for n in range(8):
            o = slice(n * C, (n + 1) * C) if n < 4 else slice((n + 1) * C - 1, n * C - 1 if n * C > 0 else None, -1)
            tm.append(dve.op(lambda e, o=o: e.tensor_tensor_scan(R[:, 2, o], R[:, 0, o], R[:, 1, o], 0.0, ALU.add, ALU.max), tR))
        t = dve.op(lambda e: e.memset(R[:, 3, :], 0.0))
        Rp = R[:, 3, :].rearrange("p (n c) -> p n c", c=C)
        Rn = R[:, 2, :].rearrange("p (n c) -> p n c", c=C)
        tp = [dve.op(lambda e: e.tensor_copy(Rp[:, 0:4, 1:C], Rn[:, 0:4, 0:C - 1]), tm, t),
              dve.op(lambda e: e.tensor_copy(Rp[:, 4:8, 0:C - 1], Rn[:, 4:8, 1:C]), tm, t)]
        i, pb, f = pA.take()
        t = pe.op(lambda e, pb=pb: e.matmul(pb[:, 0:1], R[:, 3, :], ones[0:1, 0:1], start=True, stop=True), tp, t_1, f)
        tmp = dve.op(lambda e, pb=pb: e.tensor_copy(L[:, 3:4], pb[:, 0:1]), t)
        pA.free[i] = [tmp]
        tN = dve.op(lambda e: e.tensor_scalar(X["nN"][:], X["M"][:], L[:, 3:4], -1.0, ALU.max, ALU.mult), tM, tmp)
        tNl = dve.op(lambda e: e.tensor_scalar(L[:, 4:5], L[:, 1:2], L[:, 3:4], -1.0, ALU.max, ALU.mult), tl, tmp)
        tNd = self.store(self.nN, X["nN"][:], self.slot(True), tN)
        tw = act.op(lambda e: e.activation(X["w"][:], X["u"][:], ACT.Exp, bias=L[:, 4:5]), tu, tNl, tlf)
        tdc = act.op(lambda e: e.activation(L[:, 5:6], L[:, 3:4], ACT.Exp, bias=L[:, 4:5]), tNl)
        t = dve.op(lambda e: e.tensor_tensor(X["I"][:], X["nN"][:], X["b"][:], ALU.subtract), tN, tb_, tu)
        tem = act.op(lambda e: e.activation(X["em"][:], X["I"][:], ACT.Exp), t)
        uT, wT, eT = (self.sb(n, [P, 8, C]) for n in ("uT", "wT", "eT"))
        flat2 = lambda a: a[:].rearrange("p n c -> p (n c)")
        tuT, twT, teT = (turn(flat2(a), X[n][:], r, ts) for a, n, r, ts in
                         ((wT, "w", pA, tw), (uT, "u", pB, tu), (eT, "em", pA, tem)))
        tuT, twT = twT, tuT
        mpB, dcB = (self.sb(n, [P, 8, C]) for n in ("mpB", "dcB"))
        dg = self.sb("dg", [P, 2, P])
        tB = []
        for x, (col, a, ts) in enumerate(((3, mpB, tmp), (5, dcB, tdc))):
            t = dve.op(lambda e, x=x, col=col: e.tensor_scalar(dg[:, x, :], ident[:], L[:, col:col + 1], None, ALU.mult), ts, t_id)
            i, pb, f = pB.take()
            t = pe.op(lambda e, pb=pb, x=x: e.matmul(pb[:, 0:P], ones[:], dg[:, x, :], start=True, stop=True), t, f, t_1)
            t = dve.op(lambda e, pb=pb, a=a: e.tensor_copy(flat2(a), pb[:, 0:P]), t)
            pB.free[i] = [t]
            tB.append(t)

        SC = P ** -0.5
        wv = self.ring("wv", 2, [P, 4, P + 1], dma=False)
        tkT = {}

        def kturn(c):
            i, pb, f = pA.take()
            for h in range(4):
                t = pe.op(lambda e, h=h: e.transpose(pb[:, h * P:(h + 1) * P], kC[:, h, c * P:(c + 1) * P], ident[:]),
                          tk[h], f, t_id)
            tkT[c] = act.op(lambda e: e.activation(kT[:, c].rearrange("p h d -> p (h d)"), pb[:], ACT.Copy, scale=SC), t)
            pA.free[i] = [tkT[c]]

        def weigh(d, c):
            i, w, f = wv.take()
            return i, w, pool.op(lambda e: e.tensor_tensor(
                w[:], v1[:, c], wT[:, 4 * d:4 * d + 4, c:c + 1].to_broadcast([P, 4, P + 1]), ALU.mult), tv[c], tv1, twT, f)

        def update(d, c, weighed, new, old, t_old, *free):
            i, w, t = weighed
            out, tr = [], []
            for g in range(2):
                q, pb, pf = pU.take()
                for h in (2 * g, 2 * g + 1):
                    tt = pe.op(lambda e, h=h, g=g, pb=pb: e.matmul(
                        pb[:, (h - 2 * g) * (P + 1):(h - 2 * g + 1) * (P + 1)], kT[:, c, h, :], w[:, h, :],
                        start=True, stop=True), t, tkT[c], pf)
                tr.append(tt)
                for h in (2 * g, 2 * g + 1):
                    src = pb[:, (h - 2 * g) * (P + 1):(h - 2 * g + 1) * (P + 1)]
                    if old is None:
                        o = dve.op(lambda e, h=h, src=src: e.tensor_copy(new[:, h, :], src), tt, *free)
                    else:
                        o = dve.op(lambda e, h=h, src=src: e.scalar_tensor_tensor(
                            out=new[:, h, :], in0=old[:, h, :], scalar=dcB[:, 4 * d + h, c:c + 1], in1=src,
                            op0=ALU.mult, op1=ALU.add), tt, t_old, tB, *free)
                    out.append(o)
                pU.free[q] = [o]
            wv.free[i] = tr
            return out

        tCb = {C - 1: None}
        kturn(C - 1)
        w = weigh(1, C - 1)
        for c in range(C - 1, 0, -1):
            kturn(c - 1)
            nxt = weigh(1, c - 1) if c > 1 else None
            tCb[c - 1] = update(1, c, w, Cb[:, c - 1], None if c == C - 1 else Cb[:, c], tCb[c])
            w = nxt

        qr = self.ring("q", 2, [P, 4, P])
        orr = self.ring("o", 2, [P, 4, P])
        zr = self.ring("z", 2, [P, 4, P])
        nb = self.ring("nb", 3, [P, 4, P])
        eb = self.ring("eb", 6, [P, 4, P], dma=False)
        ib = self.ring("ib", 6, [P, 4, P], dma=False)
        hb = self.ring("hb", 3, [P, 4, P], dma=False)
        yb = self.ring("yb", 2, [P, 4, P], out=True)
        rd = self.sb("rd", [P, C, 2, 4])
        bn = self.sb("bn", [P, C, 4, 6])
        mv = self.sb("mv", [P, C, 4, 2])
        rs = self.sb("rs", [P, C, 4])
        self.minus_half(4)
        pN = self.psring("pN", 4, (P, 2 * (P + 1)))
        A = {}

        def decays(c):
            cs = slice(c * P, (c + 1) * P)
            A[c] = dict(dirs=[], q=self.load(qr, self.s["mq"].rearrange("(h d) t -> d h t", d=P)[:, :, cs]))
            for d in range(2):
                src = self.nN.rearrange("(n c) t -> n c t", c=C)[4 * d:4 * d + 4, c, :]
                n = self.load(nb, src.partition_broadcast(P), after=[tNd])
                ei, x, ef = eb.take()
                tm_ = pool.op(lambda e, x=x, n=n, d=d: e.tensor_tensor(
                    x[:], n[1][:], mask[:, d:d + 1, :].to_broadcast([P, 4, P]), ALU.add), n[2], t_mask[d], ef)
                D_ = dict(x=x, ei=ei)
                if not (d == 0 and c == 0 or d == 1 and c == C - 1):
                    D_["ii"], y, yf = ib.take()
                    D_["y"] = y
                    D_["ty"] = [act.op(lambda e, y=y, n=n, d=d, h=h: e.activation(
                        y[:, h, :], n[1][:, h, :], ACT.Exp, bias=mpB[:, 4 * d + h, c:c + 1]), n[2], tB, yf)
                        for h in range(4)]
                D_["tx"] = [act.op(lambda e, x=x, d=d, h=h: e.activation(
                    x[:, h, :], x[:, h, :], ACT.Exp, bias=uT[:, 4 * d + h, c:c + 1]), tm_, tuT) for h in range(4)]
                nb.free[n[0]] = [tm_] + D_.get("ty", [])
                A[c]["dirs"].append(D_)

        def scores(c):
            cs = slice(c * P, (c + 1) * P)
            q = A[c]["q"]
            si, ps, pf = pA.take()
            for h in range(4):
                t = pe.op(lambda e, h=h: e.matmul(ps[:, h * P:(h + 1) * P], kC[:, h, cs], q[1][:, h, :],
                                                  start=True, stop=True), q[2], tk[h], pf)
            tx, tq = [], []
            for D_ in A[c]["dirs"]:
                x = D_["x"]
                D_["tP"] = dve.op(lambda e, x=x: e.scalar_tensor_tensor(
                    out=x[:], in0=ps[:].rearrange("p (h t) -> p h t", h=4), scalar=SC, in1=x[:],
                    op0=ALU.mult, op1=ALU.mult), t, D_["tx"])
                tx.append(D_["tP"])
            for D_ in A[c]["dirs"]:
                if "y" in D_:
                    y = D_["y"]
                    D_["tq"] = dve.op(lambda e, y=y: e.tensor_tensor(y[:], y[:], q[1][:], ALU.mult), D_["ty"], q[2])
                    tq.append(D_["tq"])
            pA.free[si] = tx
            qr.free[q[0]] = [t] + tq

        fw = [None, None]

        def numerators(c, weighed):
            a = A[c]
            a["num"] = []
            for d in range(2):
                D_ = a["dirs"][d]
                st_, t_st = fw if d == 0 else (Cb[:, c], tCb[c])
                for g in range(2):
                    i, pb, f = pN.take()
                    for h in (2 * g, 2 * g + 1):
                        o = pb[:, (h - 2 * g) * (P + 1):(h - 2 * g + 1) * (P + 1)]
                        inter = "tq" in D_
                        t = pe.op(lambda e, o=o, D_=D_, h=h, inter=inter: e.matmul(
                            o, D_["x"][:, h, :], v1[:, c, h, :], start=True, stop=not inter), D_["tP"], tv[c], tv1, f)
                        if inter:
                            t = pe.op(lambda e, o=o, D_=D_, h=h, st_=st_: e.matmul(
                                o, D_["y"][:, h, :], st_[:, h, :], start=False, stop=True), D_["tq"], t_st)
                    a["num"].append((i, pb, t))
                eb.free[D_["ei"]] = [t]
                if inter:
                    ib.free[D_["ii"]] = [t]
            if c < C - 1:
                fw[:] = Cb[:, c], update(0, c, weighed, Cb[:, c], fw[0], fw[1], t)

        def divide(c):
            a = A[c]
            cs = slice(c * P, (c + 1) * P)
            a["o"] = self.load(orr, self.s["mo"][cs, :].rearrange("t (h e) -> t h e", h=4))
            hi, hbuf, tH = hb.take()
            tr = {}
            for d in range(2):
                x = []
                for g in range(2):
                    i, pb, t = a["num"][2 * d + g]
                    den = pb[:].rearrange("p (h e) -> p h e", h=2)[:, :, P:P + 1]
                    r = rd[:, c, d, 2 * g:2 * g + 2].unsqueeze(2)
                    y = dve.op(lambda e, den=den, d=d, g=g, r=r: e.scalar_tensor_tensor(
                        out=r, in0=den, scalar=-1.0, in1=eT[:, 4 * d + 2 * g:4 * d + 2 * g + 2, c:c + 1],
                        op0=ALU.mult, op1=ALU.max), t, teT)
                    x.append(dve.op(lambda e, den=den, r=r: e.tensor_tensor(r, r, den, ALU.max), y))
                tr[d] = x
            tr = dve.op(lambda e: e.reciprocal(rd[:, c], rd[:, c]), tr[0], tr[1])
            for d in range(2):
                nH = []
                for g in range(2):
                    i, pb, t = a["num"][2 * d + g]
                    num = pb[:].rearrange("p (h e) -> p h e", h=2)[:, :, 0:P]
                    if d == 0:
                        x = dve.op(lambda e, num=num, g=g: e.tensor_tensor(
                            hbuf[:, 2 * g:2 * g + 2, :], num,
                            rd[:, c, 0, 2 * g:2 * g + 2].unsqueeze(2).to_broadcast([P, 2, P]), ALU.mult), tr, t, tH)
                        nH.append(x)
                    else:
                        for h in range(2):
                            x = dve.op(lambda e, num=num, g=g, h=h: e.scalar_tensor_tensor(
                                out=hbuf[:, 2 * g + h, :], in0=num[:, h, :], scalar=rd[:, c, 1, 2 * g + h:2 * g + h + 1],
                                in1=hbuf[:, 2 * g + h, :], op0=ALU.mult, op1=ALU.add), tr, t, tH)
                            nH.append(x)
                    pN.free[i] = [x]
                tH = nH
            a.update(hi=hi, hbuf=hbuf, tH=tH)

        def gate(c):
            a = A[c]
            o, hbuf = a["o"], a["hbuf"]
            a["tg"] = pool.op(lambda e: e.tensor_tensor(hbuf[:], hbuf[:], o[1][:], ALU.mult), a["tH"], o[2])
            orr.free[o[0]] = [a["tg"]]

        def moments(c):
            a = A[c]
            hbuf = a["hbuf"]
            tb = [dve.op(lambda e, h=h: e.bn_stats(bn[:, c, h, :], hbuf[:, h, :]), a["tg"]) for h in range(4)]
            tb = [dve.op(lambda e, h=h: e.bn_aggr(mv[:, c, h, :], bn[:, c, h, :]), tb[h]) for h in range(4)]
            t = dve.op(lambda e: e.tensor_scalar(rs[:, c, :].unsqueeze(2), mv[:, c, :, 1:2], EPS, None, ALU.add), tb)
            a["tr"] = pool.op(lambda e: e.tensor_tensor(rs[:, c, :], rs[:, c, :], self.mhalf[:], ALU.pow), t, self.t_mhalf)

        def normalise(c):
            a = A[c]
            hbuf = a["hbuf"]
            a["z"] = self.load(zr, self.s["mz"].rearrange("(h e) t -> e h t", e=P)[:, :, c * P:(c + 1) * P])
            a["tn"] = [dve.op(lambda e, h=h: e.tensor_scalar(
                hbuf[:, h, :], hbuf[:, h, :], mv[:, c, h, 0:1], rs[:, c, h:h + 1], ALU.subtract, ALU.mult), a["tr"])
                for h in range(4)]

        def finish(c):
            a = A.pop(c)
            z = a["z"]
            i, pb, f = pB.take()
            for h in range(4):
                t = pe.op(lambda e, h=h: e.transpose(pb[:, h * P:(h + 1) * P], a["hbuf"][:, h, :], ident[:]), a["tn"], f, t_id)
            hb.free[a["hi"]] = [t]
            yi, y, yf = yb.take()
            t = dve.op(lambda e: e.tensor_tensor(y[:], pb[:].rearrange("p (h t) -> p h t", h=4), z[1][:], ALU.mult),
                       t, z[2], yf)
            pB.free[i] = [t]
            zr.free[z[0]] = [t]
            yb.free[yi] = [self.store(self.y2T[4 * P:8 * P, :].rearrange("(h e) t -> e h t", e=P)[:, :, c * P:(c + 1) * P],
                                      y[:], yb.slots[yi], t)]

        for c in range(-2, C + 3):
            w = weigh(0, c) if 0 <= c < C - 1 else None
            for lag, step in ((3, finish), (1, gate), (-2, decays), (-1, scores), (0, lambda c: numerators(c, w)),
                              (1, moments), (2, normalise), (0, divide)):
                if 0 <= c - lag < C:
                    step(c - lag)


def program(nc, io, out, scratch="Internal", upto=9):
    kr = Kernel(nc, io, scratch)
    kr.out = out
    kr.yT = kr.dram("yT", (D, S))
    kr.mod = kr.dram("mod", (1, 3 * D))
    kr.h = kr.dram("h", (S, D))
    kr.hT2 = kr.dram("hT2", (D, S))
    kr.gt = kr.dram("gt", (P, NT * 16))
    kr.s = {n: kr.dram(n, (S, W) if n in ("mv", "mo") else (W, S))
            for n in ("nqh", "nql", "nkh", "nkl", "nz", "mq", "mk", "mv", "mo", "mz")}
    kr.Z = kr.dram("Z", (2, NA_H, 32, 17 * 40))
    kr.rpb = kr.dram("rpbp", (32, RPB))
    kr.V = kr.dram("V", (2, 32, 40, W))
    kr.nN = kr.dram("nN", (P, P))
    kr.y2T = kr.dram("y2T", (D, S))
    with kr.ctx:
        kr.phase(kr.pool_block)
        kr.phase(lambda: kr.out_block(io["pool_out_w"][0], kr.yT, io["x"][0], False))
        if upto >= 4:
            kr.phase(kr.in_block)
        if upto >= 5:
            kr.phase(kr.na_block)
        if upto >= 6:
            kr.phase(kr.ml_block)
        if upto >= 7:
            kr.phase(lambda: kr.out_block(io["w_out_2"][0], kr.y2T, kr.h, True))


_INS = ["x", "norm_w", "pool_in_w", "pool_group_w", "pool_group_b", "pool_scale", "pool_out_w", "final_norm_w",
        "c_2", "w_ada_2", "b_ada_2", "norm_w_2", "w_in_2", "b_in_2", "conv_w_2", "conv_b_2", "rpb_2", "ml_norm_w_2",
        "w_out_2", "final_norm_w_2"]


def kernel(**inputs):
    import numpy as np
    import concourse.bacc as bacc
    from concourse.bass_utils import run_bass_kernel_spmd

    nc = bacc.Bacc("TRN2", target_bir_lowering=False, num_devices=1)
    arrays, io = {}, {}
    for name in _INS:
        a = np.ascontiguousarray(inputs[name])
        arrays[f"in_{name}"] = a
        io[name] = nc.dram_tensor(f"in_{name}", a.shape, mybir.dt.from_np(a.dtype), kind="ExternalInput").ap()
    out = nc.dram_tensor("out", (1, S, D), F32, kind="ExternalOutput").ap()
    program(nc, io, out)
    r = run_bass_kernel_spmd(nc, [arrays], core_ids=[0])
    return r.results[0]["out"]
```

```python
from contextlib import ExitStack
from itertools import chain

import concourse.bass as bass
from concourse import mybir

F32 = mybir.dt.float32
F32R = mybir.dt.float32r
ALU = mybir.AluOpType
ACT = mybir.ActivationFunctionType
AX = mybir.AxisListType

P = 128
S = 2048
D = 1024
KT = D // P
NT = S // P
TB = 4
W = 512
EPS = 1e-6
NEG = -1.0e30
NA_H = 8
ML_H = 4
RPB = 128 + NA_H * 465


class Engine:

    def __init__(self, name, sem):
        self.name, self.sem, self.n, self.q, self.seen = name, sem, 0, [], {}

    def op(self, fn, *waits):
        self.q.append([fn, list(flat(waits)), (self.sem, 1)])
        self.n += 1
        return (self.sem, self.n)

    def quiet(self, fn, *waits):
        self.q.append([fn, list(flat(waits)), None])

    def dma(self, slot, out, in_, *waits, slow=False):
        slot.n += 16
        self.q.append([lambda e: e.dma_start(out, in_, allow_slow_non_contiguous=slow), list(flat(waits)), (slot.sem, 16)])
        return (slot.sem, slot.n)

    def wait(self, *waits):
        self.q.append([None, list(flat(waits)), None])

    def emit(self, e):
        for fn, waits, inc in self.q:
            for w in waits:
                if self.seen.get(id(w[0]), 0) < w[1]:
                    e.wait_ge(w[0], w[1])
                    self.seen[id(w[0])] = w[1]
            if fn is not None:
                ins = fn(e)
                if inc is not None:
                    ins.then_inc(inc[0], inc[1])
        self.q = []


def flat(ws):
    for w in ws:
        if isinstance(w, list):
            yield from flat(w)
        elif w is not None:
            yield w


class Slot:

    def __init__(self, sem):
        self.sem, self.n = sem, 0


class Ring:

    def __init__(self, bufs, slots=None):
        self.bufs, self.slots, self.i = bufs, slots, 0
        self.free = [[] for _ in bufs]

    def take(self):
        i = self.i % len(self.bufs)
        self.i += 1
        f, self.free[i] = self.free[i], None
        assert f is not None, "a buffer is taken again before its readers are queued"
        return i, self.bufs[i], f


class Kernel:
    def __init__(self, nc, io, scratch_kind):
        self.nc, self.io = nc, io
        self.ctx = ExitStack()
        self.pe, self.act, self.dve, self.pool, self.sp = (
            Engine(n, self.ctx.enter_context(nc.semaphore(f"done_{n}"))) for n in ("pe", "act", "dve", "pool", "sp"))
        self.nsem = 0
        self.slots = {False: [], True: []}
        self.pending = []
        self.kind = scratch_kind
        self.t_junk = None

    def slot(self, out=False):
        have, n = self.slots[out], self.nslot[out]
        if n == len(have):
            have.append(Slot(self.ctx.enter_context(self.nc.semaphore(f"dma_{'out' if out else 'in'}{n}"))))
        self.nslot[out] += 1
        return have[n]

    def dram(self, name, shape):
        return self.nc.dram_tensor(name, shape, F32, kind=self.kind).ap()

    def phase(self, fn):
        self.nslot = {False: 0, True: 0}
        self.pending = []
        with ExitStack() as ctx:
            self.px = ctx
            fn()
            self.sp.wait(self.pending)
            with self.nc.Block() as block:
                block.sync(self.sp.emit)
                block.scalar(self.act.emit)
                block.gpsimd(self.pool.emit)
                block.tensor(self.pe.emit)
                block.vector(self.dve.emit)

    def sb(self, name, shape, dt=F32):
        self.nsem += 1
        return self.px.enter_context(self.nc.sbuf_tensor(f"{name}_{self.nsem}", shape, dt))

    def ps(self, name, shape=(P, W), dt=F32):
        self.nsem += 1
        return self.px.enter_context(self.nc.psum_tensor(f"{name}_{self.nsem}", list(shape), dt))

    def ring(self, name, n, shape, dt=F32, dma=True, out=False):
        bufs = [self.sb(f"{name}{i}", shape, dt) for i in range(n)]
        return Ring(bufs, [self.slot(out) for _ in range(n)] if dma else None)

    def psring(self, name, n, shape=(P, W), dt=F32):
        return Ring([self.ps(f"{name}{i}", shape, dt) for i in range(n)])

    def load(self, ring, src, eng=None, dst=lambda b: b[:], after=()):
        i, b, free = ring.take()
        t = (eng or self.sp).dma(ring.slots[i], dst(b), src, free, *after)
        return i, b, t

    def store(self, dst, src, slot, *waits, eng=None):
        t = (eng or self.pool).dma(slot, dst, src, *waits)
        self.pending.append(t)
        return t

    def split(self, hi, lo, x, *waits):
        a = self.act.op(lambda e: e.activation(hi, x, ACT.Copy), *waits)
        d = self.dve.op(lambda e: e.tensor_tensor(lo, x, hi.bitcast(F32), ALU.subtract), a)
        return [a, d]

    def mm3(self, ps, lh, ll, rh, rl, first, last, *waits):
        pe = self.pe
        pe.quiet(lambda e: e.matmul(ps, lh, rh, start=first, stop=False), *waits)
        pe.quiet(lambda e: e.matmul(ps, lh, rl, start=False, stop=False))
        if last:
            return pe.op(lambda e: e.matmul(ps, ll, rh, start=False, stop=True))
        pe.quiet(lambda e: e.matmul(ps, ll, rh, start=False, stop=False))

    def identity(self):
        ident = self.sb("ident", [P, P])
        t = self.pool.op(lambda e: e.memset(ident[:], 0.0))
        t = self.pool.op(lambda e: e.affine_select(out=ident[:], in_=ident[:], compare_op=ALU.not_equal, fill=1.0,
                                                   base=0, pattern=[[-1, P]], channel_multiplier=1), t)
        return ident, t

    def row(self, vec, n, name="row"):
        t = self.sb(name, [P, n])
        return t, self.sp.dma(self.slot(), t[:], vec.partition_broadcast(P))

    def cols(self, vec, n, name="cols"):
        t = self.sb(name, [P, n])
        return t, self.sp.dma(self.slot(), t[:], vec.rearrange("(j p) -> p j", p=P), slow=True)

    def rstd(self, out, tmp, ssq, n, *waits):
        a = self.dve.op(lambda e: e.tensor_scalar(tmp, ssq, 1.0 / n, EPS, ALU.mult, ALU.add), *waits)
        return self.pool.op(lambda e: e.tensor_tensor(out, tmp, self.mhalf[:, 0:1], ALU.pow), a, self.t_mhalf)

    def minus_half(self, n=1):
        self.mhalf = self.sb("mhalf", [P, n])
        self.t_mhalf = self.pool.op(lambda e: e.memset(self.mhalf[:], -0.5))

    def sumsq(self, out, junk, x, *waits):
        self.t_junk = self.act.op(lambda e: e.activation(junk, x, ACT.Square, accum_out=out), self.t_junk, *waits)
        return self.t_junk

    def pool_block(self):
        hT = self.sb("hT", [P, 2, KT, S], F32R)
        hr = {}
        x = self.io["x"][0]
        with ExitStack() as sub:
            keep, self.px = self.px, sub
            ident, t_id = self.identity()
            xr = self.ring("x", 4, [P, D])
            xn = self.ring("xn", 2, [P, D], dma=False)
            junk = self.ps("junk", [P, D])
            st = self.sb("st", [P, NT, 3])
            tp = self.psring("tp", 4)
            self.minus_half()
            loads = {}

            def ld(m):
                i, b, t = self.load(xr, x[m * P:(m + 1) * P, :])
                loads[m] = (i, b, t, self.sumsq(st[:, m, 0:1], junk[:], b[:], t))

            def stat(m):
                loads[m] += (self.rstd(st[:, m, 2:3], st[:, m, 1:2], st[:, m, 0:1], D, loads[m][3]),)

            xns = {}

            def norm(m):
                i, b, t, _, tr = loads.pop(m)
                j, n, nf = xn.take()
                tn = self.dve.op(lambda e: e.scalar_tensor_tensor(
                    out=n[:], in0=b[:], scalar=st[:, m, 2:3], in1=nw[:], op0=ALU.mult, op1=ALU.mult), tr, t_nw, t, nf)
                xr.free[i] = [tn]
                xns[m] = (j, n, tn)

            for m in range(3):
                ld(m)
                stat(m)
            nw, t_nw = self.row(self.io["norm_w"][0], D)
            norm(0)
            for m in range(NT):
                if m + 3 < NT:
                    ld(m + 3)
                if m + 1 < NT:
                    norm(m + 1)
                j, n, tn = xns.pop(m)
                for g in range(2):
                    q, pb, pf = tp.take()
                    for k in range(4):
                        kk = 4 * g + k
                        f = lambda e, pb=pb, n=n, k=k, kk=kk: e.transpose(
                            pb[:, k * P:(k + 1) * P], n[:, kk * P:(kk + 1) * P], ident[:])
                        if k < 3:
                            self.pe.quiet(f, tn, pf, t_id)
                        else:
                            tt = self.pe.op(f)
                    sl = (slice(None), slice(4 * g, 4 * g + 4), slice(m * P, (m + 1) * P))
                    pv = pb[:].rearrange("p (k t) -> p k t", k=4)
                    hr[(m, g)] = self.split(hT[:, 0][sl], hT[:, 1][sl], pv, tt)
                    tp.free[q] = hr[(m, g)]
                xn.free[j] = [tt]
                if m + 3 < NT:
                    stat(m + 3)
            self.sp.wait(self.pending)
            self.pending = []
            with self.nc.Block() as block:
                block.sync(self.sp.emit)
                block.scalar(self.act.emit)
                block.gpsimd(self.pool.emit)
                block.tensor(self.pe.emit)
                block.vector(self.dve.emit)
            self.px = keep
        self.nslot = {False: 0, True: 0}

        win = self.io["pool_in_w"][0].rearrange("(k p) n -> p k n", p=P)
        gw = self.io["pool_group_w"][0]
        units = self.ring("wu", 4, [P, 2, KT, P], F32R, dma=False)
        raw = self.ring("raw", 2, [P, KT, P])
        graw = self.ring("graw", 1, [P, 2, 256])
        gsp = self.ring("gsp", 1, [P, 2, 2, 256], F32R, dma=False)
        ub = self.ring("ub", 2, [P, 16 + W], dma=False)
        sa = self.ring("sa", 2, [P, 16 + W], dma=False)
        pld = self.ring("pld", 1, [P, 2, 2, W], F32R, dma=False)
        sg = self.ring("sg", 3, [P, W], out=True)
        halo = self.sb("halo", [P, KT, 16])
        invc = self.sb("invc", [P, 4, 16])
        pg = self.psring("pg", 6)
        pm = self.psring("pm", 2)
        t_inv = None
        for g in range(4):
            w = 2 << g
            for c in range(16):
                t_inv = self.pool.op(lambda e, g=g, c=c, w=w: e.memset(invc[:, g, c:c + 1], 1.0 / min(c + 1, w)))
        t_h0 = self.pool.op(lambda e: e.memset(halo[:], 0.0))
        halos = {a: t_h0 for a in range(KT)}
        ada, tables = self.ada(pm), self.bias_tables()

        def unit(col):
            i, r, t = self.load(raw, win[:, :, col:col + P])
            j, u, f = units.take()
            ts = self.split(u[:, 0], u[:, 1], r[:], t, f)
            raw.free[i] = ts
            return j, u, ts

        def unit_cols(g):
            return [g * 256, g * 256 + P, D + g * 256, D + g * 256 + P]

        order = [c for g in range(4) for c in unit_cols(g)]
        ready = {}

        def prefetch(n):
            while len(ready) < min(n, 16):
                u = len(ready)
                ready[u] = unit(order[u])

        def proj(u, tb):
            j, wt, tw = ready[u]
            q, pb, pf = pg.take()
            for k in range(KT):
                t = self.mm3(pb[:], wt[:, 0, k, :], wt[:, 1, k, :], hT[:, 0, k, tb * W:(tb + 1) * W],
                             hT[:, 1, k, tb * W:(tb + 1) * W], k == 0, k == KT - 1, tw, pf)
            if tb == 3:
                units.free[j] = [t]
                prefetch(u + 5)
            return q, pb, t

        def load_gw(g):
            return self.load(graw, gw[g].rearrange("(k p) d -> p k d", p=P))

        prefetch(1)
        gld = load_gw(0)
        gb, t_gb = self.cols(self.io["pool_group_b"][0].rearrange("g c -> (g c)"), KT)
        sc, t_sc = self.cols(self.io["pool_scale"][0], KT)
        prefetch(4)
        for g in range(4):
            gi, gr, tgr = gld
            gj, gs, gf = gsp.take()
            tgs = self.split(gs[:, 0], gs[:, 1], gr[:], tgr, gf)
            graw.free[gi] = tgs
            for tb in range(4):
                pj, pl, plf = pld.take()
                tp2 = []
                for a in range(2):
                    q, pb, t = proj(4 * g + a, tb)
                    ch = 2 * g + a
                    ui, u, uf = ub.take()
                    tu = self.act.op(lambda e, u=u, pb=pb: e.activation(u[:, 16:], pb[:], ACT.Copy), t, uf)
                    pg.free[q] = [tu]
                    th = self.dve.op(lambda e, u=u, ch=ch: e.tensor_copy(u[:, 0:16], halo[:, ch, :]), halos[ch], uf)
                    halos[ch] = self.dve.op(lambda e, u=u, ch=ch: e.tensor_copy(halo[:, ch, :], u[:, W:W + 16]), tu, th)
                    cur, tc, lo = u, [tu, th], 0
                    for l in range(g + 1):
                        s = 1 << l
                        si, nx, sf = sa.take()
                        sa.free[si] = []
                        lo += s
                        tc = self.dve.op(lambda e, nx=nx, cur=cur, lo=lo, s=s: e.tensor_tensor(
                            nx[:, lo:], cur[:, lo:], cur[:, lo - s:16 + W - s], ALU.add), tc, sf)
                        cur = nx
                    c0, tr = 16, None
                    if tb == 0:
                        c0 = 32
                        tr = self.dve.op(lambda e, cur=cur, g=g: e.tensor_tensor(
                            cur[:, 16:32], cur[:, 16:32], invc[:, g, :], ALU.mult), tc, t_inv)
                        tr = self.dve.op(lambda e, cur=cur, u=u: e.tensor_tensor(
                            cur[:, 16:32], cur[:, 16:32], u[:, 16:32], ALU.subtract), tr)
                    tr = self.dve.op(lambda e, cur=cur, u=u, g=g, c0=c0: e.scalar_tensor_tensor(
                        out=cur[:, c0:], in0=cur[:, c0:], scalar=1.0 / (2 << g), in1=u[:, c0:],
                        op0=ALU.mult, op1=ALU.subtract), tc, tr)
                    ub.free[ui] = [tr, halos[ch]]
                    ts = self.split(pl[:, 0, a], pl[:, 1, a], cur[:, 16:], tr, plf)
                    sa.free[si] = ts
                    tp2 += ts
                    next(ada, None)
                gates = []
                for a in range(2):
                    q, pb, t = proj(4 * g + 2 + a, tb)
                    i, s, sf = sg.take()
                    t = self.act.op(lambda e, s=s, pb=pb: e.activation(s[:], pb[:], ACT.Silu), t, sf)
                    pg.free[q] = [t]
                    gates.append((i, s, t))
                    next(ada, None)
                for _ in range(2 if tb == 0 else 1):
                    next(tables, None)
                for a in range(2):
                    ch = 2 * g + a
                    q, pb, pf = pm.take()
                    for k in range(2):
                        t = self.mm3(pb[:], gs[:, 0, k, a * P:(a + 1) * P], gs[:, 1, k, a * P:(a + 1) * P],
                                     pl[:, 0, k], pl[:, 1, k], k == 0, k == 1, tgs, tp2, pf)
                    i, s, tsg = gates[a]
                    ty = self.dve.op(lambda e, s=s, pb=pb, ch=ch: e.scalar_tensor_tensor(
                        out=s[:], in0=pb[:], scalar=gb[:, ch:ch + 1], in1=s[:], op0=ALU.add, op1=ALU.mult), t, tsg, t_gb)
                    pm.free[q] = [ty]
                    ty = self.dve.op(lambda e, s=s, ch=ch: e.tensor_scalar(
                        s[:], s[:], sc[:, ch:ch + 1], None, ALU.mult), ty, t_sc)
                    sg.free[i] = [self.store(self.yT[ch * P:(ch + 1) * P, tb * W:(tb + 1) * W], s[:], sg.slots[i], ty)]
                pld.free[pj] = [t]
                if tb == 2 and g < 3:
                    gld = load_gw(g + 1)
            gsp.free[gj] = [t]
        for step in (ada, tables):
            for _ in step:
                pass

    def ada(self, pr):
        c = self.sb("c", [P, KT])
        ones = self.sb("ones", [P, 2])
        wr = self.ring("w", 2, [P, W])
        acc = self.sb("acc", [P, W])
        b_out = self.slot(True)
        t = self.sp.dma(self.slot(), c[:], self.io["c_2"][0].rearrange("(k p) -> p k", p=P), slow=True)
        t_c = self.act.op(lambda e: e.activation(c[:], c[:], ACT.Silu), t)
        t_1 = self.dve.op(lambda e: e.memset(ones[:], 1.0))
        t_acc = None
        def fetch():
            for j in range(6):
                sl = slice(j * W, (j + 1) * W)
                for k in range(KT):
                    yield self.load(wr, self.io["w_ada_2"][0][k * P:(k + 1) * P, sl])
                yield self.load(wr, self.io["b_ada_2"][:, sl], dst=lambda b: b[0:1, :])
            yield None

        src = fetch()
        nxt = next(src)
        for j in range(6):
            sl = slice(j * W, (j + 1) * W)
            for k in range(KT):
                yield
                (i, w, t), nxt = nxt, next(src)
                if k == 0:
                    ta = self.dve.op(lambda e, w=w: e.tensor_scalar(acc[:], w[:], c[:, 0:1], None, ALU.mult), t, t_c, t_acc)
                else:
                    ta = self.dve.op(lambda e, w=w, k=k: e.scalar_tensor_tensor(
                        out=acc[:], in0=w[:], scalar=c[:, k:k + 1], in1=acc[:], op0=ALU.mult, op1=ALU.add), t, ta)
                wr.free[i] = [ta]
            yield
            (i, b, t_b), nxt = nxt, next(src)
            q, pb, pf = pr.take()
            t_acc = self.pe.op(lambda e, pb=pb: e.matmul(pb[0:1, :], ones[:, 0:1], acc[:], start=True, stop=True), ta, t_1, pf)
            t = self.dve.op(lambda e, pb=pb, b=b: e.tensor_tensor(b[0:1, :], pb[0:1, :], b[0:1, :], ALU.add),
                            t_acc, t_b)
            pr.free[q] = [t]
            wr.free[i] = [self.store(self.mod[:, sl], b[0:1, :], b_out, t)]

    def out_block(self, w_dram, yT_dram, res, last):
        ident, t_id = self.identity()
        wv = w_dram.rearrange("(k p) n -> p k n", p=P)
        raw = self.ring("raw", 4, [P, W])
        ws = self.sb("ws", [P, 2, KT, D], F32R)
        tw = {}
        ys = self.ring("ys", 2, [P, 2, KT, W], F32R, dma=False)
        ysb = {}

        def load_w(k):
            for c in range(2):
                i, r, t = self.load(raw, wv[:, k, c * W:(c + 1) * W])
                sl = slice(c * W, (c + 1) * W)
                tw[(k, c)] = self.split(ws[:, 0, k, sl], ws[:, 1, k, sl], r[:], t)
                raw.free[i] = tw[(k, c)]

        def load_y(tb, k):
            if k == 0:
                j, y, f = ys.take()
                ysb[tb] = (j, y, [], f)
            j, y, ts, f = ysb[tb]
            i, r, t = self.load(raw, yT_dram[k * P:(k + 1) * P, tb * W:(tb + 1) * W])
            s = self.split(y[:, 0, k], y[:, 1, k], r[:], t, f)
            raw.free[i] = s
            ts.append(s)

        for k in range(KT):
            load_y(0, k)
            load_w(k)
        fw, t_fw = self.row(self.io["final_norm_w_2"] if last else self.io["final_norm_w"], D, "fw")
        if last:
            gate, t_gate = self.row(self.mod[0, 2 * D:3 * D], D, "gate")
        else:
            A, t_sc = self.row(self.mod[0, D:2 * D], D, "A")
            B, t_sh = self.row(self.mod[0, 0:D], D, "B")
            nw, t_nw = self.row(self.io["norm_w_2"][0], D, "nw")
            t_A = self.dve.op(lambda e: e.scalar_tensor_tensor(out=A[:], in0=A[:], scalar=1.0, in1=nw[:],
                                                               op0=ALU.add, op1=ALU.mult), t_sc, t_nw)
        self.minus_half()
        xr = self.ring("xr", 2, [P, D])
        hr = self.ring("hr", 4, [P, D], out=True)
        junk = self.sb("junk", [P, D])
        st = self.sb("st", [P, NT, 6])
        pg, tp = self.psring("pg", 6), self.psring("tp", 2)
        if not last:
            h1r = self.ring("h1", 2, [P, D], out=True)
            tr = self.ring("tr", 2, [P, KT, P], out=True)

        pend = []

        def norms(m, h, hi, t):
            s0 = self.sumsq(st[:, m, 0:1], junk[:], h[:], t)
            yield
            r0 = self.rstd(st[:, m, 2:3], st[:, m, 1:2], st[:, m, 0:1], D, s0)
            yield
            rows = slice(m * P, (m + 1) * P)
            if last:
                t1 = self.dve.op(lambda e: e.scalar_tensor_tensor(out=h[:], in0=h[:], scalar=st[:, m, 2:3], in1=fw[:],
                                                                  op0=ALU.mult, op1=ALU.mult), r0, t_fw, s0)
                hr.free[hi] = [self.store(self.out[0, rows, :], h[:], hr.slots[hi], t1)]
                return
            i1, h1, f1 = h1r.take()
            t1 = self.dve.op(lambda e: e.scalar_tensor_tensor(out=h1[:], in0=h[:], scalar=st[:, m, 2:3], in1=fw[:],
                                                              op0=ALU.mult, op1=ALU.mult), r0, t_fw, f1)
            s1 = self.sumsq(st[:, m, 3:4], junk[:], h1[:], t1)
            yield
            r1 = self.rstd(st[:, m, 5:6], st[:, m, 4:5], st[:, m, 3:4], D, s1)
            t_st = self.store(self.h[rows, :], h1[:], h1r.slots[i1], t1)
            yield
            t2 = self.dve.op(lambda e: e.scalar_tensor_tensor(out=h[:], in0=h1[:], scalar=st[:, m, 5:6], in1=A[:],
                                                              op0=ALU.mult, op1=ALU.mult), r1, t_A, s0)
            h1r.free[i1] = [t_st, t2, s1]
            t3 = self.dve.op(lambda e: e.tensor_tensor(h[:], h[:], B[:], ALU.add), t2, t_sh)
            pend.append((m, h, hi, t3))
            yield

        def turn():
            m, h, hi, t3 = pend.pop(0)
            oi, o, of = tr.take()
            te = []
            for g in range(2):
                q, pb, pf = tp.take()
                for k in range(4):
                    kk = 4 * g + k
                    f = lambda e, pb=pb, k=k, kk=kk: e.transpose(pb[:, k * P:(k + 1) * P], h[:, kk * P:(kk + 1) * P], ident[:])
                    tt = self.pe.op(f, t3, pf, t_id)
                e_ = self.act.op(lambda e, g=g, pb=pb: e.activation(
                    o[:, 4 * g:4 * g + 4, :], pb[:].rearrange("p (k t) -> p k t", k=4), ACT.Copy), tt, of)
                tp.free[q] = [e_]
                te.append(e_)
            hr.free[hi] = [tt]
            tr.free[oi] = [self.store(self.hT2.rearrange("(k p) t -> p k t", p=P)[:, :, m * P:(m + 1) * P],
                                      o[:], tr.slots[oi], te)]

        banks, running = {}, []

        def mm(tiles, rings):
            j, y, tys, _ = ysb[tiles[0] // 4]
            for m, ring in zip(tiles, rings):
                banks[m] = [[ring, *ring.take(), None] for _ in range(2)]
            for k in range(KT):
                for m in tiles:
                    o = (m % 4) * P
                    for c in range(2):
                        b = banks[m][c]
                        sl = slice(c * W, (c + 1) * W)
                        b[4] = self.mm3(b[2][:], y[:, 0, k, o:o + P], y[:, 1, k, o:o + P], ws[:, 0, k, sl], ws[:, 1, k, sl],
                                        k == 0, k == KT - 1, tys[k], tw[(k, c)], b[3])
            if tiles[-1] % 4 == 3:
                ys.free[j] = [(self.pe.sem, self.pe.n)]

        def evac(m):
            xi, x, tx = self.load(xr, res[m * P:(m + 1) * P, :])
            hi, h, hf = hr.take()
            th = []
            for c in range(2):
                ring, q, pb, _, t = banks[m][c]
                sl = slice(c * W, (c + 1) * W)
                if last:
                    t = self.dve.op(lambda e, pb=pb, sl=sl: e.tensor_tensor(h[:, sl], pb[:], gate[:, sl], ALU.mult),
                                    t, t_gate, hf)
                    ring.free[q] = [t]
                    t = self.pool.op(lambda e, sl=sl: e.tensor_tensor(h[:, sl], h[:, sl], x[:, sl], ALU.add), t, tx)
                else:
                    t = self.dve.op(lambda e, pb=pb, sl=sl: e.tensor_tensor(h[:, sl], pb[:], x[:, sl], ALU.add), t, tx, hf)
                    ring.free[q] = [t]
                th.append(t)
            xr.free[xi] = th
            cur, prev = norms(m, h, hi, th), running.pop() if running else iter(())
            for g in (cur, prev, cur, prev, prev):
                next(g, None)
            running.append(cur)

        mm([0, 1, 2, 3], [tp, pg, pg, pg])
        for k in range(KT):
            load_y(1, k)
        evac(0)
        evac(1)
        for m in range(4, NT):
            if m > 4 and pend:
                turn()
            mm([m], [pg])
            if m // 4 + 1 < TB:
                load_y(m // 4 + 1, 2 * (m % 4))
                load_y(m // 4 + 1, 2 * (m % 4) + 1)
            evac(m - 2)
        evac(NT - 2)
        for _ in range(3):
            next(running[0], None)
        if pend:
            turn()
        evac(NT - 1)
        for _ in range(3):
            if pend:
                turn()
            next(running[0], None)
        while pend:
            turn()

    def in_block(self):
        io = self.io
        hT = self.sb("hT", [P, 2, KT, S], F32R)
        NU = 6
        wu = self.sb("wu", [P, NU, 2, KT, P], F32R)
        ufree = [[] for _ in range(NU)]
        raw = self.ring("raw", 2, [P, KT, P])
        st = self.ring("st", 2, [P, W], out=True)
        vs = [self.slot() for _ in range(2)]
        win = io["w_in_2"][0].rearrange("(k p) n -> p k n", p=P)
        cu = self.ring("cu", 2, [P, 4 + W + 2], dma=False)
        ca = self.ring("ca", 2, [P, W + 2], out=True)
        pg = self.psring("pg", 8)

        hs = {}

        def load_h(tb, kk):
            i, r, t = self.load(raw, self.hT2.rearrange("(k p) t -> p k t", p=P)[:, 2 * kk:2 * kk + 2, tb * W:(tb + 1) * W],
                                dst=lambda b: b[:].rearrange("p k c -> p (k c)").rearrange("p (a t) -> p a t", a=2))
            v = r[:].rearrange("p k c -> p (k c)").rearrange("p (a t) -> p a t", a=2)
            sl = (slice(None), slice(2 * kk, 2 * kk + 2), slice(tb * W, (tb + 1) * W))
            s = self.split(hT[:, 0][sl], hT[:, 1][sl], v, t)
            raw.free[i] = s
            hs[(tb, 2 * kk)] = hs[(tb, 2 * kk + 1)] = s

        blocks = [(0, "nq"), (1, "nk"), (2, "nv"), (4, "mq"), (5, "mk"), (3, "nz"), (6, "mv"), (8, "mz"), (7, "mo")]
        cols = [b * W + j * P for b, _ in blocks for j in range(4)]
        ready = []

        def prefetch(n):
            while len(ready) < min(n, 36):
                u = len(ready)
                i, r, t = self.load(raw, win[:, :, cols[u]:cols[u] + P])
                s = self.split(wu[:, u % NU, 0], wu[:, u % NU, 1], r[:], t, ufree[u % NU])
                raw.free[i] = s
                ready.append(s)

        early = Ring(st.bufs, [self.slot() for _ in st.bufs])
        for k in range(KT):
            i, r, t = self.load(raw, win[:, k, 0:NU * P],
                                dst=lambda b: b[:].rearrange("p k c -> p (k c)")[:, 0:NU * P])
            v = r[:].rearrange("p k c -> p (k c)")[:, 0:NU * P].rearrange("p (u c) -> p u c", u=NU)
            raw.free[i] = tw0 = self.split(wu[:, :, 0, k, :], wu[:, :, 1, k, :], v, t)
            i, r, t = self.load(early, self.hT2[k * P:(k + 1) * P, 0:W])
            early.free[i] = th0 = self.split(hT[:, 0, k, 0:W], hT[:, 1, k, 0:W], r[:], t)
            hs[(0, k)] = tw0 + th0
        st.free = early.free
        ready += [[]] * NU
        bc, t_bc = self.cols(io["b_in_2"][0, 0:36 * P], 36)
        br = self.sb("br", [P, 3, W])
        t_br = [self.sp.dma(self.slot(), br[:, j, :], io["b_in_2"][0, c * W:(c + 1) * W].partition_broadcast(P))
                for j, c in enumerate((2, 6, 7))]
        bg = self.sb("bg", [16, 1])
        t_bg = self.sp.dma(self.slot(), bg[:], io["b_in_2"][0, 36 * P:36 * P + 16].rearrange("(p a) -> p a", a=1), slow=True)
        cw = self.sb("cw", [P, 5, 8])
        t_cw = self.sp.dma(self.slot(), cw[:], io["conv_w_2"][0].rearrange("j (c p) -> p j c", p=P), slow=True)
        cb, t_cb = self.cols(io["conv_b_2"][0], 8)
        mw, t_mw = self.cols(io["ml_norm_w_2"][0], 4)
        wgr = self.sb("wgr", [P, KT, 16])
        t_wg = self.sp.dma(self.slot(), wgr[:], win[:, :, 36 * P:36 * P + 16])
        wg = self.sb("wg", [P, 2, KT, 16], F32R)
        t_wgs = self.split(wg[:, 0], wg[:, 1], wgr[:], t_wg)

        def conv(name, j, tb, pb, t, state):
            ch = (4 if name == "mk" else 0) + j
            bcol = (4 if name == "mq" else 5) * 4 + j
            i, u, f = cu.take()
            tu = self.act.op(lambda e: e.activation(u[:, 4:4 + W], pb[:], ACT.Identity, bias=bc[:, bcol:bcol + 1]), t, f, t_bc)
            if tb == 0:
                th = self.dve.op(lambda e: e.memset(u[:, 2:4], 0.0), f)
            else:
                pu, ptu, pi = state[0]
                th = self.dve.op(lambda e: e.tensor_copy(u[:, 0:4], pu[:, W:W + 4]), f, ptu)
                cu.free[pi].append(th)
            tz = None
            lo, hi = (2 if tb == 0 else 0), (W + 2 if tb == 3 else W)
            if tb == 3:
                tz = self.dve.op(lambda e: e.memset(u[:, W + 4:W + 6], 0.0), f)
            state[0] = (u, tu, i)
            ai, a, af = ca.take()
            tc = self.dve.op(lambda e: e.tensor_scalar(a[:, lo:hi], u[:, lo:hi], cw[:, 0, ch:ch + 1], cb[:, ch:ch + 1],
                                                       ALU.mult, ALU.add), tu, th, tz, af, t_cw, t_cb)
            for w in range(1, 5):
                tc = self.dve.op(lambda e, w=w: e.scalar_tensor_tensor(
                    out=a[:, lo:hi], in0=u[:, lo + w:hi + w], scalar=cw[:, w, ch:ch + 1], in1=a[:, lo:hi],
                    op0=ALU.mult, op1=ALU.add), tc)
            cu.free[i] = [tc]
            ts = self.act.op(lambda e: e.activation(a[:, lo:hi], a[:, lo:hi], ACT.Silu), tc)
            o0 = tb * W - 2 + lo
            ca.free[ai] = [self.store(self.s[name][j * P:(j + 1) * P, o0:o0 + hi - lo], a[:, lo:hi], ca.slots[ai], ts)]
            return tu

        def evac_c(name, blk, j, tb, pb, t, state):
            if name in ("mq", "mk"):
                return conv(name, j, tb, pb, t, state)
            i, s, f = st.take()
            b = bc[:, blk * 4 + j:blk * 4 + j + 1]
            if name in ("nq", "nk"):
                i2, s2, f2 = st.take()
                hi, lo = s[:].bitcast(F32R), s2[:].bitcast(F32R)
                parts = [(hi, lo, s[:], pb[:])]
                if name == "nq":
                    parts = [tuple(v[:, o:o + P].rearrange("p (r c) -> p r c", r=4) for v in (hi, lo, s[:])) +
                             (pb[:, x * 256:(x + 1) * 256].rearrange("p (r c) -> p r c", r=4)[:, :, 32 * y:32 * y + 32],)
                             for x in range(2) for y in range(2) for o in (x * 256 + y * P,)]
                for h_, l_, hf, v in parts:
                    th = self.act.op(lambda e, h_=h_, v=v: e.activation(h_, v, ACT.Identity, bias=b), t, f, t_bc)
                for h_, l_, hf, v in parts:
                    te = self.dve.op(lambda e, l_=l_, hf=hf, v=v: e.scalar_tensor_tensor(
                        out=l_, in0=v, scalar=b, in1=hf, op0=ALU.add, op1=ALU.subtract), th, f2)
                dst = [self.s[name + x][j * P:(j + 1) * P, tb * W:(tb + 1) * W] for x in "hl"]
                st.free[i] = [self.store(dst[0], s[:], st.slots[i], th), te]
                st.free[i2] = [self.store(dst[1], s2[:], st.slots[i2], te)]
                return te
            te = t2 = self.act.op(lambda e: e.activation(s[:], pb[:], ACT.Silu, bias=b), t, f, t_bc)
            if name == "mz":
                t2 = self.dve.op(lambda e: e.tensor_scalar(s[:], s[:], mw[:, j:j + 1], None, ALU.mult), te, t_mw)
            st.free[i] = [self.store(self.s[name][j * P:(j + 1) * P, tb * W:(tb + 1) * W], s[:], st.slots[i], t2)]
            return te

        def gates():
            for tb in range(TB):
                q, pb, pf = pg.take()
                ts = slice(tb * W, (tb + 1) * W)
                for k in range(KT):
                    t = self.mm3(pb[0:16, :], wg[:, 0, k], wg[:, 1, k], hT[:, 0, k, ts], hT[:, 1, k, ts],
                                 k == 0, k == KT - 1, t_wgs, pf, hs[(tb, k)])
                i, s, f = st.take()
                t = self.act.op(lambda e, s=s, pb=pb: e.activation(s[0:16, :], pb[0:16, :], ACT.Identity, bias=bg[:, 0:1]),
                                t, f, t_bg)
                pg.free[q] = [t]
                st.free[i] = [self.store(self.gt[:, ts], s[0:16, :], st.slots[i], t)]

        for bi, (blk, name) in enumerate(blocks):
            u0 = 4 * bi
            if name == "nz":
                gates()
            if name in ("nv", "mv", "mo"):
                s0 = u0 % NU
                assert s0 + 4 <= NU
                x = ("nv", "mv", "mo").index(name)
                tw = ready[u0:u0 + 4]
                for m in range(NT):
                    q, pb, pf = pg.take()
                    for k in range(KT):
                        lh, ll = hT[:, 0, k, m * P:(m + 1) * P], hT[:, 1, k, m * P:(m + 1) * P]
                        t = self.mm3(pb[:], lh, ll, wu[:, s0:s0 + 4, 0, k, :], wu[:, s0:s0 + 4, 1, k, :],
                                     k == 0, k == KT - 1, tw, pf, hs[(m // 4, k)])
                    i, s, f = st.take()
                    t = self.dve.op(lambda e, s=s, pb=pb, x=x: e.tensor_tensor(s[:], pb[:], br[:, x, :], ALU.add), t, f, t_br[x])
                    pg.free[q] = [t]
                    if name == "mo":
                        t = self.act.op(lambda e, s=s: e.activation(s[:], s[:], ACT.Sigmoid), t)
                    if name == "nv":
                        st.free[i] = [self.store(self.V[a, 2 * m + y], s[64 * y + k0:64 * y + k0 + 40, :], vs[i], t, eng=self.sp)
                                      for y in range(2) for a, k0 in enumerate((0, 24))][-1:]
                    else:
                        st.free[i] = [self.store(self.s[name][m * P:(m + 1) * P, :], s[:], st.slots[i], t)]
                for j in range(4):
                    ufree[s0 + j] = [(self.pe.sem, self.pe.n)]
                prefetch(u0 + 4 + NU)
            else:
                order = [(u0 + j, tb) for j in range(4) for tb in range(TB)]
                if bi < 2:
                    order = [(u, tb) for tb in range(TB) for u in range(NU)] if bi == 0 else order[8:]
                if bi == 0:
                    first = [pg.take() for _ in range(NU)]
                    for k in range(KT):
                        for u in range(NU):
                            tf = self.mm3(first[u][1][:], wu[:, u, 0, k, :], wu[:, u, 1, k, :], hT[:, 0, k, 0:W],
                                          hT[:, 1, k, 0:W], k == 0, k == KT - 1, hs[(0, k)], first[u][2])
                            if k == KT - 1:
                                first[u] += (tf,)
                    for kk in range(3):
                        load_h(1, kk)
                for u, tb in order:
                        blk, name = blocks[u // 4]
                        j = u % 4
                        if tb == 0:
                            state = [None]
                        if bi == 0 and tb == 0:
                            q, pb, _, t = first[u]
                            pg.free[q] = [evac_c(name, blk, j, tb, pb, t, state)]
                            if u == 0:
                                load_h(1, 3)
                            continue
                        if bi == 0 and tb < 3 and u < 4:
                            load_h(tb + 1, u)
                        q, pb, pf = pg.take()
                        for k in range(KT):
                            t = self.mm3(pb[:], wu[:, u % NU, 0, k, :], wu[:, u % NU, 1, k, :],
                                         hT[:, 0, k, tb * W:(tb + 1) * W], hT[:, 1, k, tb * W:(tb + 1) * W],
                                         k == 0, k == KT - 1, ready[u], pf, hs[(tb, k)])
                        pg.free[q] = [evac_c(name, blk, j, tb, pb, t, state)]
                        if tb == 3:
                            ufree[u % NU] = [t]
                            prefetch(u + 1 + NU)

    def bias_tables(self):
        z = self.sb("z", [32, 64])
        t = self.dve.op(lambda e: e.memset(z[:], 0.0))
        n = NA_H * 465
        t_rpb = [
            self.store(self.rpb[:, 0:64], z[:], self.slot(True), t),
            self.store(self.rpb[:, 64 + n:128 + n], z[:], self.slot(True), t),
            self.store(self.rpb[:, 64:64 + n], self.io["rpb_2"].rearrange("a h y x -> (a h y x)").partition_broadcast(32),
                       self.slot(True))]
        zr = self.ring("zr", 1, [32, 17, 40])
        zo = [self.slot(True) for _ in range(2)]
        for a, X in enumerate((15, 7)):
            for h in range(NA_H):
                src = bass.AP(tensor=self.rpb.tensor, offset=64 + X + h * 465, ap=[[RPB - 1, 32], [31, 15], [1, 40]])
                i, zb, t = self.load(zr, src, dst=lambda b: b[:, 1:16, :], after=t_rpb)
                yield
                t = self.pool.op(lambda e, zb=zb: e.tensor_scalar(zb[:, 1:16, :], zb[:, 1:16, :], 8.0, 1.0,
                                                                  ALU.mult, ALU.mult), t)
                for y in (0, 16):
                    t = self.pool.op(lambda e, zb=zb, y=y: e.memset(zb[:, y, :], NEG), t)
                for c0, c1, base, step, cm in (((0, 40, 8, 1, -1), (16, 40, -9, -1, 1)) if a == 0 else
                                               ((0, 24, 0, 1, -1), (0, 40, 15, -1, 1))):
                    t = self.pool.op(lambda e, v=zb[:, 1:16, c0:c1], base=base, step=step, cm=cm, n=c1 - c0: e.affine_select(
                        out=v, in_=v, compare_op=ALU.is_ge, fill=NEG, base=base, pattern=[[0, 15], [step, n]],
                        channel_multiplier=cm), t)
                zr.free[i] = [self.store(self.Z[a, h], zb[:].rearrange("c y k -> c (y k)"), zo[i], t)]

    def na_block(self):
        self.gates_out = [self.ctx.enter_context(self.nc.sbuf_tensor(n, [P, 8, NT], F32)) for n in ("wT", "uT", "eT", "mpB", "dcB")]
        ident, t_id = self.identity()
        kinds = {"mid": (0, 12, 3), "top": (480, 9, 7), "bot": (840, 9, 2)}
        tabs = self.ring("tab", 2, [P, 2, 2, 1200])
        tslots = [[self.slot() for _ in range(6)] for _ in range(2)]
        hd = self.ring("hd", 4, [P, 3, S], F32R, dma=False)
        hslots = [[self.slot() for _ in range(3)] for _ in range(4)]
        zr = self.ring("z", 2, [P, S], dma=False)
        zslots = [[self.slot() for _ in range(3)] for _ in range(2)]
        vr = self.ring("v", 4, [120, 4, P])
        sr = self.ring("s", 5, [P, 480], dma=False)
        pr = self.ring("p", 5, [P, 480], dma=False)
        ptr = self.ring("pt", 3, [120, W], dma=False)
        yr = self.ring("y", 2, [P, 256], out=True)
        st = self.sb("st", [P, 128, 4])
        pS, pT, pO = self.psring("pS", 3), self.psring("pT", 2), self.psring("pO", 2)
        gates = self.gates(ident, t_id, self.psring("pG", 1))
        heads = {}

        def prep(hp):
            qk = [hd.take() for _ in range(2)]
            ti, tab, tf = tabs.take()
            zi, zb, zf = zr.take()
            cuts = (0, 768, 1280, S) if hp == 0 else (0, S)
            H = heads[hp] = dict(qk=qk, ti=ti, tab=tab, tq={}, tt={}, z=(zi, zb), tz=[], cuts=cuts[:-1])

            def part(hh, x):
                i, b, f = qk[hh]
                r = slice((2 * hp + hh) * 64, (2 * hp + hh + 1) * 64)
                c = slice(cuts[x], cuts[x + 1])
                for y, n in enumerate(("nqh", "nql", "nkh", "nkh", "nkl", "nkl")):
                    yield
                    H["tq"][hh, x] = self.sp.dma(hslots[i][x], b[64 * (y % 2):64 * (y % 2) + 64, y // 2, c].bitcast(F32),
                                                 self.s[n][r, c], f)

            def table(n, kind):
                off, nk, dd = kinds[kind]
                for a in range(2):
                    for ri in range(4):
                        y0 = 1 + dd - ri
                        yield
                        H["tt"][kind, a] = (self.sp if hp or n else self.act).dma(
                            tslots[ti][2 * n + a], tab[32 * ri:32 * ri + 32, :, a, off:off + nk * 40],
                            self.Z[a, 2 * hp:2 * hp + 2, :, y0 * 40:(y0 + nk) * 40].rearrange("h c y -> c h y"), tf)

            def gate(x):
                yield
                c = slice(cuts[x], cuts[x + 1])
                H["tz"].append(self.sp.dma(zslots[zi][x], zb[:, c], self.s["nz"][hp * P:(hp + 1) * P, c], zf))

            if hp:
                small = chain(*(table(n, kind) for n, kind in enumerate(("top", "mid", "bot"))))
                for _ in chain(part(0, 0), part(1, 0), gate(0)):
                    yield
                    for _ in range(2):
                        if next(small, 0) is None:
                            yield
                return
            yield from table(0, "top")
            yield from part(0, 0)
            yield from part(1, 0)
            yield from gate(0)
            yield from table(1, "mid")
            for x in range(1, len(cuts) - 1):
                yield from part(0, x)
                yield from part(1, x)
                yield from gate(x)
            yield from table(2, "bot")

        last = []

        def window(hp, kind):
            H = heads[hp]
            tab, tt = H["tab"], [H["tt"][kind, a] for a in range(2)]
            off, nk, _ = kinds[kind]
            tm = last[-1:]
            if kind == "mid":
                for ri in range(4):
                    for c0, c1 in ((0, ri * 40), ((ri + 8) * 40, 480)):
                        if c1 > c0:
                            tm = [self.pool.op(lambda e, ri=ri, c0=c0, c1=c1: e.memset(
                                tab[32 * ri:32 * ri + 32, :, :, c0:c1], NEG), tt, tm)]
            else:
                c0 = off + (320 if kind == "top" else 0)
                tm = [self.pool.op(lambda e, c0=c0: e.memset(tab[:, :, :, c0:c0 + 40], NEG), tt, tm)]
            last.extend(tm)
            H["t", kind] = [tt, tm]

        tiles = []
        for hp in range(4):
            for i in range(8):
                for a in range(2):
                    for hh in range(2):
                        tiles.append((hp, i, a, hh))
        info = {}

        def stage_q(n):
            hp, i, a, hh = tiles[n]
            H = heads[hp]
            kind = "top" if i == 0 else "bot" if i == 7 else "mid"
            off, nk, _ = kinds[kind]
            ks = {"top": 0, "bot": 23, "mid": 4 * i - 4}[kind]
            c0, k0 = (0, 0) if a == 0 else (32, 24)
            N = nk * 40
            if hh == 0:
                src = self.V[a, ks:ks + nk].rearrange("r c d -> (r c) d")[:, hp * P:(hp + 1) * P]
                vi, v, tv = self.load(vr, src.rearrange("(j p) d -> p j d", p=120), dst=lambda b: b[:, 0:nk // 3, :])
                info[n] = dict(v=v, vi=vi, tv=tv)
            else:
                info[n] = dict(v=info[n - 1]["v"], vi=info[n - 1]["vi"], tv=info[n - 1]["tv"])
            d = info[n]
            hi_, b, _ = H["qk"][hh]
            tq = [H["tq"][hh, x] for x, c in enumerate(H["cuts"]) if c < 64 * (ks + nk)]
            q = b[:, 0, (2 * i + a) * P:(2 * i + a + 1) * P]
            k = [b[:, x, :].rearrange("p (r c) -> p r c", c=64)[:, ks:ks + nk, k0:k0 + 40] for x in (1, 2)]
            si, ps, pf = pS.take()
            self.pe.quiet(lambda e: e.matmul(ps[:, 0:N], q, k[0], start=True, stop=False), tq, pf)
            t = self.pe.op(lambda e: e.matmul(ps[:, 0:N], q, k[1], start=False, stop=True))
            if n % 32 >= 30:
                hd.free[hi_] = [t]
            d = info[n]
            d.update(si=si, ps=ps, t=t, N=N, nk=nk, kind=kind, off=off)

        def stage_a(n):
            hp, i, a, hh = tiles[n]
            H, d = heads[hp], info[n]
            si, ps, t, N, off, kind = (d[x] for x in ("si", "ps", "t", "N", "off", "kind"))
            bi, s, sf = sr.take()
            tab = H["tab"][:, hh, a, off:off + N]
            t = self.dve.op(lambda e: e.tensor_tensor_reduce(
                out=s[:, 0:N], in0=ps[:, 0:N], in1=tab, scale=0.125, scalar=-3.0e38, op0=ALU.add, op1=ALU.max,
                accum_out=st[:, n, 0:1]), t, H["t", kind], sf)
            pS.free[si] = [t]
            tn = self.dve.op(lambda e: e.tensor_scalar(st[:, n, 1:2], st[:, n, 0:1], -1.0, None, ALU.mult), t)
            pi, p, pff = pr.take()
            te = self.act.op(lambda e: e.activation(p[:, 0:N], s[:, 0:N], ACT.Exp, bias=st[:, n, 1:2],
                                                    accum_out=st[:, n, 2:3]), tn, t, pff)
            sr.free[bi] = [te]
            d.update(p=p, pi=pi, te=te)
            if n % 32 == 31:
                tabs.free[H["ti"]] = [t]

        def stage_r(n):
            d = info[n]
            p, N = d["p"], d["N"]
            tr = self.dve.op(lambda e: e.reciprocal(st[:, n, 3:4], st[:, n, 2:3]), d["te"])
            d["te"] = self.pool.op(lambda e: e.tensor_scalar(p[:, 0:N], p[:, 0:N], st[:, n, 3:4], 1.0, ALU.mult, ALU.mult),
                                   d["te"], tr, last[-1:])

        def stage_b(n):
            d = info[n]
            nj = d["nk"] // 3
            qi, ps, pf = pT.take()
            for j in range(nj):
                t = self.pe.op(lambda e, j=j: e.transpose(ps[0:120, j * P:(j + 1) * P], d["p"][:, j * 120:(j + 1) * 120],
                                                          ident[:]), d["te"], pf, t_id)
            pr.free[d["pi"]] = [t]
            d.update(qi=qi, ps=ps, t=t)

        def stage_e(n):
            d = info[n]
            nj, qi, ps, t = d["nk"] // 3, d["qi"], d["ps"], d["t"]
            i, pt, f = ptr.take()
            if n % 2:
                te = self.act.op(lambda e: e.activation(pt[:, 0:nj * P], ps[0:120, 0:nj * P], ACT.Copy), t, f)
            else:
                te = self.dve.op(lambda e: e.tensor_copy(pt[:, 0:nj * P], ps[0:120, 0:nj * P]), t, f)
            pT.free[qi] = [te]
            d.update(pt=pt, pti=i, tpt=te)

        def stage_c(n):
            hp, i, a, hh = tiles[n]
            d = info[n]
            nj = d["nk"] // 3
            if hh == 0:
                d["oi"], d["o"], d["of"] = pO.take()
            else:
                d["oi"], d["o"], d["of"] = (info[n - 1][x] for x in ("oi", "o", "of"))
            po = d["o"]
            for j in range(nj):
                t = self.pe.op(lambda e, j=j: e.matmul(po[64 * hh:64 * hh + 64, 0:P], d["v"][:, j, 64 * hh:64 * hh + 64],
                                                       d["pt"][:, j * P:(j + 1) * P], start=(j == 0),
                                                       stop=(j == nj - 1)), d["tpt"], d["tv"], d["of"])
            ptr.free[d["pti"]] = [t]
            if hh == 0:
                return
            vr.free[d["vi"]] = [t]
            H = heads[hp]
            if a == 0:
                yb[0] = yr.take()
            yi, y, yf = yb[0]
            c0 = 32 * a
            z = H["z"][1][:].rearrange("p (r c) -> p r c", c=64)[:, 4 * i:4 * i + 4, c0:c0 + 32]
            t = self.dve.op(lambda e: e.tensor_tensor(y[:].rearrange("p (r c) -> p r c", c=64)[:, :, c0:c0 + 32],
                                                      po[:, 0:P].rearrange("p (r c) -> p r c", c=32), z, ALU.mult),
                            t, [x for x, c in zip(H["tz"], H["cuts"]) if c < 256 * (i + 1)], yf)
            pO.free[d["oi"]] = [t]
            if a == 1:
                yr.free[yi] = [self.store(self.y2T[hp * P:(hp + 1) * P, i * 256:(i + 1) * 256], y[:], yr.slots[yi], t)]
            if n % 32 == 31:
                zr.free[H["z"][0]] = [t]

        yb = {}
        coming = prep(0)
        for _ in range(21):
            next(coming)
        window(0, "top")
        stage_q(0)
        for n in range(128 + 5):
            hp = n // 32 + 1
            if n == 3:
                window(0, "mid")
            if n == 24:
                window(0, "bot")
            if (n == 15 or n > 32 and n % 32 == 5) and hp < 4:
                for _ in coming:
                    pass
                coming = prep(hp)
            if n % 32 == 29 and hp < 4:
                for _ in coming:
                    pass
                for kind in kinds:
                    window(hp, kind)
            for _ in range(3 if n < 32 else 1 + n % 2):
                next(coming, None)
            if n % 2:
                next(gates, None)
            for lag, step in ((-1, stage_q), (0, stage_a), (1, stage_r), (3, stage_b), (4, stage_e), (5, stage_c)):
                if 0 <= n - lag < 128:
                    step(n - lag)
        for _ in gates:
            pass

    def gates(self, ident, t_id, ring):
        dve, act, pe, pool, sp = self.dve, self.act, self.pe, self.pool, self.sp
        C = NT
        ones, zero = self.sb("ones", [P, P]), self.sb("zero", [P, P])
        t_1 = pool.op(lambda e: e.memset(ones[:], 1.0))
        t_0 = pool.op(lambda e: e.memset(zero[:], 0.0))
        X = {n: self.sb(n, [P, P]) for n in ("I", "F", "lf", "b", "u", "M", "nN", "w", "em")}
        tIF = {n: [sp.dma(self.slot(), X[n][64 * d:64 * d + 64, :],
                          self.gt[8 * d + 4 * f:8 * d + 4 * f + 4, :].rearrange("h (c t) -> (h c) t", c=C)) for d in range(2)]
               for f, n in enumerate("IF")}
        yield
        def turn(dst, src, *ts):
            i, pb, f = ring.take()
            t = pe.op(lambda e: e.transpose(pb[:, 0:P], src, ident[:]), t_id, f, *ts)
            yield
            t = dve.op(lambda e: e.tensor_copy(dst, pb[:, 0:P]), t)
            ring.free[i] = [t]
            return t

        tI, tF = tIF["I"], tIF["F"]
        t = act.op(lambda e: e.activation(X["w"][:], X["F"][:], ACT.Abs), tF)
        t = act.op(lambda e: e.activation(X["em"][:], X["w"][:], ACT.Exp, scale=-1.0), t)
        t = act.op(lambda e: e.activation(X["u"][:], X["em"][:], ACT.Ln, bias=1.0), t)
        yield
        tlf = dve.op(lambda e: e.scalar_tensor_tensor(out=X["lf"][:], in0=X["F"][:], scalar=0.0, in1=X["u"][:],
                                                      op0=ALU.min, op1=ALU.subtract), t, tF)

        def both(fn, *ts):
            return [dve.op(lambda e, r=r, o=o: fn(e, r, o), *ts)
                    for r, o in ((slice(0, 64), slice(None)), (slice(64, 128), slice(None, None, -1)))]

        tb_ = both(lambda e, r, o: e.tensor_tensor_scan(X["b"][r, o], ones[r, :], X["lf"][r, o], 0.0,
                                                        ALU.mult, ALU.add), tlf, t_1)
        tu = dve.op(lambda e: e.tensor_tensor(X["u"][:], X["I"][:], X["b"][:], ALU.subtract), tI, tb_)
        yield
        tM = both(lambda e, r, o: e.tensor_tensor_scan(X["M"][r, o], zero[r, :], X["u"][r, o], -3.0e38,
                                                       ALU.add, ALU.max), tu, t_0)
        yield
        L = self.sb("L", [P, 8])
        tl = []
        for r, z in ((slice(0, 64), P - 1), (slice(64, 128), 0)):
            tl.append(dve.op(lambda e, r=r, z=z: e.tensor_copy(L[r, 0:1], X["b"][r, z:z + 1]), tb_))
            tl.append(dve.op(lambda e, r=r, z=z: e.tensor_copy(L[r, 1:2], X["M"][r, z:z + 1]), tM))
        tl.append(dve.op(lambda e: e.tensor_tensor(L[:, 2:3], L[:, 0:1], L[:, 1:2], ALU.add), tl))
        R = self.sb("R", [1, 4, P])
        tR = []
        for x, col in enumerate((0, 2)):
            i, pb, f = ring.take()
            t = pe.op(lambda e, pb=pb, col=col: e.matmul(pb[0:1, 0:P], L[:, col:col + 1], ident[:], start=True, stop=True),
                      tl, f, t_id)
            yield
            t = dve.op(lambda e, pb=pb, x=x: e.tensor_copy(R[:, x, :], pb[0:1, 0:P]), t)
            ring.free[i] = [t]
            tR.append(t)
        yield
        tm = []
        for n in range(8):
            o = slice(n * C, (n + 1) * C) if n < 4 else slice((n + 1) * C - 1, n * C - 1 if n * C > 0 else None, -1)
            tm.append(dve.op(lambda e, o=o: e.tensor_tensor_scan(R[:, 2, o], R[:, 0, o], R[:, 1, o], 0.0, ALU.add, ALU.max), tR))
        t = dve.op(lambda e: e.memset(R[:, 3, :], 0.0))
        Rp = R[:, 3, :].rearrange("p (n c) -> p n c", c=C)
        Rn = R[:, 2, :].rearrange("p (n c) -> p n c", c=C)
        tp = [dve.op(lambda e: e.tensor_copy(Rp[:, 0:4, 1:C], Rn[:, 0:4, 0:C - 1]), tm, t),
              dve.op(lambda e: e.tensor_copy(Rp[:, 4:8, 0:C - 1], Rn[:, 4:8, 1:C]), tm, t)]
        i, pb, f = ring.take()
        t = pe.op(lambda e, pb=pb: e.matmul(pb[:, 0:1], R[:, 3, :], ones[0:1, 0:1], start=True, stop=True), tp, t_1, f)
        yield
        tmp = dve.op(lambda e, pb=pb: e.tensor_copy(L[:, 3:4], pb[:, 0:1]), t)
        ring.free[i] = [tmp]
        tN = dve.op(lambda e: e.tensor_scalar(X["nN"][:], X["M"][:], L[:, 3:4], -1.0, ALU.max, ALU.mult), tM, tmp)
        tNl = dve.op(lambda e: e.tensor_scalar(L[:, 4:5], L[:, 1:2], L[:, 3:4], -1.0, ALU.max, ALU.mult), tl, tmp)
        tNd = self.store(self.nN, X["nN"][:], self.slot(True), tN)
        tw = act.op(lambda e: e.activation(X["w"][:], X["u"][:], ACT.Exp, bias=L[:, 4:5]), tu, tNl, tlf)
        tdc = act.op(lambda e: e.activation(L[:, 5:6], L[:, 3:4], ACT.Exp, bias=L[:, 4:5]), tNl)
        t = dve.op(lambda e: e.tensor_tensor(X["I"][:], X["nN"][:], X["b"][:], ALU.subtract), tN, tb_, tu)
        tem = act.op(lambda e: e.activation(X["em"][:], X["I"][:], ACT.Exp), t)
        yield
        wT, uT, eT, mpB, dcB = self.gates_out
        flat2 = lambda a: a[:].rearrange("p n c -> p (n c)")
        for a, n, ts in ((wT, "w", tw), (uT, "u", tu), (eT, "em", tem)):
            yield from turn(flat2(a), X[n][:], ts)
        dg = self.sb("dg", [P, 2, P])
        for x, (col, a, ts) in enumerate(((3, mpB, tmp), (5, dcB, tdc))):
            t = dve.op(lambda e, x=x, col=col: e.tensor_scalar(dg[:, x, :], ident[:], L[:, col:col + 1], None, ALU.mult), ts, t_id)
            i, pb, f = ring.take()
            t = pe.op(lambda e, pb=pb, x=x: e.matmul(pb[:, 0:P], ones[:], dg[:, x, :], start=True, stop=True), t, f, t_1)
            yield
            t = dve.op(lambda e, pb=pb, a=a: e.tensor_copy(flat2(a), pb[:, 0:P]), t)
            ring.free[i] = [t]

    def ml_block(self):
        dve, act, pe, pool, sp = self.dve, self.act, self.pe, self.pool, self.sp
        C = NT
        ident, t_id = self.identity()
        mask = self.sb("mask", [P, 2, P])
        t_mask = []
        for d in range(2):
            t = pool.op(lambda e, d=d: e.memset(mask[:, d, :], 0.0))
            s = 1 if d == 0 else -1
            t_mask.append(pool.op(lambda e, d=d, s=s: e.affine_select(
                out=mask[:, d, :], in_=mask[:, d, :], compare_op=ALU.is_ge, fill=NEG, base=0,
                pattern=[[s, P]], channel_multiplier=-s), t))
        kC = self.sb("kC", [P, 4, S])
        v1 = self.sb("v1", [P, C, 4, P + 1])
        tk, tv = {}, {}
        for c in range(C - 1, -1, -1):
            if c in (15, 13, 11, 7, 3):
                n = 2 if c > 12 else 4
                t = sp.dma(self.slot(), kC[:, :, (c + 1 - n) * P:(c + 1) * P],
                           self.s["mk"].rearrange("(h d) t -> d h t", d=P)[:, :, (c + 1 - n) * P:(c + 1) * P])
                tk.update({c - x: t for x in range(n)})
            tv[c] = sp.dma(self.slot(), v1[:, c, :, 0:P], self.s["mv"][c * P:(c + 1) * P, :].rearrange("t (h e) -> t h e", h=4))
        tv1 = pool.op(lambda e: e.memset(v1[:, :, :, P:P + 1], 1.0))
        kT = self.sb("kT", [P, C, 4, P])
        Cb = self.sb("Cb", [P, C, 4, P + 1])
        pA = self.psring("pA", 1)
        pB = self.psring("pB", 1)
        pU, pN = self.psring("pU", 2, (P, 2 * (P + 1))), self.psring("pN", 2, (P, 2 * W))
        pW = Ring(pU.bufs + [b[:, g * W:(g + 1) * W] for b in pN.bufs for g in range(2)])

        wT, uT, eT, mpB, dcB = self.gates_out
        tuT = twT = teT = tB = tNd = None

        SC = P ** -0.5
        wv = self.ring("wv", 3, [P, 4, P + 1], dma=False)
        tkT = {}

        def kturn(c):
            ring = (pA, pB)[c % 2]
            i, pb, f = ring.take()
            for h in range(4):
                t = pe.op(lambda e, h=h: e.transpose(pb[:, h * P:(h + 1) * P], kC[:, h, c * P:(c + 1) * P], ident[:]),
                          tk[c], f, t_id)
            tkT[c] = act.op(lambda e: e.activation(kT[:, c].rearrange("p h d -> p (h d)"), pb[:], ACT.Copy, scale=SC), t)
            ring.free[i] = [tkT[c]]

        def weigh(d, c):
            i, w, f = wv.take()
            return i, w, pool.op(lambda e: e.tensor_tensor(
                w[:], v1[:, c], wT[:, 4 * d:4 * d + 4, c:c + 1].to_broadcast([P, 4, P + 1]), ALU.mult), tv[c], tv1, twT, f)

        def products(weighed, c, ring):
            i, w, t = weighed
            out = []
            for g in range(2):
                q, pb, pf = ring.take()
                for h in (2 * g, 2 * g + 1):
                    tt = pe.op(lambda e, h=h, g=g, pb=pb: e.matmul(
                        pb[:, (h - 2 * g) * (P + 1):(h - 2 * g + 1) * (P + 1)], kT[:, c, h, :], w[:, h, :],
                        start=True, stop=True), t, tkT[c], pf)
                out.append((ring, q, pb, tt))
            wv.free[i] = [tt]
            return out

        def update(d, c, prods, new, old, t_old, *free):
            out = []
            for g, (ring, q, pb, tt) in enumerate(prods):
                for h in (2 * g, 2 * g + 1):
                    src = pb[:, (h - 2 * g) * (P + 1):(h - 2 * g + 1) * (P + 1)]
                    if old is None:
                        o = dve.op(lambda e, h=h, src=src: e.tensor_copy(new[:, h, :], src), tt, *free)
                    else:
                        o = dve.op(lambda e, h=h, src=src: e.scalar_tensor_tensor(
                            out=new[:, h, :], in0=old[:, h, :], scalar=dcB[:, 4 * d + h, c:c + 1], in1=src,
                            op0=ALU.mult, op1=ALU.add), tt, t_old, tB, *free)
                    out.append(o)
                ring.free[q] = [o]
            return out

        tCb = {C - 1: None}
        for c in (C - 1, C - 2):
            kturn(c)
        w = [weigh(1, C - 1), weigh(1, C - 2)]
        for c in range(C - 1, 0, -1):
            if c > 1:
                kturn(c - 2)
            if c > 2:
                w.append(weigh(1, c - 2))
            tCb[c - 1] = update(1, c, products(w.pop(0), c, pW), Cb[:, c - 1], None if c == C - 1 else Cb[:, c], tCb[c])
        pU.free, pN.free = pW.free[:2], [pW.free[2] + pW.free[3], pW.free[4] + pW.free[5]]

        qr = self.ring("q", 2, [P, 4, P])
        orr = self.ring("o", 2, [P, 4, P])
        zr = self.ring("z", 2, [P, 4, P])
        nb = self.ring("nb", 3, [P, 4, P])
        eb = self.ring("eb", 6, [P, 4, P], dma=False)
        ib = self.ring("ib", 6, [P, 4, P], dma=False)
        hb = self.ring("hb", 3, [P, 4, P], dma=False)
        yb = self.ring("yb", 2, [P, 4, P])
        rd = self.sb("rd", [P, C, 2, 4])
        bn = self.sb("bn", [P, C, 4, 6])
        mv = self.sb("mv", [P, C, 4, 2])
        rs, mb = self.sb("rs", [P, C, 4]), self.sb("mb", [P, C, 4])
        self.minus_half(4)
        A = {}

        def decays(c):
            cs = slice(c * P, (c + 1) * P)
            A[c] = dict(dirs=[], q=self.load(qr, self.s["mq"].rearrange("(h d) t -> d h t", d=P)[:, :, cs]))
            for d in range(2):
                src = self.nN.rearrange("(n c) t -> n c t", c=C)[4 * d:4 * d + 4, c, :]
                n = self.load(nb, src.partition_broadcast(P), after=[tNd])
                ei, x, ef = eb.take()
                tm_ = pool.op(lambda e, x=x, n=n, d=d: e.tensor_tensor(
                    x[:], n[1][:], mask[:, d:d + 1, :].to_broadcast([P, 4, P]), ALU.add), n[2], t_mask[d], ef)
                D_ = dict(x=x, ei=ei)
                if not (d == 0 and c == 0 or d == 1 and c == C - 1):
                    D_["ii"], y, yf = ib.take()
                    D_["y"] = y
                    D_["ty"] = [act.op(lambda e, y=y, n=n, d=d, h=h: e.activation(
                        y[:, h, :], n[1][:, h, :], ACT.Exp, bias=mpB[:, 4 * d + h, c:c + 1]), n[2], tB, yf)
                        for h in range(4)]
                D_["tx"] = [act.op(lambda e, x=x, d=d, h=h: e.activation(
                    x[:, h, :], x[:, h, :], ACT.Exp, bias=uT[:, 4 * d + h, c:c + 1]), tm_, tuT) for h in range(4)]
                nb.free[n[0]] = [tm_] + D_.get("ty", [])
                A[c]["dirs"].append(D_)

        def scores(c):
            cs = slice(c * P, (c + 1) * P)
            q = A[c]["q"]
            si, ps, pf = pA.take()
            for h in range(4):
                t = pe.op(lambda e, h=h: e.matmul(ps[:, h * P:(h + 1) * P], kC[:, h, cs], q[1][:, h, :],
                                                  start=True, stop=True), q[2], tk[c], pf)
            tx, tq = [], []
            for D_ in A[c]["dirs"]:
                x = D_["x"]
                D_["tP"] = dve.op(lambda e, x=x: e.scalar_tensor_tensor(
                    out=x[:], in0=ps[:].rearrange("p (h t) -> p h t", h=4), scalar=SC, in1=x[:],
                    op0=ALU.mult, op1=ALU.mult), t, D_["tx"])
                tx.append(D_["tP"])
            for D_ in A[c]["dirs"]:
                if "y" in D_:
                    y = D_["y"]
                    D_["tq"] = dve.op(lambda e, y=y: e.tensor_tensor(y[:], y[:], q[1][:], ALU.mult), D_["ty"], q[2])
                    tq.append(D_["tq"])
            pA.free[si] = tx
            qr.free[q[0]] = [t] + tq

        fw = [None, None]

        def weights(c):
            A[c]["w"] = weigh(0, c) if c < C - 1 else None

        def numerators(c):
            a = A[c]
            a["num"] = []
            for d in range(2):
                D_ = a["dirs"][d]
                st_, t_st = fw if d == 0 else (Cb[:, c], tCb[c])
                i, pb, f = pN.take()
                for h in range(4):
                    o0 = (h // 2) * W + (h % 2) * (P + 1)
                    o = pb[:, o0:o0 + P + 1]
                    inter = "tq" in D_
                    t = pe.op(lambda e, o=o, D_=D_, h=h, inter=inter: e.matmul(
                        o, D_["x"][:, h, :], v1[:, c, h, :], start=True, stop=not inter), D_["tP"], tv[c], tv1, f)
                    if inter:
                        t = pe.op(lambda e, o=o, D_=D_, h=h, st_=st_: e.matmul(
                            o, D_["y"][:, h, :], st_[:, h, :], start=False, stop=True), D_["tq"], t_st)
                a["num"].append((i, pb, t))
                eb.free[D_["ei"]] = [t]
                if inter:
                    ib.free[D_["ii"]] = [t]
            a["used"] = t
            a["prods"] = products(a["w"], c, pU) if c < C - 1 else None

        def advance(c):
            if c < C - 1:
                fw[:] = Cb[:, c], update(0, c, A[c]["prods"], Cb[:, c], fw[0], fw[1], A[c]["used"])

        def divide(c):
            a = A[c]
            cs = slice(c * P, (c + 1) * P)
            a["o"] = self.load(orr, self.s["mo"][cs, :].rearrange("t (h e) -> t h e", h=4))
            hi, hbuf, tH = hb.take()
            heads = lambda v: v.rearrange("p (g h) e -> p g h e", g=2)
            num, tr = [], []
            for d in range(2):
                i, pb, t = a["num"][d]
                n = pb[:].rearrange("p (g x) -> p g x", g=2)[:, :, 0:2 * (P + 1)].rearrange("p g (h e) -> p g h e", h=2)
                den, r = n[:, :, :, P:P + 1], heads(rd[:, c, d, :].unsqueeze(2))
                x = dve.op(lambda e, den=den, d=d, r=r: e.scalar_tensor_tensor(
                    out=r, in0=den, scalar=-1.0, in1=heads(eT[:, 4 * d:4 * d + 4, c:c + 1]), op0=ALU.mult, op1=ALU.max), t, teT)
                tr.append(dve.op(lambda e, den=den, r=r: e.tensor_tensor(r, r, den, ALU.max), x))
                num.append(n[:, :, :, 0:P])
            tr = dve.op(lambda e: e.reciprocal(rd[:, c], rd[:, c]), tr)
            tH = dve.op(lambda e: e.tensor_tensor(
                heads(hbuf[:]), num[0], heads(rd[:, c, 0, :].unsqueeze(2)).to_broadcast([P, 2, 2, P]), ALU.mult), tr, tH)
            pN.free[a["num"][0][0]] = [tH]
            tH = [dve.op(lambda e, h=h: e.scalar_tensor_tensor(
                out=hbuf[:, h, :], in0=num[1][:, h // 2, h % 2, :], scalar=rd[:, c, 1, h:h + 1], in1=hbuf[:, h, :],
                op0=ALU.mult, op1=ALU.add), tH) for h in range(4)]
            pN.free[a["num"][1][0]] = [tH[-1]]
            a.update(hi=hi, hbuf=hbuf, tH=tH)

        def gate(c):
            a = A[c]
            o, hbuf = a["o"], a["hbuf"]
            a["tg"] = pool.op(lambda e: e.tensor_tensor(hbuf[:], hbuf[:], o[1][:], ALU.mult), a["tH"], o[2])
            orr.free[o[0]] = [a["tg"]]

        def moments(c):
            a = A[c]
            hbuf = a["hbuf"]
            tb = [dve.op(lambda e, h=h: e.bn_stats(bn[:, c, h, :], hbuf[:, h, :]), a["tg"]) for h in range(4)]
            tb = [dve.op(lambda e, h=h: e.bn_aggr(mv[:, c, h, :], bn[:, c, h, :]), tb[h]) for h in range(4)]
            t = dve.op(lambda e: e.tensor_scalar(rs[:, c, :].unsqueeze(2), mv[:, c, :, 1:2], EPS, None, ALU.add), tb)
            t = pool.op(lambda e: e.tensor_tensor(rs[:, c, :], rs[:, c, :], self.mhalf[:], ALU.pow), t, self.t_mhalf)
            t = pool.op(lambda e: e.tensor_tensor(mb[:, c, :], mv[:, c, :, 0], rs[:, c, :], ALU.mult), t)
            a["tmb"] = pool.op(lambda e: e.tensor_scalar(mb[:, c, :], mb[:, c, :], -1.0, 1.0, ALU.mult, ALU.mult), t)

        def normalise(c):
            a = A[c]
            hbuf = a["hbuf"]
            a["z"] = self.load(zr, self.s["mz"].rearrange("(h e) t -> e h t", e=P)[:, :, c * P:(c + 1) * P])
            a["tn"] = [act.op(lambda e, h=h: e.activation(
                hbuf[:, h, :], hbuf[:, h, :], ACT.Identity, bias=mb[:, c, h:h + 1], scale=rs[:, c, h:h + 1]), a["tmb"])
                for h in range(4)]

        def finish(c):
            a = A.pop(c)
            z = a["z"]
            i, pb, f = pB.take()
            for h in range(4):
                t = pe.op(lambda e, h=h: e.transpose(pb[:, h * P:(h + 1) * P], a["hbuf"][:, h, :], ident[:]), a["tn"], f, t_id)
            hb.free[a["hi"]] = [t]
            yi, y, yf = yb.take()
            t = dve.op(lambda e: e.tensor_tensor(y[:], pb[:].rearrange("p (h t) -> p h t", h=4), z[1][:], ALU.mult),
                       t, z[2], yf)
            pB.free[i] = [t]
            zr.free[z[0]] = [t]
            out.append((c, yi, y, t))

        def store():
            c, yi, y, t = out.pop()
            yb.free[yi] = [self.store(self.y2T[4 * P:8 * P, :].rearrange("(h e) t -> e h t", e=P)[:, :, c * P:(c + 1) * P],
                                      y[:], yb.slots[yi], t, eng=sp)]

        out = []
        for c in range(-2, C + 3):
            for lag, step in ((3, finish), (2, normalise), (1, gate), (0, weights), (-2, decays), (-1, scores),
                              (0, numerators), (1, moments), (0, divide), (0, advance)):
                if 0 <= c - lag < C:
                    step(c - lag)
            if out:
                store()


def program(nc, io, out, scratch="Internal", upto=9):
    kr = Kernel(nc, io, scratch)
    kr.out = out
    kr.yT = kr.dram("yT", (D, S))
    kr.mod = kr.dram("mod", (1, 3 * D))
    kr.h = kr.dram("h", (S, D))
    kr.hT2 = kr.dram("hT2", (D, S))
    kr.gt = kr.dram("gt", (16, S))
    kr.s = {n: kr.dram(n, (S, W) if n in ("mv", "mo") else (W, S))
            for n in ("nqh", "nql", "nkh", "nkl", "nz", "mq", "mk", "mv", "mo", "mz")}
    kr.Z = kr.dram("Z", (2, NA_H, 32, 17 * 40))
    kr.rpb = kr.dram("rpbp", (32, RPB))
    kr.V = kr.dram("V", (2, 32, 40, W))
    kr.nN = kr.dram("nN", (P, P))
    kr.y2T = kr.dram("y2T", (D, S))
    with kr.ctx:
        kr.phase(kr.pool_block)
        kr.phase(lambda: kr.out_block(io["pool_out_w"][0], kr.yT, io["x"][0], False))
        if upto >= 4:
            kr.phase(kr.in_block)
        if upto >= 5:
            kr.phase(kr.na_block)
        if upto >= 6:
            kr.phase(kr.ml_block)
        if upto >= 7:
            kr.phase(lambda: kr.out_block(io["w_out_2"][0], kr.y2T, kr.h, True))


_INS = ["x", "norm_w", "pool_in_w", "pool_group_w", "pool_group_b", "pool_scale", "pool_out_w", "final_norm_w",
        "c_2", "w_ada_2", "b_ada_2", "norm_w_2", "w_in_2", "b_in_2", "conv_w_2", "conv_b_2", "rpb_2", "ml_norm_w_2",
        "w_out_2", "final_norm_w_2"]


def kernel(**inputs):
    import numpy as np
    import concourse.bacc as bacc
    from concourse.bass_utils import run_bass_kernel_spmd

    nc = bacc.Bacc("TRN2", target_bir_lowering=False, num_devices=1)
    arrays, io = {}, {}
    for name in _INS:
        a = np.ascontiguousarray(inputs[name])
        arrays[f"in_{name}"] = a
        io[name] = nc.dram_tensor(f"in_{name}", a.shape, mybir.dt.from_np(a.dtype), kind="ExternalInput").ap()
    out = nc.dram_tensor("out", (1, S, D), F32, kind="ExternalOutput").ap()
    program(nc, io, out)
    r = run_bass_kernel_spmd(nc, [arrays], core_ids=[0])
    return r.results[0]["out"]
```
